# Optimizing a Trainium2 kernel written in Bass

```python
import math
import jax, jax.numpy as jnp
from jax import lax
import numpy as np

D_MODEL = 1024
BATCH = 1
SEQ = 256
DEPTH = 1

HEAD_DIM = 128
HEADS_PER_GROUP = 4
ATTN_GROUPS = ((128, 1), (512, 4), (2048, 16))
N_ATTN_GROUPS = len(ATTN_GROUPS)
ATTN_HEADS = HEADS_PER_GROUP * N_ATTN_GROUPS
ATTN_QK_WIDTH = ATTN_HEADS * HEAD_DIM
ATTN_OUT_WIDTH = HEADS_PER_GROUP * HEAD_DIM
BLOCK = 128
ROPE_THETA = 500000.0
ROPE_DIM = HEAD_DIM // 4
SSM_WIDTH = 512
SSM_GROUP = 16
SSM_GROUPS = SSM_WIDTH // SSM_GROUP
SSM_STATE = 64
DT_MIN = 0.001
DT_MAX = 0.1
D_FF = -(-8 * D_MODEL // (3 * 256)) * 256
PLE_DIM = 256
EPS = 1e-6
IN_WIDTH = 3 * ATTN_QK_WIDTH + SSM_WIDTH + 2 * D_MODEL


def rmsnorm(x, g):
    xf = x.astype(jnp.float32)
    y = xf * lax.rsqrt(jnp.mean(xf * xf, axis=-1, keepdims=True) + EPS)
    return (y * g.astype(jnp.float32)).astype(x.dtype)

def partial_rotary(x, positions):
    half = ROPE_DIM // 2
    inv_freq = ROPE_THETA ** (-jnp.arange(half, dtype=jnp.float32) * 2.0 / ROPE_DIM)
    ang = positions.astype(jnp.float32)[..., None] * inv_freq
    cos = jnp.cos(ang)[:, :, None, :]
    sin = jnp.sin(ang)[:, :, None, :]
    xr = x[..., :ROPE_DIM].astype(jnp.float32)
    x1, x2 = xr[..., :half], xr[..., half:]
    rot = jnp.concatenate([x1 * cos - x2 * sin, x2 * cos + x1 * sin], axis=-1).astype(x.dtype)
    return jnp.concatenate([rot, x[..., ROPE_DIM:]], axis=-1)

def dilated_band_attention(q, k, v, dilation, band):
    B, S, H, Dh = q.shape
    L = S // dilation
    Lp = -(-L // BLOCK) * BLOCK
    nb = Lp // BLOCK

    def to_sub(t):
        t = jnp.moveaxis(t.reshape(B, L, dilation, H, Dh), 2, 1)
        t = jnp.pad(t, ((0, 0), (0, 0), (0, Lp - L), (0, 0), (0, 0)))
        return t.reshape(B, dilation, nb, BLOCK, H, Dh)

    def with_prev(t):
        prev = jnp.pad(t, ((0, 0), (0, 0), (1, 0), (0, 0), (0, 0), (0, 0)))[:, :, :-1]
        return jnp.concatenate([prev, t], axis=3)

    def from_sub(t):
        rest = t.shape[4:]
        t = t.reshape((B, dilation, Lp) + rest)[:, :, :L]
        return jnp.moveaxis(t, 1, 2).reshape((B, S) + rest)

    qb = to_sub(q)
    kk = with_prev(to_sub(k))
    vv = with_prev(to_sub(v))
    scale = 1.0 / math.sqrt(Dh)
    s = jnp.einsum('brnqhd,brnkhd->brnhqk', qb, kk,
                   preferred_element_type=jnp.float32) * scale
    qi = jnp.arange(BLOCK)[:, None]
    kj = jnp.arange(2 * BLOCK)[None, :]
    rel = BLOCK + qi - kj
    in_band = (rel >= 0) & (rel <= band)
    not_first = (jnp.arange(nb) > 0)[:, None, None]
    valid = in_band[None] & (not_first | (kj >= BLOCK)[None])
    s = jnp.where(valid[None, None, :, None], s, -jnp.inf)
    m = jnp.max(s, axis=-1, keepdims=True)
    pexp = jnp.exp(s - m)
    den = jnp.sum(pexp, axis=-1, keepdims=True)
    o = jnp.einsum('brnhqk,brnkhd->brnqhd', pexp, vv.astype(jnp.float32))
    o = o / jnp.swapaxes(den[..., 0], -1, -2)[..., None]
    lse = jnp.swapaxes(m[..., 0] + jnp.log(den[..., 0]), -1, -2)
    return from_sub(o), from_sub(lse)

def _complex_affine_combine(e1, e2):
    a1r, a1i, b1r, b1i = e1
    a2r, a2i, b2r, b2i = e2
    ar = a1r * a2r - a1i * a2i
    ai = a1r * a2i + a1i * a2r
    br = a2r * b1r - a2i * b1i + b2r
    bi = a2r * b1i + a2i * b1r + b2i
    return (ar, ai, br, bi)

def s5_ssm(u, a_re, a_im, log_dt, b_re, b_im, c_re, c_im, d_skip):
    B, S, _ = u.shape
    uf = u.astype(jnp.float32).reshape(B, S, SSM_GROUPS, SSM_GROUP)
    dt = jnp.exp(log_dt.astype(jnp.float32))[:, None]
    lr = a_re.astype(jnp.float32)
    li = a_im.astype(jnp.float32)
    mag = jnp.exp(lr * dt)
    bar_re = mag * jnp.cos(li * dt)
    bar_im = mag * jnp.sin(li * dt)
    nr = bar_re - 1.0
    ni = bar_im
    den = lr * lr + li * li
    z_re = (nr * lr + ni * li) / den
    z_im = (ni * lr - nr * li) / den
    br_ = b_re.astype(jnp.float32)
    bi_ = b_im.astype(jnp.float32)
    bb_re = z_re[..., None] * br_ - z_im[..., None] * bi_
    bb_im = z_re[..., None] * bi_ + z_im[..., None] * br_
    bu_re = jnp.einsum('bsgc,gpc->bsgp', uf, bb_re)
    bu_im = jnp.einsum('bsgc,gpc->bsgp', uf, bb_im)
    ar = jnp.broadcast_to(bar_re, bu_re.shape)
    ai = jnp.broadcast_to(bar_im, bu_im.shape)
    _, _, h_re, h_im = lax.associative_scan(_complex_affine_combine, (ar, ai, bu_re, bu_im), axis=1)
    y = (jnp.einsum('bsgp,gcp->bsgc', h_re, c_re.astype(jnp.float32))
         - jnp.einsum('bsgp,gcp->bsgc', h_im, c_im.astype(jnp.float32))
         + d_skip.astype(jnp.float32) * uf)
    return y.reshape(B, S, SSM_WIDTH).astype(u.dtype)

def hybrid_layer(h, p_l, positions, g_mix, w_in, a_re, a_im, log_dt, b_re, b_im, c_re, c_im,
                 d_skip, w_attn_proj, w_glu_a, w_glu_b, w_out, g_ffn, w_ffn_gate, w_ffn_up,
                 w_ffn_down, w_ple_gate, w_ple_proj):
    B, S, _ = h.shape
    n = rmsnorm(h, g_mix)
    z = n @ w_in
    o0 = ATTN_QK_WIDTH
    q = z[..., 0:o0].reshape(B, S, ATTN_HEADS, HEAD_DIM)
    k = z[..., o0:2 * o0].reshape(B, S, ATTN_HEADS, HEAD_DIM)
    v = z[..., 2 * o0:3 * o0].reshape(B, S, ATTN_HEADS, HEAD_DIM)
    o1 = 3 * o0
    u = z[..., o1:o1 + SSM_WIDTH]
    o2 = o1 + SSM_WIDTH
    gate_attn = jax.nn.sigmoid(z[..., o2:o2 + D_MODEL])
    gate_ssm = jax.nn.sigmoid(z[..., o2 + D_MODEL:o2 + 2 * D_MODEL])

    q = partial_rotary(q, positions)
    k = partial_rotary(k, positions)
    outs = []
    lses = []
    for gi, (window, dilation) in enumerate(ATTN_GROUPS):
        hs = slice(gi * HEADS_PER_GROUP, (gi + 1) * HEADS_PER_GROUP)
        o_g, l_g = dilated_band_attention(q[:, :, hs], k[:, :, hs], v[:, :, hs],
                                          dilation, window // dilation)
        outs.append(o_g)
        lses.append(l_g)
    wts = jax.nn.softmax(jnp.stack(lses, axis=0), axis=0)
    attn = jnp.sum(wts[..., None] * jnp.stack(outs, axis=0), axis=0)
    attn_d = attn.reshape(B, S, ATTN_OUT_WIDTH).astype(h.dtype) @ w_attn_proj

    y = jax.nn.gelu(s5_ssm(u, a_re, a_im, log_dt, b_re, b_im, c_re, c_im, d_skip))
    ssm_d = (y @ w_glu_a) * jax.nn.sigmoid(y @ w_glu_b)

    h = h + (gate_attn * attn_d + gate_ssm * ssm_d) @ w_out

    n2 = rmsnorm(h, g_ffn)
    h = h + (jax.nn.silu(n2 @ w_ffn_gate) * (n2 @ w_ffn_up)) @ w_ffn_down

    h = h + jax.nn.sigmoid(h @ w_ple_gate) * (p_l.astype(h.dtype) @ w_ple_proj)
    return h

def first_inputs(seed: int = 0) -> dict:
    key = jax.random.key(seed)
    ks = jax.random.split(key, 26)
    f32 = jnp.float32

    def nrm(k, shape, fan_in):
        return jax.random.normal(k, shape, f32) * (fan_in ** -0.5)

    x = jax.random.normal(ks[0], (BATCH, SEQ, D_MODEL), f32)
    p = jax.random.normal(ks[1], (DEPTH, BATCH, SEQ, PLE_DIM), f32)
    positions = jnp.broadcast_to(jnp.arange(SEQ, dtype=jnp.int32)[None, :], (BATCH, SEQ))
    g_mix = 1.0 + 0.05 * jax.random.normal(ks[2], (DEPTH, D_MODEL), f32)
    w_in = nrm(ks[3], (DEPTH, D_MODEL, IN_WIDTH), D_MODEL)
    a_re = -0.5 + 0.01 * jax.random.normal(ks[4], (DEPTH, SSM_GROUPS, SSM_STATE), f32)
    a_im = (jnp.pi * jnp.arange(SSM_STATE, dtype=f32)[None, None, :]
            + 0.01 * jax.random.normal(ks[5], (DEPTH, SSM_GROUPS, SSM_STATE), f32))
    log_dt = jax.random.uniform(ks[6], (DEPTH, SSM_GROUPS), f32,
                                minval=math.log(DT_MIN), maxval=math.log(DT_MAX))
    b_re = nrm(ks[7], (DEPTH, SSM_GROUPS, SSM_STATE, SSM_GROUP), 2 * SSM_GROUP)
    b_im = nrm(ks[8], (DEPTH, SSM_GROUPS, SSM_STATE, SSM_GROUP), 2 * SSM_GROUP)
    c_re = nrm(ks[9], (DEPTH, SSM_GROUPS, SSM_GROUP, SSM_STATE), SSM_STATE)
    c_im = nrm(ks[10], (DEPTH, SSM_GROUPS, SSM_GROUP, SSM_STATE), SSM_STATE)
    d_skip = jax.random.normal(ks[11], (DEPTH, SSM_GROUPS, SSM_GROUP), f32)
    w_attn_proj = nrm(ks[12], (DEPTH, ATTN_OUT_WIDTH, D_MODEL), ATTN_OUT_WIDTH)
    w_glu_a = nrm(ks[13], (DEPTH, SSM_WIDTH, D_MODEL), SSM_WIDTH)
    w_glu_b = nrm(ks[14], (DEPTH, SSM_WIDTH, D_MODEL), SSM_WIDTH)
    w_out = nrm(ks[15], (DEPTH, D_MODEL, D_MODEL), D_MODEL)
    g_ffn = 1.0 + 0.05 * jax.random.normal(ks[16], (DEPTH, D_MODEL), f32)
    w_ffn_gate = nrm(ks[17], (DEPTH, D_MODEL, D_FF), D_MODEL)
    w_ffn_up = nrm(ks[18], (DEPTH, D_MODEL, D_FF), D_MODEL)
    w_ffn_down = nrm(ks[19], (DEPTH, D_FF, D_MODEL), D_FF)
    w_ple_gate = nrm(ks[20], (DEPTH, D_MODEL, D_MODEL), D_MODEL)
    w_ple_proj = nrm(ks[21], (DEPTH, PLE_DIM, D_MODEL), PLE_DIM)
    g_final = 1.0 + 0.05 * jax.random.normal(ks[22], (D_MODEL,), f32)
    return {"x": x, "p": p, "positions": positions, "g_mix": g_mix, "w_in": w_in,
            "a_re": a_re, "a_im": a_im, "log_dt": log_dt, "b_re": b_re, "b_im": b_im,
            "c_re": c_re, "c_im": c_im, "d_skip": d_skip, "w_attn_proj": w_attn_proj,
            "w_glu_a": w_glu_a, "w_glu_b": w_glu_b, "w_out": w_out, "g_ffn": g_ffn,
            "w_ffn_gate": w_ffn_gate, "w_ffn_up": w_ffn_up, "w_ffn_down": w_ffn_down,
            "w_ple_gate": w_ple_gate, "w_ple_proj": w_ple_proj, "g_final": g_final}

def first_block(x, p, positions, g_mix, w_in, a_re, a_im, log_dt, b_re, b_im, c_re, c_im, d_skip,
              w_attn_proj, w_glu_a, w_glu_b, w_out, g_ffn, w_ffn_gate, w_ffn_up, w_ffn_down,
              w_ple_gate, w_ple_proj, g_final):
    h = x
    for i in range(DEPTH):
        h = hybrid_layer(h, p[i], positions, g_mix[i], w_in[i], a_re[i], a_im[i], log_dt[i],
                         b_re[i], b_im[i], c_re[i], c_im[i], d_skip[i], w_attn_proj[i],
                         w_glu_a[i], w_glu_b[i], w_out[i], g_ffn[i], w_ffn_gate[i], w_ffn_up[i],
                         w_ffn_down[i], w_ple_gate[i], w_ple_proj[i])
    return rmsnorm(h, g_final)


DEPTH_2 = 2

GRID_W = 64
CTX_LEN = 256
N_MIXERS = 4
Q_BLOCK = 128
ROPE_THETA_2 = 10000.0
NORM_EPS = 1e-6
CONV_WIDTH = 31
CONV_PAD = CONV_WIDTH // 2
GQA_HEADS = 16
GQA_KV_HEADS = 4
GQA_GROUP = GQA_HEADS // GQA_KV_HEADS
GQA_HEAD_DIM = D_MODEL // GQA_HEADS
POOL_WINDOWS = (2, 4, 8, 16)
POOL_GROUP = D_MODEL // len(POOL_WINDOWS)
MLA_HEADS = 16
MLA_NOPE = 64
MLA_ROPE = 32
MLA_V = 64
MLA_QK = MLA_NOPE + MLA_ROPE
MLA_Q_LORA = 768
MLA_KV_LORA = 256
D_FF_2 = 4 * D_MODEL
N_CONV = (DEPTH_2 + 3) // N_MIXERS
N_GQA = (DEPTH_2 + 2) // N_MIXERS
N_POOL = (DEPTH_2 + 1) // N_MIXERS
N_MLA = DEPTH_2 // N_MIXERS


def rms_norm(x, g):
    xf = x.astype(jnp.float32)
    y = xf * lax.rsqrt(jnp.mean(xf * xf, axis=-1, keepdims=True) + NORM_EPS)
    return (y * g.astype(jnp.float32)).astype(x.dtype)

def layer_norm(x, g, b):
    xf = x.astype(jnp.float32)
    mu = jnp.mean(xf, axis=-1, keepdims=True)
    var = jnp.mean(jnp.square(xf - mu), axis=-1, keepdims=True)
    y = (xf - mu) * lax.rsqrt(var + NORM_EPS)
    return (y * g.astype(jnp.float32) + b.astype(jnp.float32)).astype(x.dtype)

def modulate(h, shift, scale):
    return h * (1 + scale[..., None, :]) + shift[..., None, :]

def axial_tables(row, col, rot_dim):
    quarter = rot_dim // 4
    inv = ROPE_THETA_2 ** (-jnp.arange(quarter, dtype=jnp.float32) / quarter)
    ang_r = row[:, None] * inv
    ang_c = col[:, None] * inv
    return (jnp.cos(ang_r), jnp.sin(ang_r), jnp.cos(ang_c), jnp.sin(ang_c))

def _rotate(v, cos, sin):
    a, b = jnp.split(v, 2, axis=-1)
    cos = cos.astype(v.dtype)
    sin = sin.astype(v.dtype)
    return jnp.concatenate([a * cos - b * sin, b * cos + a * sin], axis=-1)

def apply_axial_rope(x, tables):
    cr, sr, cc, sc = tables
    xr, xc = jnp.split(x, 2, axis=-1)
    return jnp.concatenate([_rotate(xr, cr, sr), _rotate(xc, cc, sc)], axis=-1)

def softmax_attend(q, k, v):
    s = jnp.einsum('bkgqd,bkld->bkgql', q, k).astype(jnp.float32) * (q.shape[-1] ** -0.5)
    p = jax.nn.softmax(s, axis=-1).astype(v.dtype)
    return jnp.einsum('bkgql,bkld->bkgqd', p, v)

def blocked_attend(q, k, v):
    b, kh, g, t, dq = q.shape
    nb = t // Q_BLOCK
    qb = q.reshape(b, kh, g, nb, Q_BLOCK, dq).transpose(3, 0, 1, 2, 4, 5)
    out = lax.map(lambda qq: softmax_attend(qq, k, v), qb)
    return out.transpose(1, 2, 3, 0, 4, 5).reshape(b, kh, g, t, v.shape[-1])

def merge_heads(o):
    b, kh, g, t, dv = o.shape
    return o.transpose(0, 3, 1, 2, 4).reshape(b, t, kh * g * dv)

def conv_module(h, w_pw1, w_dw, b_dw, ln_g, ln_b, w_pw2):
    u = h @ w_pw1
    a, gate = jnp.split(u, 2, axis=-1)
    u = a * jax.nn.sigmoid(gate)
    u = lax.conv_general_dilated(
        u, w_dw[:, None, :].astype(u.dtype), window_strides=(1,),
        padding=[(CONV_PAD, CONV_PAD)], dimension_numbers=('NWC', 'WIO', 'NWC'),
        feature_group_count=D_MODEL) + b_dw
    u = jax.nn.silu(layer_norm(u, ln_g, ln_b))
    return u @ w_pw2

def gqa_project(h, w_qkv, q_norm, k_norm):
    b, t, _ = h.shape
    nq = GQA_HEADS * GQA_HEAD_DIM
    nk = GQA_KV_HEADS * GQA_HEAD_DIM
    qkv = h @ w_qkv
    q = qkv[..., :nq].reshape(b, t, GQA_KV_HEADS, GQA_GROUP, GQA_HEAD_DIM).transpose(0, 2, 3, 1, 4)
    k = qkv[..., nq:nq + nk].reshape(b, t, GQA_KV_HEADS, GQA_HEAD_DIM).transpose(0, 2, 1, 3)
    v = qkv[..., nq + nk:].reshape(b, t, GQA_KV_HEADS, GQA_HEAD_DIM).transpose(0, 2, 1, 3)
    return rms_norm(q, q_norm), rms_norm(k, k_norm), v

def gqa_mixer(hl, hc, w_qkv, q_norm, k_norm, w_o, tables, with_ctx):
    ql, kl, vl = gqa_project(hl, w_qkv, q_norm, k_norm)
    qc, kc, vc = gqa_project(hc, w_qkv, q_norm, k_norm)
    ql = apply_axial_rope(ql, tables)
    kl = apply_axial_rope(kl, tables)
    k_all = jnp.concatenate([kc, kl], axis=2)
    v_all = jnp.concatenate([vc, vl], axis=2)
    ol = merge_heads(blocked_attend(ql, k_all, v_all)) @ w_o
    oc = merge_heads(softmax_attend(qc, kc, vc)) @ w_o if with_ctx else None
    return ol, oc

def pool_mixer(h, w_pool, scale):
    b, t, _ = h.shape
    hf = h.astype(jnp.float32)
    cs = jnp.concatenate([jnp.zeros((b, 1, D_MODEL), jnp.float32), jnp.cumsum(hf, axis=1)], axis=1)
    pos = jnp.arange(t)
    outs = []
    for g, w in enumerate(POOL_WINDOWS):
        lo = jnp.clip(pos - w // 2, 0, t)
        hi = jnp.clip(pos + w - w // 2, 0, t)
        csg = cs[..., g * POOL_GROUP:(g + 1) * POOL_GROUP]
        win = jnp.take(csg, hi, axis=1) - jnp.take(csg, lo, axis=1)
        cnt = (hi - lo).astype(jnp.float32)[:, None]
        outs.append(win / cnt - hf[..., g * POOL_GROUP:(g + 1) * POOL_GROUP])
    p = jnp.stack(outs, axis=2).astype(h.dtype)
    y = jnp.einsum('btgc,gcd->btgd', p, w_pool).reshape(b, t, D_MODEL)
    return y * scale

def mla_project(h, w_dq, q_lora_norm, w_uq, w_dkv, kv_lora_norm, w_ukv, q_norm, k_norm):
    b, t, _ = h.shape
    cq = rms_norm(h @ w_dq, q_lora_norm)
    q = (cq @ w_uq).reshape(b, t, MLA_HEADS, MLA_QK).transpose(0, 2, 1, 3)
    dkv = h @ w_dkv
    ckv = rms_norm(dkv[..., :MLA_KV_LORA], kv_lora_norm)
    k_rope = dkv[..., MLA_KV_LORA:]
    kv = (ckv @ w_ukv).reshape(b, t, MLA_HEADS, MLA_NOPE + MLA_V).transpose(0, 2, 1, 3)
    k_nope, v = kv[..., :MLA_NOPE], kv[..., MLA_NOPE:]
    k = jnp.concatenate([k_nope, jnp.broadcast_to(k_rope[:, None], (b, MLA_HEADS, t, MLA_ROPE))], axis=-1)
    return rms_norm(q, q_norm), rms_norm(k, k_norm), v

def rope_tail(x, tables):
    return jnp.concatenate([x[..., :MLA_NOPE], apply_axial_rope(x[..., MLA_NOPE:], tables)], axis=-1)

def mla_mixer(hl, hc, w_dq, q_lora_norm, w_uq, w_dkv, kv_lora_norm, w_ukv, q_norm, k_norm, w_o,
              tables, with_ctx):
    args = (w_dq, q_lora_norm, w_uq, w_dkv, kv_lora_norm, w_ukv, q_norm, k_norm)
    ql, kl, vl = mla_project(hl, *args)
    qc, kc, vc = mla_project(hc, *args)
    ql = rope_tail(ql, tables)[:, :, None]
    kl = rope_tail(kl, tables)
    k_all = jnp.concatenate([kc, kl], axis=2)
    v_all = jnp.concatenate([vc, vl], axis=2)
    ol = merge_heads(blocked_attend(ql, k_all, v_all)) @ w_o
    oc = merge_heads(softmax_attend(qc[:, :, None], kc, vc)) @ w_o if with_ctx else None
    return ol, oc

def sq_relu_mlp(h, w1, w2):
    return jnp.square(jax.nn.relu(h @ w1)) @ w2

def second_inputs(seed: int = 0) -> dict:
    key = jax.random.key(seed)
    ks = jax.random.split(key, 31)
    f32 = jnp.float32

    def nrm(k, shape, scale):
        return jax.random.normal(k, shape, f32) * scale

    def gain(k, shape):
        return 1.0 + 0.05 * jax.random.normal(k, shape, f32)

    d = D_MODEL
    return {
        'x': nrm(ks[0], (BATCH, SEQ, d), 1.0),
        'c': nrm(ks[1], (BATCH, d), 1.0),
        'ctx': nrm(ks[2], (BATCH, CTX_LEN, d), 1.0),
        'c_ctx': nrm(ks[3], (d,), 1.0),
        'norm1_g': gain(ks[4], (DEPTH_2, d)),
        'norm2_g': gain(ks[5], (DEPTH_2, d)),
        'w_mod': nrm(ks[6], (DEPTH_2, d, 6 * d), 0.5 * d ** -0.5),
        'b_mod': nrm(ks[7], (DEPTH_2, 6 * d), 0.02),
        'w_ff1': nrm(ks[8], (DEPTH_2, d, D_FF_2), d ** -0.5),
        'w_ff2': nrm(ks[9], (DEPTH_2, D_FF_2, d), D_FF_2 ** -0.5),
        'conv_w_pw1': nrm(ks[10], (N_CONV, d, 2 * d), d ** -0.5),
        'conv_w_dw': nrm(ks[11], (N_CONV, CONV_WIDTH, d), CONV_WIDTH ** -0.5),
        'conv_b_dw': nrm(ks[12], (N_CONV, d), 0.02),
        'conv_ln_g': gain(ks[13], (N_CONV, d)),
        'conv_ln_b': nrm(ks[14], (N_CONV, d), 0.02),
        'conv_w_pw2': nrm(ks[15], (N_CONV, d, d), d ** -0.5),
        'gqa_w_qkv': nrm(ks[16], (N_GQA, d, (GQA_HEADS + 2 * GQA_KV_HEADS) * GQA_HEAD_DIM), d ** -0.5),
        'gqa_q_norm': gain(ks[17], (N_GQA, GQA_HEAD_DIM)),
        'gqa_k_norm': gain(ks[18], (N_GQA, GQA_HEAD_DIM)),
        'gqa_w_o': nrm(ks[19], (N_GQA, GQA_HEADS * GQA_HEAD_DIM, d), (GQA_HEADS * GQA_HEAD_DIM) ** -0.5),
        'pool_w': nrm(ks[20], (N_POOL, len(POOL_WINDOWS), POOL_GROUP, POOL_GROUP), POOL_GROUP ** -0.5),
        'pool_scale': gain(ks[21], (N_POOL, d)),
        'mla_w_dq': nrm(ks[22], (N_MLA, d, MLA_Q_LORA), d ** -0.5),
        'mla_q_lora_norm': gain(ks[23], (N_MLA, MLA_Q_LORA)),
        'mla_w_uq': nrm(ks[24], (N_MLA, MLA_Q_LORA, MLA_HEADS * MLA_QK), MLA_Q_LORA ** -0.5),
        'mla_w_dkv': nrm(ks[25], (N_MLA, d, MLA_KV_LORA + MLA_ROPE), d ** -0.5),
        'mla_kv_lora_norm': gain(ks[26], (N_MLA, MLA_KV_LORA)),
        'mla_w_ukv': nrm(ks[27], (N_MLA, MLA_KV_LORA, MLA_HEADS * (MLA_NOPE + MLA_V)), MLA_KV_LORA ** -0.5),
        'mla_q_norm': gain(ks[28], (N_MLA, MLA_QK)),
        'mla_k_norm': gain(ks[29], (N_MLA, MLA_QK)),
        'mla_w_o': nrm(ks[30], (N_MLA, MLA_HEADS * MLA_V, d), (MLA_HEADS * MLA_V) ** -0.5),
    }

def second_block(x, c, ctx, c_ctx, norm1_g, norm2_g, w_mod, b_mod, w_ff1, w_ff2,
              conv_w_pw1, conv_w_dw, conv_b_dw, conv_ln_g, conv_ln_b, conv_w_pw2,
              gqa_w_qkv, gqa_q_norm, gqa_k_norm, gqa_w_o, pool_w, pool_scale,
              mla_w_dq, mla_q_lora_norm, mla_w_uq, mla_w_dkv, mla_kv_lora_norm, mla_w_ukv,
              mla_q_norm, mla_k_norm, mla_w_o):
    seq = x.shape[1]
    rows = seq // GRID_W
    row_ids = jnp.repeat(jnp.arange(rows, dtype=jnp.float32), GRID_W)
    col_ids = jnp.tile(jnp.arange(GRID_W, dtype=jnp.float32), rows)
    tab_gqa = axial_tables(row_ids, col_ids, GQA_HEAD_DIM)
    tab_mla = axial_tables(row_ids, col_ids, MLA_ROPE)

    sc = jax.nn.silu(c)
    scc = jax.nn.silu(c_ctx)
    xl, xc = x, ctx
    for i in range(DEPTH_2):
        m = i % N_MIXERS
        j = i // N_MIXERS
        with_ctx = i < DEPTH_2 - 1
        mod_l = jnp.split(sc @ w_mod[i] + b_mod[i], 6, axis=-1)
        mod_c = jnp.split(scc @ w_mod[i] + b_mod[i], 6, axis=-1)

        hl = modulate(rms_norm(xl, norm1_g[i]), mod_l[0], mod_l[1])
        hc = modulate(rms_norm(xc, norm1_g[i]), mod_c[0], mod_c[1])
        if m == 0:
            cargs = (conv_w_pw1[j], conv_w_dw[j], conv_b_dw[j], conv_ln_g[j], conv_ln_b[j], conv_w_pw2[j])
            ol = conv_module(hl, *cargs)
            oc = conv_module(hc, *cargs) if with_ctx else None
        elif m == 1:
            ol, oc = gqa_mixer(hl, hc, gqa_w_qkv[j], gqa_q_norm[j], gqa_k_norm[j], gqa_w_o[j],
                               tab_gqa, with_ctx)
        elif m == 2:
            ol = pool_mixer(hl, pool_w[j], pool_scale[j])
            oc = pool_mixer(hc, pool_w[j], pool_scale[j]) if with_ctx else None
        else:
            ol, oc = mla_mixer(hl, hc, mla_w_dq[j], mla_q_lora_norm[j], mla_w_uq[j], mla_w_dkv[j],
                               mla_kv_lora_norm[j], mla_w_ukv[j], mla_q_norm[j], mla_k_norm[j],
                               mla_w_o[j], tab_mla, with_ctx)
        xl = xl + mod_l[2][:, None, :] * ol
        if with_ctx:
            xc = xc + mod_c[2] * oc

        hl = modulate(rms_norm(xl, norm2_g[i]), mod_l[3], mod_l[4])
        xl = xl + mod_l[5][:, None, :] * sq_relu_mlp(hl, w_ff1[i], w_ff2[i])
        if with_ctx:
            hc = modulate(rms_norm(xc, norm2_g[i]), mod_c[3], mod_c[4])
            xc = xc + mod_c[5] * sq_relu_mlp(hc, w_ff1[i], w_ff2[i])
    return xl


def setup_inputs(seed=0):
    out = dict(first_inputs(seed))
    for name, value in second_inputs(seed + 1).items():
        if name != "x":
            out[name + "_2"] = value
    return out


def reference(
    x, p, positions, g_mix, w_in, a_re, a_im, log_dt, b_re, b_im, c_re, c_im, d_skip,
    w_attn_proj, w_glu_a, w_glu_b, w_out, g_ffn, w_ffn_gate, w_ffn_up, w_ffn_down, w_ple_gate,
    w_ple_proj, g_final, c_2, ctx_2, c_ctx_2, norm1_g_2, norm2_g_2, w_mod_2, b_mod_2, w_ff1_2,
    w_ff2_2, conv_w_pw1_2, conv_w_dw_2, conv_b_dw_2, conv_ln_g_2, conv_ln_b_2, conv_w_pw2_2,
    gqa_w_qkv_2, gqa_q_norm_2, gqa_k_norm_2, gqa_w_o_2, pool_w_2, pool_scale_2, mla_w_dq_2,
    mla_q_lora_norm_2, mla_w_uq_2, mla_w_dkv_2, mla_kv_lora_norm_2, mla_w_ukv_2, mla_q_norm_2,
    mla_k_norm_2, mla_w_o_2,
):
    x = first_block(
        x, p, positions, g_mix, w_in, a_re, a_im, log_dt, b_re, b_im, c_re, c_im, d_skip,
        w_attn_proj, w_glu_a, w_glu_b, w_out, g_ffn, w_ffn_gate, w_ffn_up, w_ffn_down,
        w_ple_gate, w_ple_proj, g_final,
    )
    return second_block(
        x, c_2, ctx_2, c_ctx_2, norm1_g_2, norm2_g_2, w_mod_2, b_mod_2, w_ff1_2, w_ff2_2,
        conv_w_pw1_2, conv_w_dw_2, conv_b_dw_2, conv_ln_g_2, conv_ln_b_2, conv_w_pw2_2,
        gqa_w_qkv_2, gqa_q_norm_2, gqa_k_norm_2, gqa_w_o_2, pool_w_2, pool_scale_2, mla_w_dq_2,
        mla_q_lora_norm_2, mla_w_uq_2, mla_w_dkv_2, mla_kv_lora_norm_2, mla_w_ukv_2,
        mla_q_norm_2, mla_k_norm_2, mla_w_o_2,
    )


_drawn_inputs = setup_inputs


def setup_inputs(seed=0):
    import zlib

    import numpy as np

    out = dict(_drawn_inputs(seed))
    spreads = {}
    factors = {'g_mix': 3.822,
     'a_re': 8.0,
     'a_im': 3.353,
     'log_dt': 3.443,
     'b_re': 4.783,
     'b_im': 4.719,
     'c_re': 4.659,
     'c_im': 4.687,
     'ctx_2': 4.027,
     'norm1_g_2': 5.177,
     'conv_b_dw_2': 8.0,
     'conv_ln_g_2': 5.015,
     'conv_ln_b_2': 8.0,
     'gqa_q_norm_2': 8.0,
     'gqa_k_norm_2': 8.0}
    for name, (base, spread) in spreads.items():
        noise = np.random.default_rng([zlib.crc32(name.encode()), seed]).standard_normal(out[name].shape)
        drawn = base * np.exp(spread * noise) if base else spread * noise
        out[name] = __import__('jax').numpy.asarray(drawn.astype(out[name].dtype))
    for name, factor in factors.items():
        out[name] = (out[name] * factor).astype(out[name].dtype)
    return out
```

```python
from contextlib import ExitStack

import numpy as np

import concourse.bass as bass
from concourse import mybir

ALU = mybir.AluOpType
ACT = mybir.ActivationFunctionType
F32 = mybir.dt.float32
F32R = mybir.dt.float32r
I32 = mybir.dt.int32
AX_X = mybir.AxisListType.X

P = 128
TR = 8
D = 1024
KD = D // P
T1 = 256
HD = 128
NHG = 4
NG = 3
QKW = NHG * NG * HD
SSMW = 512
NTILE = 16
DFF = 2816
DFF2 = 4096
EPS = 1e-6
NSCORE = -1e30
BLK = 2048
RAW = 4
TWO_PI = 2.0 * np.pi
C1 = 6.28125
C2 = float(np.float32(TWO_PI - C1))
C3 = float(np.float32(TWO_PI - C1 - np.float64(np.float32(TWO_PI - C1))))
MAGIC = 12582912.0
L2E = float(np.float32(1.0 / np.log(2.0)))
LN2A = 0.693359375
LN2B = float(np.float32(np.log(2.0) - 0.693359375))
PI_LO = 3.1415925

PHASES = [("in", 28), ("attnproj", 2), ("glu", 4), ("out", 4), ("ffn", 22), ("down", 11), ("ple", 5),
          ("pw1", 8), ("pw2", 4), ("ff1a", 16), ("ff2a", 16), ("qkv", 6), ("wo", 4), ("ff1b", 16), ("ff2b", 16)]
FIRST = {}
_b = 0
for _name, _n in PHASES:
    FIRST[_name] = _b
    _b += _n
NBLOCKS = _b
COUNT = dict(PHASES)
U0, Q0, K0, V0, GATE0 = 0, 2, 8, 14, 20
MODS = 48
HALVES = 48


class Pos:

    def __init__(self, b, l, i=0):
        self.b, self.l, self.q, self.k, self.h = b + 4 * i, l + 4 * i, b // 4 + i, b % 4, l // 2 + 2 * i
        self.least = l


def each_block(eng, phase, body, roll=True):
    b0, n = FIRST[phase], COUNT[phase]
    l = 0
    while l < n:
        if roll and l >= 4 and (b0 + l) % 4 == 0 and n - l >= 8:
            quads = (n - l - 1) // 4
            with eng.Fori(0, quads) as i:
                for k in range(4):
                    body(Pos(b0 + l + k, l + k, i))
            l += 4 * quads
        else:
            body(Pos(b0 + l, l))
            l += 1


CONV_DVE = [0, 2, 4, 5, 6]
CONV_POOL = [1, 3]
CONV_PE = [7]
TAPS = 31
PRE, EV, LNP = 12, 4, 21
CONV_ORDER = [0, 2, 1, 4, 3, 5, 7, 6]

CONSTS = [("ident", 128), ("ones", 128), ("halves", 128), ("rotg", 128), ("invf", 1),
          ("gmix", 8), ("gffn", 8), ("gfinal", 8), ("convb", 8), ("lng", 8), ("lnb", 8), ("g1", 16), ("g2", 16),
          ("bmod", 96), ("qn", 1), ("kn", 1), ("dskip", 4), ("lr", 16), ("li", 16), ("ldt", 16), ("cc", 16)]
CW = sum(w for _, w in CONSTS)


def program(nc, I, out):
    ctx = ExitStack()
    with ctx:
        def sb(name, shape, dt=F32):
            return ctx.enter_context(nc.sbuf_tensor(name, shape, dt))

        def sem(name):
            return ctx.enter_context(nc.semaphore(name))

        raw = sb("raw", [P, RAW, BLK])
        whi = sb("whi", [P, 2, BLK], F32R)
        wlo = sb("wlo", [P, 2, BLK], F32R)
        ahi = sb("ahi", [P, 4096], F32R)
        alo = sb("alo", [P, 4096], F32R)
        X = sb("X", [P, 2, KD, T1])
        cst = sb("cst", [P, CW])
        C = {}
        at = 0
        for name, w in CONSTS:
            C[name] = cst[:, at:at + w]
            at += w
        rope = sb("rope", [P, 2, T1])
        rstd = sb("rstd", [P, 512])
        sp = sb("sp", [P, 24, 16])
        mods = sb("mods", [P, 2, MODS, 2])
        amul = sb("amul", [P, 8, 2])
        scc = sb("scc", [P, 46])
        stat = sb("stat", [P, 64])
        modrow = rstd[:, :].rearrange("p (r w) -> p r w", r=2)
        A = sb("A", [P, 22016])

        def area(start, n):
            return A[:, start:start + n]

        o = 0
        q_s = area(o, 3072).rearrange("p (h t) -> p h t", h=12); o += 3072
        k_s = area(o, 3072).rearrange("p (h t) -> p h t", h=12); o += 3072
        v_s = area(o, 3072).rearrange("p (a w) -> p a w", a=2); o += 3072
        u_s = area(o, 1024).rearrange("p (c t) -> p c t", c=4); o += 1024
        GATES = o
        tab = area(o, 2048).rearrange("p (r s j t) -> p r s j t", r=2, s=2, j=2); o += 2048
        tta = area(o, 512); o += 512
        ttb = area(o, 512); o += 512
        h_s = area(o, 1024).rearrange("p (r s t) -> p r s t", r=2, s=2); o += 1024
        gates = area(GATES, 4096).rearrange("p (c t) -> p c t", c=16)
        WORK = o
        p1 = area(o, 512).rearrange("p (s t) -> p s t", s=2); o += 512
        p2 = area(o, 512).rearrange("p (s t) -> p s t", s=2); o += 512
        w_s = area(o, 512).rearrange("p (s t) -> p s t", s=2); o += 512
        g_s = area(o, 1024).rearrange("p (r s t) -> p r s t", r=2, s=2); o += 1024
        q1 = area(o, 512).rearrange("p (s t) -> p s t", s=2); o += 512
        q2 = area(o, 512).rearrange("p (s t) -> p s t", s=2); o += 512
        sm = area(WORK, 768)
        pr = area(WORK + 768, 1536).rearrange("p (r w) -> p r w", r=2)
        pt = area(WORK + 2304, 768)
        bl = area(o, 1024).rearrange("p (c s w) -> p c s w", c=4, s=2); o += 1024
        ct = area(o, 1024).rearrange("p (s j w) -> p s j w", s=2, j=NTILE); o += 1024
        MODRAW = o
        modraw = area(o, 2048).rearrange("p (r w) -> p r w", r=2); o += 2048
        assert o <= 22016, o
        crw = area(6144, 1024).rearrange("p (s j w) -> p s j w", s=2, j=NTILE)
        ctt = area(7168, 1024).rearrange("p (s j w) -> p s j w", s=2, j=NTILE)
        posw = area(8192, 1024)[0:32, :].rearrange("p (r w) -> p r w", r=4)
        msk = X[:, 1, :, :].rearrange("p c t -> p (c t)")
        mask0 = msk[:, 0:384]
        mask1 = msk[:, 384:1152]
        rotb = msk[0:32, 1152:1664].rearrange("p (a t) -> p a t", a=2)
        powers = msk[:, 1664:1920].rearrange("p (n s j) -> p n s j", n=8, s=2)
        mix = area(0, 2048)
        glus = area(2048, 1024)
        glut = area(3072, 1024)
        hid1 = area(0, DFF // P * T1)
        sg1 = area(6144, 1024).rearrange("p (r w) -> p r w", r=2)
        tg1 = area(7168, 1024).rearrange("p (r w) -> p r w", r=2)
        pin = area(8192, 512)
        plep = area(6144, 2048)
        hid = area(0, 32 * 512)
        rl = area(16384, 1024).rearrange("p (r w) -> p r w", r=2)
        UPW = T1 + 30
        upad = area(0, 16 * UPW).rearrange("p (c s t) -> p c s t", c=KD, s=2)
        cacc = area(16 * UPW, 4096).rearrange("p (c s t) -> p c s t", c=KD, s=2)
        SB2 = 16 * UPW + 4096
        wdw = area(SB2, KD * 31).rearrange("p (c j) -> p c j", c=KD)
        sgc = area(SB2 + 248, 1024).rearrange("p (r w) -> p r w", r=2)
        ctp = area(SB2 + 248 + 1024, 1024).rearrange("p (r w) -> p r w", r=2)
        mean_s = area(SB2 + 2296, 512)
        csq = area(SB2 + 2808, 2048).rearrange("p (r w) -> p r w", r=4)
        diag = area(14336, 1024).rearrange("p (r w) -> p r w", r=8)
        assert SB2 + 2808 + 2048 <= 14336
        modraw1 = area(15872, 6144).rearrange("p (r w) -> p r w", r=6)
        qg = area(0, 2048).rearrange("p (c t) -> p c t", c=8)
        kg = area(2048, 1024).rearrange("p (c t) -> p c t", c=2)
        vg = area(3072, 1024).rearrange("p (a w) -> p a w", a=4)
        gtab = area(17408, 512).rearrange("p (s t) -> p s t", s=2)
        gt1 = area(4608, 1024).rearrange("p (r w) -> p r w", r=2)
        gt2 = area(5632, 1024).rearrange("p (r w) -> p r w", r=2)
        gsq = area(6656, 3072)
        pg = area(9728, 2048).rearrange("p (r a w) -> p r a w", r=2, a=2)
        ptg = area(11776, 2048).rearrange("p (r w) -> p r w", r=2)
        pb = [ctx.enter_context(nc.psum_tensor(f"bank{n}", [P, 512], F32)) for n in range(8)]

        landed = [sem(f"raw_landed{n}") for n in range(RAW)]
        whi_ready = sem("whi_ready")
        wlo_ready = sem("wlo_ready")
        block_done = sem("block_done")
        modraw_landed = [sem(f"modraw_landed{n}") for n in range(2)]
        modraw1_landed = [sem(f"modraw1_landed{n}") for n in range(6)]
        modraw_used = sem("modraw_used")
        modrow_ready = sem("modrow_ready")
        mod_turned = sem("mod_turned")
        mod_ready = sem("mod_ready")
        x_landed = sem("x_landed")
        cst_landed = sem("cst_landed")
        ssm_landed = sem("ssm_landed")
        mask_landed = sem("mask_landed")
        pos_landed = sem("pos_landed")
        ctx_landed = sem("ctx_landed")
        p_landed = sem("p_landed")
        dw_landed = sem("dw_landed")
        gtab_landed = sem("gtab_landed")
        out_stored = sem("out_stored")
        sq_ready = sem("sq_ready")
        sq_used = sem("sq_used")
        std_ready = sem("std_ready")
        rstd_ready = sem("rstd_ready")
        n_ready = sem("n_ready")
        nhi_ready = sem("nhi_ready")
        nlo_ready = sem("nlo_ready")
        evac = {name: sem("evac_" + name) for name, _ in PHASES}
        dch = sem("dve_chain")
        pch = sem("pool_chain")
        ach = sem("act_chain")
        scc_ready = sem("scc_ready")
        sin_in = sem("sin_in")
        sin_out = sem("sin_out")
        rtab_ready = sem("rtab_ready")
        tab_ready = sem("tab_ready")
        ct_ready = sem("ct_ready")
        bu_done = sem("bu_done")
        bu_used = sem("bu_used")
        g_ready = sem("g_ready")
        h_ready = sem("h_ready")
        y_done = sem("y_done")
        ysum_ready = sem("ysum_ready")
        gelu_ready = sem("gelu_ready")
        yhi_ready = sem("yhi_ready")
        ylo_ready = sem("ylo_ready")
        rot_done = sem("rot_done")
        roped = sem("roped")
        s_done = sem("scores_done")
        s_used = sem("scores_used")
        nmax_ready = sem("nmax_ready")
        exp_done = sem("exp_done")
        pn_ready = sem("probs_ready")
        pt_done = sem("probs_transposed")
        pt_ready = sem("pt_ready")
        o_done = sem("o_done")
        ohi_ready = sem("ohi_ready")
        olo_ready = sem("olo_ready")
        gsig_ready = sem("gsig_ready")
        gate_ready = sem("gate_ready")
        mix_ready = sem("mix_ready")
        mixhi_ready = sem("mixhi_ready")
        mixlo_ready = sem("mixlo_ready")
        sig_ready = sem("sig_ready")
        th_ready = sem("th_ready")
        hhi_ready = sem("hidden_hi_ready")
        hlo_ready = sem("hidden_lo_ready")
        x_ready = sem("x_ready")
        phi_ready = sem("p_hi_ready")
        plo_ready = sem("p_lo_ready")
        xhi_ready = sem("x_hi_ready")
        xlo_ready = sem("x_lo_ready")
        plep_ready = sem("plep_ready")
        am_ready = sem("amul_ready")
        pad_ready = sem("pad_ready")
        u_ready = sem("conv_in_ready")
        cp_ready = sem("conv_product_ready")
        cp_used = sem("conv_product_used")
        conv_pool = sem("conv_pool")
        conv_dve = sem("conv_dve")
        diag_ready = sem("diag_ready")
        tap_done = sem("tap_done")
        conv_out = sem("conv_out")
        msum_done = sem("mean_done")
        mean_ready = sem("mean_ready")
        cen_ready = sem("centred_ready")
        vsq_ready = sem("var_sq_ready")
        vsum_done = sem("var_sum_done")
        lstd_ready = sem("ln_std_ready")
        lnx_ready = sem("ln_scaled_ready")
        lns_ready = sem("ln_silu_ready")
        lny_ready = sem("ln_silu_product_ready")
        lnhi_ready = sem("ln_hi_ready")
        lnlo_ready = sem("ln_lo_ready")
        relu_ready = sem("relu_ready")
        hid_sq = sem("hidden_ready")
        conv_init = sem("conv_init")
        gq_sq = sem("gq_squares")
        gq_ms = sem("gq_sums")
        gq_std = sem("gq_std")
        gq_n = sem("gq_normed")
        gq_rot = sem("gq_rotated")
        gq_ready = sem("gq_ready")

        block = ctx.enter_context(nc.Block())

        def cols(w, lo, n, kn=KD):
            return w.rearrange("(c p) m -> p c m", p=P)[:, 0:kn, bass.ds(lo, n)]

        def rows(w, k0):
            return w.rearrange("(c p) m -> p c m", p=P)[:, bass.ds(k0, 2), :]

        def in_col(l):
            if l < Q0:
                return 3 * QKW + 256 * l
            if l < GATE0:
                return 256 * (l - Q0)
            return 3 * QKW + SSMW + 256 * (l - GATE0)

        def source(phase, p):
            l, odd = p.l, p.least % 2
            if phase == "in":
                return cols(I["w_in"], in_col(l), 256)
            if phase == "attnproj":
                return cols(I["w_attn_proj"], 512 * l, 512, 4)
            if phase == "glu":
                return cols(I["w_glu_b" if odd else "w_glu_a"], 512 * p.h, 512, 4)
            if phase == "out":
                return cols(I["w_out"], 256 * l, 256)
            if phase == "ffn":
                return cols(I["w_ffn_up" if odd else "w_ffn_gate"], 256 * p.h, 256)
            if phase == "down":
                return rows(I["w_ffn_down"], 2 * l)
            if phase == "ple":
                return rows(I["w_ple_proj"], 0) if p.least == 0 else cols(I["w_ple_gate"], 256 * (l - 1), 256)
            if phase == "pw1":
                return cols(I["pw1"], (D if odd else 0) + 256 * p.h, 256)
            if phase == "pw2":
                return cols(I["pw2"], 256 * l, 256)
            if phase in ("ff1a", "ff1b"):
                return cols(I["w_ff1"][int(phase == "ff1b")], 256 * l, 256)
            if phase in ("ff2a", "ff2b"):
                return rows(I["w_ff2"][int(phase == "ff2b")], 2 * l)
            if phase == "qkv":
                return cols(I["w_qkv"], D + 256 * l if p.least < 2 else 256 * (l - 2), 256)
            return cols(I["w_o"], 256 * l, 256)

        @block.sync
        def _(sync):
            def load(phase, p):
                if p.b is not None and (p.least >= 4 or FIRST[phase] >= 4):
                    sync.wait_ge(wlo_ready, p.b - 3)
                src = source(phase, p)
                dst = raw[:, p.k, :].rearrange("p (c m) -> p c m", c=src.shape[1])
                sync.dma_start(dst, src).then_inc(landed[p.k], 16)

            def load_mod(layer, t):
                ring_, landed_ = (modraw1, modraw1_landed) if layer else (modraw, modraw_landed)
                n = len(landed_)
                if t >= n:
                    sync.wait_ge(modraw_used, layer * HALVES + t - n + 1)
                m, c = divmod(t, KD)
                sync.dma_start(ring_[:, t % n, :], I["w_mod"][layer][P * c:P * c + P, D * m:D * m + D])\
                    .then_inc(landed_[t % n], 16)

            sync.dma_start(X[:, 0, :, :], I["x"]).then_inc(x_landed, 16)
            for name, _ in PHASES:
                if name == "in":
                    for l in range(28):
                        load(name, Pos(l, l))
                        if 4 <= l:
                            load_mod(0, 2 * (l - 4))
                            load_mod(0, 2 * (l - 4) + 1)
                        if l == 4:
                            sync.dma_start(msk[:, 0:1152], I["masks"]).then_inc(mask_landed, 16)
                    continue
                if name == "out":
                    sync.wait_ge(s_used, TR)
                    sync.wait_ge(roped, 12)
                    sync.wait_ge(y_done, NTILE)
                    sync.dma_start(X[:, 1, :, :], I["ctx"]).then_inc(ctx_landed, 16)
                    sync.wait_ge(o_done, TR)
                    sync.dma_start(pin, I["p"]).then_inc(p_landed, 16)
                if name == "pw1":
                    for l in range(8):
                        load(name, Pos(FIRST[name] + l, l))
                        if l == 4:
                            sync.wait_ge(nlo_ready, 16)
                        if l >= 4:
                            load_mod(1, l - 4)
                    load_mod(1, 4)
                    load_mod(1, 5)
                else:
                    each_block(sync, name, lambda p: load(name, p))
                if name == "pw2":
                    for t in range(6, HALVES):
                        load_mod(1, t)
                    sync.wait_ge(modraw_used, 2 * HALVES)
                    sync.dma_start(gtab, I["gtab"]).then_inc(gtab_landed, 16)
            for u in range(4):
                sync.wait_ge(evac["ff2b"], 2 * (u + 1))
                sync.dma_start(out[:, 2 * u:2 * u + 2, :], X[:, 0, 2 * u:2 * u + 2, :]).then_inc(out_stored, 16)
            sync.wait_ge(out_stored, 64)

        NU = [4, 4, 4, 8, 8, 8, 4]
        NBASE = [sum(NU[:r]) for r in range(8)]
        SQ_AT = [0, 8704, 8704, 14336, 0, 0, 0]
        NB_AT = [4096, 10752, 10752, 16384, 4096, 4096, 4096]

        def unit(t, r, u):
            return t[:, 0, 2 * u:2 * u + 2, :] if NU[r] == 4 else t[:, :, u, :]

        def ring(at, u):
            return area(at + 512 * (u % 4), 512).rearrange("p (a t) -> p a t", a=2)

        def flat(at, u):
            return area(at + 512 * (u % 4), 512)

        def squares(act, r, waits):
            for u in range(NU[r]):
                for s, v in waits(u):
                    act.wait_ge(s, v)
                if u >= 4:
                    act.wait_ge(sq_used, NBASE[r] + u - 3)
                act.activation(ring(SQ_AT[r], u), unit(X, r, u), ACT.Square).then_inc(sq_ready, 1)

        def sums(pe, r):
            for u in range(NU[r]):
                pe.wait_ge(sq_ready, NBASE[r] + u + 1)
                s = flat(SQ_AT[r], u)
                if NU[r] == 4:
                    pe.matmul(pb[7][:, 0:256], C["ones"], s[:, 0:256], start=(u == 0), stop=False)
                    mm = pe.matmul(pb[7][:, 0:256], C["ones"], s[:, 256:512], start=False, stop=(u == 3))
                else:
                    mm = pe.matmul(pb[7][:, :], C["ones"], s, start=(u == 0), stop=(u == 7))
                mm.then_inc(sq_used, 1)

        def std(act, r):
            w = 256 if NU[r] == 4 else 512
            act.wait_ge(sq_used, NBASE[r + 1])
            act.activation(rstd[:, 0:w], pb[7][:, 0:w], ACT.Sqrt, scale=1.0 / D, bias=epsb).then_inc(std_ready, 1)

        def hi_parts(act, r):
            for u in range(NU[r]):
                act.wait_ge(n_ready, NBASE[r] + u + 1)
                act.activation(ahi[:, 512 * u:512 * u + 512], flat(NB_AT[r], u), ACT.Copy).then_inc(nhi_ready, 1)

        def lo_parts(pool, r):
            for u in range(NU[r]):
                pool.wait_ge(nhi_ready, NBASE[r] - 4 * (r > 2) + u + 1)
                pool.tensor_tensor(alo[:, 512 * u:512 * u + 512], flat(NB_AT[r], u),
                                   ahi[:, 512 * u:512 * u + 512].bitcast(F32), ALU.subtract).then_inc(nlo_ready, 1)

        def wait_norm(pe, r, kc=None):
            n = NU[r] if kc is None else (kc // 2 + 1 if NU[r] == 4 else kc + 1)
            pe.wait_ge(nlo_ready, NBASE[r] - 4 * (r > 2) + n)

        epsb = stat[:, 60:61]

        @block.scalar
        def _(act):
            chain = [0]

            def link(ins):
                chain[0] += 1
                ins.then_inc(ach, 1)
                act.wait_ge(ach, chain[0])

            def hi(p_b, q, k):
                b, kk, qq = p_b + 2, (k + 2) % 4, q + (k + 2) // 4
                act.wait_ge(landed[kk], qq * 16 + 16)
                act.wait_ge(block_done, p_b + 1)
                act.activation(whi[:, k % 2, :], raw[:, kk, :], ACT.Copy).then_inc(whi_ready, 1)

            def ahead(p):
                if not (p.least + 2 >= COUNT[ph[0]] and ph[0] == PHASES[-1][0]):
                    hi(p.b, p.q, p.k)

            ph = ["in"]

            act.dma_start(cst[:, :], I["consts"]).then_inc(cst_landed, 16)
            act.dma_start(crw, I["ct"]).then_inc(ssm_landed, 16)
            act.dma_start(bl, I["bl"]).then_inc(ssm_landed, 16)
            act.dma_start(posw[:, 0, :].bitcast(I32), I["pos"]).then_inc(pos_landed, 16)
            for b in range(2):
                if b == 0:
                    act.wait_ge(am_ready, 1)
                    squares(act, 0, lambda u: [(x_landed, 16)])
                act.wait_ge(landed[b], 16)
                act.activation(whi[:, b, :], raw[:, b, :], ACT.Copy).then_inc(whi_ready, 1)
            std(act, 0)
            act.wait_ge(cst_landed, 16)
            hi_parts(act, 0)
            act.wait_ge(sin_in, 1)
            act.activation(sp[:, 8, :], sp[:, 6, :], ACT.Sin).then_inc(sin_out, 1)
            act.activation(sp[:, 9, :], sp[:, 7, :], ACT.Sin).then_inc(sin_out, 1)
            act.wait_ge(sin_in, 2)
            act.activation(rope[0:32, 1, :], posw[:, 1, :], ACT.Sin).then_inc(sin_out, 1)
            act.activation(rope[0:32, 0, :], posw[:, 2, :], ACT.Sin).then_inc(sin_out, 1)
            act.activation(scc[:, 0:16], C["cc"], ACT.Sigmoid).then_inc(scc_ready, 1)

            def attention_exp(n):
                w = 384 if n % 2 == 0 else 768
                act.wait_ge(nmax_ready, n + 1)
                if n >= 2:
                    act.wait_ge(pt_done, n - 1)
                act.activation(pr[:, n % 2, 0:w], sm[:, 0:w], ACT.Exp, bias=stat[:, n:n + 1],
                               accum_out=stat[:, 8 + n:9 + n]).then_inc(exp_done, 1)

            def attention_pt(n):
                act.wait_ge(pt_done, n + 1)
                if n >= 1:
                    act.wait_ge(o_done, n)
                for kt in range(1 + n % 2):
                    c = act.activation(pt[:, 384 * kt:384 * kt + 384], pb[2 + kt][:, 0:384], ACT.Copy)
                c.then_inc(pt_ready, 1)

            def attention_out(n):
                c0 = 2048 + 256 * (n // 2) + 128 * (n % 2)
                act.wait_ge(o_done, n + 1)
                act.activation(ahi[:, c0:c0 + 128], pb[6][:, 0:128], ACT.Copy).then_inc(ohi_ready, 1)

            def attention_early(n):
                if 0 <= n - 4 < TR:
                    attention_out(n - 4)
                if 0 <= n - 1 < TR:
                    attention_exp(n - 1)

            def attention_late(n):
                if 0 <= n - 2 < TR:
                    attention_pt(n - 2)

            def gelu(c):
                act.wait_ge(ysum_ready, c + 1)
                act.activation(u_s[:, c, :], u_s[:, c, :], ACT.Gelu_apprx_tanh).then_inc(gelu_ready, 1)

            def yhi(c):
                act.wait_ge(gelu_ready, c + 1)
                act.activation(ahi[:, 3072 + 256 * c:3328 + 256 * c], u_s[:, c, :], ACT.Copy).then_inc(yhi_ready, 1)

            def mod_rows(layer, m):
                n = 6 * layer + m
                act.wait_ge(modraw_used, HALVES * layer + KD * (m + 1))
                if m >= 2:
                    act.wait_ge(mod_turned, n - 1)
                bank = pb[2 + m % 2] if layer else pb[7]
                act.activation(modrow[:, m % 2, :], bank[:, 0:256], ACT.Copy).then_inc(modrow_ready, 1)

            for l in range(28):
                p = Pos(l, l)
                if l % 4 == 2 and l > 2:
                    mod_rows(0, (l - 6) // 4)
                attention_early(l - GATE0)
                ahead(p)
                bank = pb[l % 2][:, :].rearrange("p (a t) -> p a t", a=2)
                act.wait_ge(block_done, p.b + 1)
                if l < Q0:
                    act.activation(u_s[:, 2 * l:2 * l + 2, :], bank, ACT.Copy).then_inc(evac["in"], 1)
                elif l < K0:
                    act.activation(q_s[:, 2 * (l - Q0):2 * (l - Q0) + 2, :], bank, ACT.Copy).then_inc(evac["in"], 1)
                elif l < V0:
                    act.activation(k_s[:, 2 * (l - K0):2 * (l - K0) + 2, :], bank, ACT.Copy).then_inc(evac["in"], 1)
                elif l < GATE0:
                    if l == V0:
                        act.wait_ge(ct_ready, 1)
                    act.activation(v_s[:, :, 256 * (l - V0):256 * (l - V0) + 256], bank, ACT.Copy)\
                       .then_inc(evac["in"], 1)
                else:
                    if l == GATE0:
                        act.wait_ge(y_done, NTILE)
                    act.activation(gates[:, 2 * (l - GATE0):2 * (l - GATE0) + 2, :], bank, ACT.Tanh, scale=0.5)\
                       .then_inc(evac["in"], 1)
                if l == 22:
                    for c in range(4):
                        gelu(c)
                    for c in range(4):
                        yhi(c)
                attention_late(l - GATE0)
            for n in range(8, TR + 4):
                attention_early(n)
                attention_late(n)

            ph[0] = "attnproj"
            each_block(act, "attnproj", ahead)
            ph[0] = "glu"
            for l in range(4):
                p = Pos(FIRST["glu"] + l, l)
                ahead(p)
                if l % 2:
                    act.wait_ge(block_done, p.b + 1)
                    if l == 3:
                        act.wait_ge(mix_ready, 1)
                    for s in range(2):
                        c = act.activation(glus[:, 512 * s:512 * s + 512], pb[6 + s][:, :], ACT.Sigmoid)
                    c.then_inc(gsig_ready, 1)
            for j in range(2):
                act.wait_ge(mix_ready, j + 1)
                for s in range(2):
                    act.activation(ahi[:, 1024 * j + 512 * s:1024 * j + 512 * s + 512],
                                   mix[:, 1024 * j + 512 * s:1024 * j + 512 * s + 512], ACT.Copy)\
                       .then_inc(mixhi_ready, 1)
            ph[0] = "out"
            each_block(act, "out", ahead)
            squares(act, 1, lambda u: [(evac["out"], u + 1)])
            std(act, 1)
            hi_parts(act, 1)

            ph[0] = "ffn"

            def act_ffn(p):
                ahead(p)
                if p.least % 2 == 0:
                    act.wait_ge(block_done, p.b + 1)
                    if p.least >= 4:
                        act.wait_ge(evac["ffn"], p.l - 2)
                    act.activation(sg1[:, p.least // 2 % 2, :], pb[p.k][:, :], ACT.Sigmoid).then_inc(sig_ready, 1)

            each_block(act, "ffn", act_ffn)

            def hidden_hi(l, base, total, w, h, at, l_static):
                if l_static + 2 >= total:
                    return
                s = (l_static + 2) % 4
                if l_static + 2 >= 4:
                    act.wait_ge(block_done, base + l - 1)
                act.activation(ahi[:, at + w * s:at + w * s + w], h[:, bass.ds(w * (l + 2), w)], ACT.Copy)\
                   .then_inc(hhi_ready, 1)

            ph[0] = "down"
            for l in (-2, -1):
                act.wait_ge(evac["ffn"], 2 * (l + 3))
                hidden_hi(l, FIRST["down"], 11, 512, hid1, 2048, l)

            def act_down(p):
                hidden_hi(p.l, FIRST["down"], 11, 512, hid1, 2048, p.least)
                ahead(p)

            act.wait_ge(evac["ffn"], 22)
            each_block(act, "down", act_down, roll=False)
            act.wait_ge(p_landed, 16)
            act.activation(ahi[:, 3584:4096], pin, ACT.Copy).then_inc(phi_ready, 1)
            for u in range(4):
                act.wait_ge(evac["down"], u + 1)
                act.activation(ahi[:, 512 * u:512 * u + 512].rearrange("p (a t) -> p a t", a=2),
                               X[:, 0, 2 * u:2 * u + 2, :], ACT.Copy).then_inc(xhi_ready, 1)
            ph[0] = "ple"
            for l in range(5):
                p = Pos(FIRST["ple"] + l, l)
                ahead(p)
                act.wait_ge(block_done, p.b + 1)
                if l == 0:
                    for s in range(4):
                        c = act.activation(plep[:, 512 * s:512 * s + 512], pb[4 + s][:, :], ACT.Copy)
                    c.then_inc(plep_ready, 1)
                else:
                    act.activation(area(8704 + 512 * (l - 1), 512), pb[l - 1][:, :], ACT.Sigmoid).then_inc(sig_ready, 1)
            squares(act, 2, lambda u: [(evac["ple"], u + 1)])
            std(act, 2)
            squares(act, 3, lambda u: [(n_ready, NBASE[3]), (ctx_landed, 16)])
            std(act, 3)
            act.dma_start(wdw, I["w_dw"]).then_inc(dw_landed, 16)
            hi_parts(act, 3)

            ph[0] = "pw1"
            taps = [(c, j) for c in CONV_POOL for j in range(31)]

            def diagonal(i):
                if i >= 8:
                    act.wait_ge(tap_done, i - 7)
                act.activation(diag[:, i % 8, :], C["ident"], ACT.Copy,
                               scale=wdw[:, CONV_PE[i // TAPS], i % TAPS:i % TAPS + 1]).then_inc(diag_ready, 1)

            def convolved(n):
                c = CONV_PE[n]
                act.wait_ge(tap_done, TAPS * (n + 1))
                act.activation(cacc[:, c, :, :], pb[n][:, :].rearrange("p (s t) -> p s t", s=2), ACT.Identity,
                               bias=C["convb"][:, c:c + 1]).then_inc(conv_out, 1)

            def products(p, most):
                while taps and most > 0 and (p is None or taps[0][0] // 2 * 2 + 1 < p.l):
                    c, j = taps.pop(0)
                    most -= 1
                    src = upad[:, c, :, j:j + T1]
                    if j == 0:
                        act.wait_ge(dw_landed, 16)
                        act.wait_ge(pad_ready, 1)
                        act.wait_ge(u_ready, c + 1)
                        act.activation(cacc[:, c, :, :], src, ACT.Identity, bias=C["convb"][:, c:c + 1],
                                       scale=wdw[:, c, 0:1]).then_inc(conv_init, 1)
                        continue
                    n = 30 * CONV_POOL.index(c) + j - 1
                    if n >= 2:
                        act.wait_ge(cp_used, n - 1)
                    act.activation(ctp[:, n % 2, :].rearrange("p (s t) -> p s t", s=2), src, ACT.Copy,
                                   scale=wdw[:, c, j:j + 1]).then_inc(cp_ready, 1)

            def act_pw1(p):
                ahead(p)
                if p.least % 2:
                    act.wait_ge(block_done, p.b + 1)
                    for m in range(2):
                        n = p.l - 1 + m
                        if n >= 2:
                            act.wait_ge(u_ready, n - 1)
                        act.activation(sgc[:, m, :], pb[2 * p.k + m][:, :], ACT.Sigmoid).then_inc(sig_ready, 1)
                products(p, 7)

            each_block(act, "pw1", act_pw1, roll=False)
            mod_rows(1, 0)
            for i in range(len(CONV_PE) * TAPS):
                diagonal(i)
                products(None, 1)
            products(None, 6)
            convolved(0)
            for m in range(1, 4):
                products(None, 5)
                mod_rows(1, m)
            products(None, 1000)
            for u in range(KD):
                act.wait_ge(cen_ready, u + 1)
                if u >= 4:
                    act.wait_ge(vsum_done, u - 3)
                act.activation(csq[:, u % 4, :], cacc[:, u, :, :].rearrange("p s t -> p (s t)"), ACT.Square)\
                   .then_inc(vsq_ready, 1)
            act.wait_ge(vsum_done, KD)
            act.activation(rstd[:, :], pb[6][:, :], ACT.Sqrt, scale=1.0 / D, bias=epsb).then_inc(lstd_ready, 1)
            for u in range(KD):
                act.wait_ge(lnx_ready, u + 1)
                act.activation(csq[:, u % 4, :], cacc[:, u, :, :].rearrange("p s t -> p (s t)"), ACT.Sigmoid)\
                   .then_inc(lns_ready, 1)
                if u >= 1:
                    v = u - 1
                    act.wait_ge(lny_ready, v + 1)
                    act.activation(ahi[:, 512 * v:512 * v + 512], cacc[:, v, :, :].rearrange("p s t -> p (s t)"),
                                   ACT.Copy).then_inc(lnhi_ready, 1)
            act.wait_ge(lny_ready, KD)
            act.activation(ahi[:, 512 * 7:4096], cacc[:, 7, :, :].rearrange("p s t -> p (s t)"),
                           ACT.Copy).then_inc(lnhi_ready, 1)
            mod_rows(1, 4)
            mod_rows(1, 5)
            ph[0] = "pw2"
            each_block(act, "pw2", ahead)

            def relus(p):
                ahead(p)
                act.wait_ge(block_done, p.b + 1)
                one = ph[0] == "ff1b"
                for m in range(1 if one else 2):
                    if one:
                        n, w = p.l, 32 + p.l
                        par, src = (p.least % 2), pb[p.k]
                        first = p.least < 2
                    else:
                        n, w = p.l * 2 + m, p.l * 2 + m
                        par, src = m, pb[2 * p.k + m]
                        first = p.least < 1
                    if not first:
                        act.wait_ge(hid_sq, w - 1)
                    act.activation(rl[:, par, :], src[:, :], ACT.Relu).then_inc(relu_ready, 1)

            squares(act, 4, lambda u: [(evac["pw2"], u + 1)])
            std(act, 4)
            hi_parts(act, 4)
            ph[0] = "ff1a"
            each_block(act, "ff1a", relus)

            def down2(name, hbase, w, u_at):
                ph[0] = name
                act.wait_ge(block_done, FIRST[name])
                base = FIRST[name]
                for l in (-2, -1):
                    act.wait_ge(hid_sq, hbase + (2 if w == 1024 else 1) * (l + 3))
                    hidden_hi(l, base, 16, w, hid, u_at, l)
                act.wait_ge(hid_sq, hbase + (32 if w == 1024 else 16))

                def body(p):
                    hidden_hi(p.l, base, 16, w, hid, u_at, p.least)
                    ahead(p)

                each_block(act, name, body, roll=False)

            down2("ff2a", 0, 1024, 0)
            squares(act, 5, lambda u: [(evac["ff2a"], u + 1)])
            std(act, 5)
            hi_parts(act, 5)

            ph[0] = "qkv"
            for l in range(6):
                p = Pos(FIRST["qkv"] + l, l)
                ahead(p)
                act.wait_ge(block_done, p.b + 1)
                if l == 0:
                    for m in range(2):
                        c = act.activation(kg[:, m, :], pb[m][:, :], ACT.Copy)
                elif l == 1:
                    for a in range(2):
                        c = act.activation(vg[:, 2 * a:2 * a + 2, :], pb[2 + a][:, :].rearrange("p (a w) -> p a w", a=2),
                                           ACT.Copy)
                else:
                    c = act.activation(qg[:, 2 * (l - 2):2 * (l - 2) + 2, :],
                                       pb[2 + l][:, :].rearrange("p (a t) -> p a t", a=2), ACT.Copy)
                c.then_inc(evac["qkv"], 1)

            act.wait_ge(evac["qkv"], 6)
            allqk = area(0, 3072)
            for n in range(6):
                act.activation(gsq[:, 512 * n:512 * n + 512], allqk[:, 512 * n:512 * n + 512], ACT.Square)\
                   .then_inc(gq_sq, 1)
            for n in range(6):
                act.wait_ge(gq_ms, n + 1)
                act.activation(gsq[:, 512 * n:512 * n + 512], pb[n % 4][:, :], ACT.Sqrt, scale=1.0 / 64, bias=epsb)\
                   .then_inc(gq_std, 1)

            def gexp(h):
                for qt in range(2):
                    act.wait_ge(nmax_ready, TR + h + 1)
                    if h >= 2 and qt == 0:
                        act.wait_ge(pt_done, TR + h - 1)
                    act.activation(pg[:, h % 2, qt, :], pb[2 * (h % 2) + qt][:, :], ACT.Exp,
                                   bias=stat[:, 16 + 2 * (h % 2) + qt:17 + 2 * (h % 2) + qt], scale=0.125,
                                   accum_out=stat[:, 20 + 2 * (h % 2) + qt:21 + 2 * (h % 2) + qt]).then_inc(exp_done, 1)

            def gpt(h):
                act.wait_ge(pt_done, TR + h + 1)
                if h >= 2:
                    act.wait_ge(o_done, TR + h - 1)
                for s in range(2):
                    c = act.activation(ptg[:, h % 2, 512 * s:512 * s + 512], pb[4 + s][:, :], ACT.Copy)
                c.then_inc(pt_ready, 1)

            def gout(h):
                kh, g = h // 4, h % 4
                lo_, c0 = 64 * (kh % 2), 256 * (4 * (kh // 2) + g)
                act.wait_ge(o_done, TR + h + 1)
                act.activation(ahi[lo_:lo_ + 64, c0:c0 + 256], pb[6 + h % 2][lo_:lo_ + 64, 0:256], ACT.Copy)\
                   .then_inc(ohi_ready, 1)

            for h in range(1, 16 + 4):
                if h - 1 < 16:
                    gexp(h - 1)
                if h >= 4:
                    gout(h - 4)
                if 0 <= h - 2 < 16:
                    gpt(h - 2)
            ph[0] = "wo"
            each_block(act, "wo", ahead)
            squares(act, 6, lambda u: [(evac["wo"], u + 1)])
            std(act, 6)
            hi_parts(act, 6)
            ph[0] = "ff1b"
            each_block(act, "ff1b", relus)
            down2("ff2b", 32, 512, 2048)

        @block.vector
        def _(dve):
            chain = [0]

            def link(ins):
                chain[0] += 1
                ins.then_inc(dch, 1)
                dve.wait_ge(dch, chain[0])

            def lo(p_b, k):
                dve.wait_ge(whi_ready, p_b + 3)
                dve.tensor_tensor(wlo[:, k % 2, :], raw[:, (k + 2) % 4, :], whi[:, k % 2, :].bitcast(F32),
                                  ALU.subtract).then_inc(wlo_ready, 1)

            ph = ["in"]

            def ahead(p):
                if not (p.least + 2 >= COUNT[ph[0]] and ph[0] == PHASES[-1][0]):
                    lo(p.b, p.k)

            def reduce_angle(a, k, tmp, width):
                link(dve.tensor_scalar(k, a, 1.0 / TWO_PI, MAGIC, ALU.mult, ALU.add))
                link(dve.tensor_scalar(k, k, -MAGIC, None, ALU.add))
                for c in (C1, C2, C3):
                    link(dve.scalar_tensor_tensor(a, k, -c, a, ALU.mult, ALU.add))
                link(dve.tensor_scalar(a, a, PI_LO, -PI_LO, ALU.min, ALU.max))
                link(dve.tensor_scalar(tmp, a, np.pi / 2, None, ALU.add))
                link(dve.tensor_scalar(k, tmp, np.pi, -TWO_PI, ALU.is_gt, ALU.mult))
                link(dve.tensor_tensor(tmp, tmp, k, ALU.add))
                link(dve.tensor_scalar(tmp, tmp, PI_LO, -PI_LO, ALU.min, ALU.max))

            def exact_exp(dst, a, k, r, bits):
                link(dve.tensor_scalar(a, a, -87.0, 88.0, ALU.max, ALU.min))
                link(dve.tensor_scalar(k, a, L2E, MAGIC, ALU.mult, ALU.add))
                link(dve.tensor_scalar(k, k, -MAGIC, None, ALU.add))
                link(dve.tensor_scalar(k, k, -126.0, 127.0, ALU.max, ALU.min))
                link(dve.scalar_tensor_tensor(r, k, -LN2A, a, ALU.mult, ALU.add))
                link(dve.scalar_tensor_tensor(r, k, -LN2B, r, ALU.mult, ALU.add))
                link(dve.tensor_scalar(k, k, 127.0, 8388608.0, ALU.add, ALU.mult))
                link(dve.tensor_copy(bits.bitcast(I32), k))
                link(dve.tensor_scalar(dst, r, 1.0 / 5040, 1.0 / 720, ALU.mult, ALU.add))
                for c in (1 / 120, 1 / 24, 1 / 6, 0.5, 1.0, 1.0):
                    link(dve.tensor_tensor(dst, dst, r, ALU.mult))
                    link(dve.tensor_scalar(dst, dst, c, None, ALU.add))
                link(dve.tensor_tensor(dst, dst, bits, ALU.mult))

            dve.memset(scc[:, 16:46], 0.0)
            dve.memset(stat[:, 60:61], EPS).then_inc(am_ready, 1)
            dve.wait_ge(cst_landed, 16)
            dt_, mag, th = sp[:, 0, :], sp[:, 1, :], sp[:, 6, :]
            exact_exp(dt_, C["ldt"], sp[:, 2, :], sp[:, 3, :], sp[:, 4, :])
            link(dve.tensor_tensor(sp[:, 5, :], C["lr"], dt_, ALU.mult))
            exact_exp(mag, sp[:, 5, :], sp[:, 2, :], sp[:, 3, :], sp[:, 4, :])
            link(dve.tensor_tensor(th, C["li"], dt_, ALU.mult))
            reduce_angle(th, sp[:, 2, :], sp[:, 7, :], 16)
            dve.tensor_copy(sp[:, 2, :], sp[:, 7, :]).then_inc(sin_in, 1)

            def reciprocal_std(r):
                w = 256 if NU[r] == 4 else 512
                dve.wait_ge(std_ready, r + 1)
                link(dve.reciprocal(rstd[:, 0:w], rstd[:, 0:w]))

            def halves(ap, w):
                return ap[:, 0:w].rearrange("p (a t) -> p a t", t=256)

            def norm_gain(r, g, prior):
                reciprocal_std(r)
                for u in range(4):
                    nb = ring(NB_AT[r], u)
                    for a in range(2):
                        c = 2 * u + a
                        dst = X[:, 0, c, :] if r == 2 else nb[:, a, :]
                        i = dve.scalar_tensor_tensor(dst, X[:, 0, c, :], g[:, c:c + 1], rstd[:, 0:256],
                                                     ALU.mult, ALU.mult)
                    i.then_inc(n_ready, 1)

            dve.wait_ge(x_landed, 16)
            norm_gain(0, C["gmix"], None)
            for b in range(2):
                dve.wait_ge(whi_ready, b + 1)
                dve.tensor_tensor(wlo[:, b, :], raw[:, b, :], whi[:, b, :].bitcast(F32), ALU.subtract)\
                   .then_inc(wlo_ready, 1)

            dve.wait_ge(pos_landed, 16)
            ang, cosa, kk = posw[:, 1, :], posw[:, 2, :], posw[:, 3, :]
            link(dve.tensor_copy(ang, posw[:, 0, :].bitcast(I32)))
            link(dve.tensor_scalar(ang, ang, C["invf"][0:32, :], None, ALU.mult))
            reduce_angle(ang, kk, cosa, 256)
            dve.tensor_copy(kk, cosa).then_inc(sin_in, 1)

            dve.wait_ge(sin_out, 2)
            zr, zi, den, t0, t1 = (sp[:, n, :] for n in (10, 11, 12, 13, 14))
            lr, li = C["lr"], C["li"]
            link(dve.tensor_tensor(t0, mag, sp[:, 9, :], ALU.mult))
            link(dve.tensor_scalar(t0, t0, -1.0, None, ALU.add))
            link(dve.tensor_tensor(t1, mag, sp[:, 8, :], ALU.mult))
            link(dve.tensor_tensor(den, lr, lr, ALU.mult))
            link(dve.tensor_tensor(zr, li, li, ALU.mult))
            link(dve.tensor_tensor(den, den, zr, ALU.add))
            link(dve.reciprocal(den, den))
            link(dve.tensor_tensor(zr, t0, lr, ALU.mult))
            link(dve.tensor_tensor(sp[:, 15, :], t1, li, ALU.mult))
            link(dve.tensor_tensor(zr, zr, sp[:, 15, :], ALU.add))
            link(dve.tensor_tensor(zr, zr, den, ALU.mult))
            link(dve.tensor_tensor(zi, t1, lr, ALU.mult))
            link(dve.tensor_tensor(sp[:, 15, :], t0, li, ALU.mult))
            link(dve.tensor_tensor(zi, zi, sp[:, 15, :], ALU.subtract))
            link(dve.tensor_tensor(zi, zi, den, ALU.mult))
            dve.wait_ge(ssm_landed, 32)
            dve.wait_ge(nlo_ready, 4)

            def zb(z):
                return z.unsqueeze(2).broadcast_to([P, NTILE, 32])

            link(dve.tensor_tensor(ct[:, 0], crw[:, 0], zb(zr), ALU.mult))
            link(dve.tensor_tensor(ctt[:, 0], crw[:, 1], zb(zi), ALU.mult))
            link(dve.tensor_tensor(ct[:, 0], ct[:, 0], ctt[:, 0], ALU.subtract))
            link(dve.tensor_tensor(ct[:, 1], crw[:, 0], zb(zi), ALU.mult))
            link(dve.tensor_tensor(ctt[:, 1], crw[:, 1], zb(zr), ALU.mult))
            link(dve.tensor_tensor(ct[:, 1], ct[:, 1], ctt[:, 1], ALU.add))
            link(dve.tensor_scalar(ct[:, 1], ct[:, 1], -1.0, None, ALU.mult))
            dve.wait_ge(scc_ready, 1)
            dve.tensor_tensor(scc[:, 0:16], scc[:, 0:16], C["cc"], ALU.mult).then_inc(ct_ready, 1)

            def ssm_in(j):
                s, jj = j // 2 % 2, j % 2
                bu = pb[2 + 2 * (j % 2)][:, :].rearrange("p (s t) -> p s t", s=2)
                cb = tab[:, s, 0, jj, :].unsqueeze(1).broadcast_to([P, 2, T1])
                sbb = tab[:, s, 1, jj, :].unsqueeze(1).broadcast_to([P, 2, T1])
                dve.wait_ge(tab_ready, j // 2 + 1)
                dve.wait_ge(bu_done, j + 1)
                dve.tensor_tensor(p1, bu, cb, ALU.mult)
                dve.tensor_tensor(p2, bu, sbb, ALU.mult).then_inc(bu_used, 1)
                dve.wait_ge(bu_used, j + 1)
                dve.tensor_tensor(w_s[:, 0, :], p1[:, 0, :], p2[:, 1, :], ALU.add)
                link(dve.tensor_tensor(w_s[:, 1, :], p1[:, 1, :], p2[:, 0, :], ALU.subtract))
                if j >= 2:
                    dve.wait_ge(h_ready, j - 1)
                m = mag[:, j:j + 1].broadcast_to([P, T1])
                dve.tensor_tensor_scan(g_s[:, j % 2, 0, :], m, w_s[:, 0, :], 0.0, ALU.mult, ALU.add)
                dve.tensor_tensor_scan(g_s[:, j % 2, 1, :], m, w_s[:, 1, :], 0.0, ALU.mult, ALU.add)\
                   .then_inc(g_ready, 1)

            def ssm_out(c):
                dve.wait_ge(y_done, 4 * c + 4)
                dve.scalar_tensor_tensor(u_s[:, c, :], u_s[:, c, :], C["dskip"][:, c:c + 1],
                                         pb[6][:, 256 * (c % 2):256 * (c % 2) + 256], ALU.mult, ALU.add)\
                   .then_inc(ysum_ready, 1)

            def rotate(n):
                t = q_s if n < 6 else k_s
                m = n % 6
                part = t[0:32, 2 * m:2 * m + 2, :]
                cb = rope[0:32, 0, :].unsqueeze(1).broadcast_to([32, 2, T1])
                sbb = rope[0:32, 1, :].unsqueeze(1).broadcast_to([32, 2, T1])
                if n == 0:
                    dve.wait_ge(sin_out, 4)
                dve.wait_ge(rot_done, n + 1)
                dve.tensor_tensor(rotb, pb[3][0:32, :].rearrange("p (a t) -> p a t", a=2), sbb, ALU.mult)
                link(dve.tensor_tensor(part, part, cb, ALU.mult))
                dve.tensor_tensor(part, part, rotb, ALU.add).then_inc(roped, 1)

            def attention_max(n):
                w = 384 if n % 2 == 0 else 768
                dve.wait_ge(s_done, n + 1)
                if n == 0:
                    dve.wait_ge(mask_landed, 16)
                    dve.wait_ge(y_done, NTILE)
                if n >= 1:
                    dve.wait_ge(exp_done, n)
                for kt in range(1 + n % 2):
                    mk = (mask0 if n % 2 == 0 else mask1)[:, 384 * kt:384 * kt + 384]
                    i = dve.scalar_tensor_tensor(sm[:, 384 * kt:384 * kt + 384], pb[4 + kt][:, 0:384],
                                                 HD ** -0.5, mk, ALU.mult, ALU.add)
                i.then_inc(s_used, 1)
                dve.wait_ge(s_used, n + 1)
                link(dve.reduce_max(stat[:, 24:25], sm[:, 0:w], AX_X))
                dve.tensor_scalar(stat[:, n:n + 1], stat[:, 24:25], -1.0, None, ALU.mult).then_inc(nmax_ready, 1)

            def attention_scale(n):
                w = 384 if n % 2 == 0 else 768
                dve.wait_ge(exp_done, n + 1)
                link(dve.reciprocal(stat[:, 25:26], stat[:, 8 + n:9 + n]))
                dve.tensor_scalar(pr[:, n % 2, 0:w], pr[:, n % 2, 0:w], stat[:, 25:26], None, ALU.mult)\
                   .then_inc(pn_ready, 1)

            def attention_lo(n):
                c0 = 2048 + 256 * (n // 2) + 128 * (n % 2)
                dve.wait_ge(ohi_ready, n + 1)
                dve.tensor_tensor(alo[:, c0:c0 + 128], pb[6][:, 0:128], ahi[:, c0:c0 + 128].bitcast(F32),
                                  ALU.subtract).then_inc(olo_ready, 1)

            def attention(n):
                if 0 <= n - 4 < TR:
                    attention_lo(n - 4)
                if 0 <= n - 1 < TR:
                    attention_max(n - 1)
                    attention_scale(n - 1)

            def store_mods(layer):
                dve.wait_ge(mod_turned, 6 * layer + 6)
                for n in range(2):
                    own = [t.rearrange("p (m g n) -> p m g n", m=6, n=2)[:, :, :, n] for t in
                           (C["bmod"][:, MODS * layer:MODS * layer + MODS],)][0]
                    i = dve.tensor_tensor(
                        mods[:, layer, :, :].rearrange("p (a n) s -> p a n s", n=2)[:, :, n, :]
                        .rearrange("p (m g) s -> p m g s", m=6),
                        pb[7][:, 256:352].rearrange("p (m n g s) -> p m n g s", m=6, n=2, g=4)[:, :, n, :, :],
                        own.unsqueeze(3).broadcast_to([P, 6, 4, 2]), ALU.add)
                i.then_inc(mod_ready, 1)

            for l in range(28):
                if l in (9, 13, 17, 21):
                    ssm_out((l - 9) // 4)
                if Q0 <= l - 1 < V0:
                    rotate(l - 1 - Q0)
                attention(l - GATE0)
                ahead(Pos(l, l))
                if 3 <= l < 3 + NTILE:
                    ssm_in(l - 3)
            for n in range(8, TR + 4):
                attention(n)
            store_mods(0)

            ph[0] = "attnproj"

            def dve_attnproj(p):
                ahead(p)
                dve.wait_ge(block_done, p.b + 1)
                dve.wait_ge(gate_ready, 8)
                for s in range(2):
                    i = dve.tensor_tensor(mix[:, 1024 * p.l + 512 * s:1024 * p.l + 512 * s + 512],
                                          pb[2 * p.l + s][:, :],
                                          area(GATES, 4096)[:, 1024 * p.l + 512 * s:1024 * p.l + 512 * s + 512],
                                          ALU.mult)
                i.then_inc(evac["attnproj"], 1)

            each_block(dve, "attnproj", dve_attnproj)
            ph[0] = "glu"
            for l in range(4):
                p = Pos(FIRST["glu"] + l, l)
                ahead(p)
                if l % 2 == 0:
                    continue
                j = l // 2
                dve.wait_ge(gsig_ready, j + 1)
                for s in range(2):
                    i = dve.tensor_tensor(glut[:, 512 * s:512 * s + 512], glus[:, 512 * s:512 * s + 512],
                                          pb[4 + s][:, :], ALU.mult)
                i.then_inc(evac["glu"], 2)
                dve.wait_ge(evac["glu"], 2 * (j + 1))
                link(dve.tensor_tensor(glut, glut, area(GATES + 2048 + 1024 * j, 1024), ALU.mult))
                dve.tensor_tensor(mix[:, 1024 * j:1024 * j + 1024], mix[:, 1024 * j:1024 * j + 1024], glut, ALU.add)\
                   .then_inc(mix_ready, 1)
            for j in range(4):
                dve.wait_ge(mixhi_ready, j + 1)
                dve.tensor_tensor(alo[:, 512 * j:512 * j + 512], mix[:, 512 * j:512 * j + 512],
                                  ahi[:, 512 * j:512 * j + 512].bitcast(F32), ALU.subtract).then_inc(mixlo_ready, 1)
            ph[0] = "out"

            def add_to_x(name, p, bank):
                dve.wait_ge(block_done, p.b + 1)
                xu = X[:, 0, 2 * p.l:2 * p.l + 2, :]
                dve.tensor_tensor(xu, xu, bank[:, :].rearrange("p (a t) -> p a t", a=2), ALU.add)\
                   .then_inc(evac[name], 1)
                ahead(p)

            each_block(dve, "out", lambda p: add_to_x("out", p, pb[p.l]))
            norm_gain(1, C["gffn"], None)
            ph[0] = "ffn"

            def dve_ffn(p):
                if p.least % 2 == 0:
                    ahead(p)
                    return
                r = p.least // 2 % 2
                dve.wait_ge(sig_ready, p.h + 1)
                dve.tensor_tensor(tg1[:, r, :], sg1[:, r, :], pb[(p.k + 3) % 4][:, :], ALU.mult).then_inc(th_ready, 1)
                dve.wait_ge(th_ready, p.h + 1)
                dve.wait_ge(block_done, p.b + 1)
                dve.tensor_tensor(hid1[:, bass.ds(512 * p.h, 512)], tg1[:, r, :], pb[p.k][:, :], ALU.mult)\
                   .then_inc(evac["ffn"], 2)
                ahead(p)

            each_block(dve, "ffn", dve_ffn)
            ph[0] = "down"
            each_block(dve, "down", ahead, roll=False)
            dve.wait_ge(block_done, FIRST["ple"])
            for u in range(4):
                xu = X[:, 0, 2 * u:2 * u + 2, :]
                dve.tensor_tensor(xu, xu, pb[u][:, :].rearrange("p (a t) -> p a t", a=2), ALU.add)\
                   .then_inc(evac["down"], 1)
            for u in range(4):
                dve.wait_ge(xhi_ready, u + 1)
                dve.tensor_tensor(alo[:, 512 * u:512 * u + 512].rearrange("p (a t) -> p a t", a=2),
                                  X[:, 0, 2 * u:2 * u + 2, :],
                                  ahi[:, 512 * u:512 * u + 512].bitcast(F32).rearrange("p (a t) -> p a t", a=2),
                                  ALU.subtract).then_inc(xlo_ready, 1)
            ph[0] = "ple"
            for l in range(5):
                p = Pos(FIRST["ple"] + l, l)
                if l:
                    u = l - 1
                    s = area(8704 + 512 * u, 512)
                    dve.wait_ge(sig_ready, 11 + u + 1)
                    dve.wait_ge(plep_ready, 1)
                    link(dve.tensor_tensor(s, s, plep[:, 512 * u:512 * u + 512], ALU.mult))
                    xu = X[:, 0, 2 * u:2 * u + 2, :]
                    dve.tensor_tensor(xu, xu, s.rearrange("p (a t) -> p a t", a=2), ALU.add).then_inc(evac["ple"], 1)
                ahead(p)
            norm_gain(2, C["gfinal"], None)

            def modulate_amul(layer, s, g):
                sc = mods[:, layer, 8 * s:8 * s + 8, :]
                gb = g.unsqueeze(2).broadcast_to([P, 8, 2])
                link(dve.scalar_tensor_tensor(amul[:, :, :], sc, 1.0, gb, ALU.add, ALU.mult))

            def norm_mod(r, layer, shift, g):
                modulate_amul(layer, shift + 1, g)
                reciprocal_std(r)
                rs = rstd[:, :].rearrange("p (s t) -> p s t", s=2)
                nb0 = NBASE[r] - 4 * (r > 2)
                for u in range(NU[r]):
                    nb = ring(NB_AT[r], u)
                    if u >= 4:
                        dve.wait_ge(nlo_ready, nb0 + u - 3)
                    if NU[r] == 8:
                        link(dve.tensor_tensor(nb, X[:, :, u, :], rs, ALU.mult))
                        for s in range(2):
                            i = dve.tensor_scalar(nb[:, s, :], nb[:, s, :], amul[:, u, s:s + 1],
                                                  mods[:, layer, 8 * shift + u, s:s + 1], ALU.mult, ALU.add)
                    else:
                        link(dve.tensor_tensor(nb, X[:, 0, 2 * u:2 * u + 2, :],
                                               rstd[:, 0:256].unsqueeze(1).broadcast_to([P, 2, T1]), ALU.mult))
                        for a in range(2):
                            c = 2 * u + a
                            i = dve.tensor_scalar(nb[:, a, :], nb[:, a, :], amul[:, c, 0:1],
                                                  mods[:, layer, 8 * shift + c, 0:1], ALU.mult, ALU.add)
                    i.then_inc(n_ready, 1)

            norm_mod(3, 0, 0, C["g1"][:, 0:8])

            ph[0] = "pw1"
            taps = [(c, j) for c in CONV_DVE for j in range(31)]

            def convolve(p, most):
                while taps and most > 0 and (p is None or taps[0][0] // 2 * 2 + 1 <= p.l):
                    c, j = taps.pop(0)
                    most -= 1
                    src, acc = upad[:, c, :, j:j + T1], cacc[:, c, :, :]
                    if j == 0:
                        dve.wait_ge(dw_landed, 16)
                        dve.wait_ge(pad_ready, 1)
                        dve.wait_ge(u_ready, c + 1)
                        link(dve.tensor_scalar(acc, src, wdw[:, c, 0:1], C["convb"][:, c:c + 1], ALU.mult, ALU.add))
                    elif j < 30:
                        link(dve.scalar_tensor_tensor(acc, src, wdw[:, c, j:j + 1], acc, ALU.mult, ALU.add))
                    else:
                        dve.scalar_tensor_tensor(acc, src, wdw[:, c, j:j + 1], acc, ALU.mult, ALU.add)\
                           .then_inc(conv_dve, 1)

            def dve_pw1(p):
                if p.least % 2:
                    for m in range(2):
                        c = p.l - 1 + m
                        dve.wait_ge(sig_ready, 15 + c + 1)
                        dve.tensor_tensor(upad[:, c, :, 15:15 + T1],
                                          sgc[:, m, :].rearrange("p (s t) -> p s t", s=2),
                                          pb[2 * ((p.k + 3) % 4) + m][:, :].rearrange("p (s t) -> p s t", s=2),
                                          ALU.mult).then_inc(u_ready, 1)
                ahead(p)
                convolve(p, 10)

            each_block(dve, "pw1", dve_pw1, roll=False)
            convolve(None, 1000)
            dve.wait_ge(msum_done, 1)
            link(dve.tensor_scalar(mean_s, pb[6][:, :], 1.0 / D, None, ALU.mult))
            for u in range(KD):
                cu = cacc[:, u, :, :].rearrange("p s t -> p (s t)")
                dve.tensor_tensor(cu, cu, mean_s, ALU.subtract).then_inc(cen_ready, 1)
            dve.wait_ge(lstd_ready, 1)
            link(dve.reciprocal(rstd[:, :], rstd[:, :]))
            for u in range(KD):
                cu = cacc[:, u, :, :].rearrange("p s t -> p (s t)")
                link(dve.tensor_tensor(cu, cu, rstd[:, :], ALU.mult))
                dve.tensor_scalar(cu, cu, C["lng"][:, u:u + 1], C["lnb"][:, u:u + 1], ALU.mult, ALU.add)\
                   .then_inc(lnx_ready, 1)
                if u >= 1:
                    v = u - 1
                    cv = cacc[:, v, :, :].rearrange("p s t -> p (s t)")
                    dve.wait_ge(lns_ready, v + 1)
                    dve.tensor_tensor(cv, cv, csq[:, v % 4, :], ALU.mult).then_inc(lny_ready, 1)
            cv = cacc[:, 7, :, :].rearrange("p s t -> p (s t)")
            dve.wait_ge(lns_ready, 8)
            dve.tensor_tensor(cv, cv, csq[:, 3, :], ALU.mult).then_inc(lny_ready, 1)

            def gated_add(layer, gate, c, s, src):
                xs = X[:, s, c, :]
                return dve.scalar_tensor_tensor(xs, src, mods[:, layer, 8 * gate + c, s:s + 1], xs,
                                                ALU.mult, ALU.add)

            ph[0] = "pw2"
            for l in range(4):
                p = Pos(FIRST["pw2"] + l, l)
                dve.wait_ge(block_done, p.b + 1)
                if l == 2:
                    store_mods(1)
                for m in range(2):
                    for s in range(2):
                        i = gated_add(0, 2, 2 * l + m, s, pb[2 * p.k + m][:, 256 * s:256 * s + 256])
                    i.then_inc(evac["pw2"], 1)
                ahead(p)
            norm_mod(4, 0, 3, C["g2"][:, 0:8])
            ph[0] = "ff1a"

            def squares_ff(p):
                ahead(p)

            each_block(dve, "ff1a", squares_ff)
            ph[0] = "ff2a"
            each_block(dve, "ff2a", ahead)
            dve.wait_ge(block_done, FIRST["qkv"])
            for c in range(8):
                for s in range(2):
                    i = gated_add(0, 5, c, s, pb[c][:, 256 * s:256 * s + 256])
                i.then_inc(evac["ff2a"], 1)
            norm_mod(5, 1, 0, C["g1"][:, 8:16])

            ph[0] = "qkv"
            for l in range(6):
                ahead(Pos(FIRST["qkv"] + l, l))
            dve.wait_ge(gtab_landed, 16)
            for n in range(6):
                x = area(512 * n, 512)
                rs = gsq[:, 512 * n:512 * n + 512]
                dve.wait_ge(gq_std, n + 1)
                link(dve.reciprocal(rs, rs))
                g = C["qn"] if n < 4 else C["kn"]
                dve.scalar_tensor_tensor(x, x, g, rs, ALU.mult, ALU.mult).then_inc(gq_n, 1)
            for n in range(6):
                x = area(512 * n, 512)
                if n < 4:
                    part = x.rearrange("p (a t) -> p a t", a=2)
                    rot = pb[n][:, :].rearrange("p (a t) -> p a t", a=2)
                    cb, sbb = (gtab[:, s, :].unsqueeze(1).broadcast_to([P, 2, T1]) for s in range(2))
                    a, b = (t[:, n % 2, :].rearrange("p (a t) -> p a t", a=2) for t in (gt1, gt2))
                else:
                    part, rot = x[:, 0:256], pb[n - 4][:, 0:256]
                    cb, sbb = gtab[:, 0, :], gtab[:, 1, :]
                    a, b = gt1[:, n % 2, 0:256], gt2[:, n % 2, 0:256]
                dve.wait_ge(gq_rot, n + 1)
                dve.tensor_tensor(b, rot, sbb, ALU.mult)
                link(dve.tensor_tensor(a, part, cb, ALU.mult))
                dve.tensor_tensor(part, a, b, ALU.add).then_inc(gq_ready, 1)

            def gmax(h):
                s0, s1 = 16 + 2 * (h % 2), 32 + 2 * (h % 2)
                dve.wait_ge(s_done, TR + h + 1)
                for qt in range(2):
                    i = dve.reduce_max(stat[:, s1 + qt:s1 + qt + 1], pb[2 * (h % 2) + qt][:, :], AX_X)
                link(i)
                dve.tensor_scalar(stat[:, s0:s0 + 2], stat[:, s1:s1 + 2], -0.125, None, ALU.mult).then_inc(nmax_ready, 1)

            def gscale(h):
                s0, s1 = 20 + 2 * (h % 2), 36 + 2 * (h % 2)
                dve.wait_ge(exp_done, TR + 2 * (h + 1))
                link(dve.reciprocal(stat[:, s1:s1 + 2], stat[:, s0:s0 + 2]))
                for qt in range(2):
                    i = dve.tensor_scalar(pg[:, h % 2, qt, :], pg[:, h % 2, qt, :], stat[:, s1 + qt:s1 + qt + 1],
                                          None, ALU.mult)
                i.then_inc(pn_ready, 1)

            def glo(h):
                kh, g = h // 4, h % 4
                l0, c0 = 64 * (kh % 2), 256 * (4 * (kh // 2) + g)
                dve.wait_ge(ohi_ready, 8 + h + 1)
                dve.tensor_tensor(alo[l0:l0 + 64, c0:c0 + 256], pb[6 + h % 2][l0:l0 + 64, 0:256],
                                  ahi[l0:l0 + 64, c0:c0 + 256].bitcast(F32), ALU.subtract).then_inc(olo_ready, 1)

            for h in range(1, 16 + 4):
                if h - 1 < 16:
                    gmax(h - 1)
                if h >= 4:
                    glo(h - 4)
                if h - 1 < 16:
                    gscale(h - 1)
            ph[0] = "wo"
            for l in range(4):
                p = Pos(FIRST["wo"] + l, l)
                dve.wait_ge(block_done, p.b + 1)
                for m in range(2):
                    i = gated_add(1, 2, 2 * l + m, 0, pb[l][:, 256 * m:256 * m + 256])
                i.then_inc(evac["wo"], 1)
                ahead(p)
            norm_mod(6, 1, 3, C["g2"][:, 8:16])
            ph[0] = "ff1b"
            each_block(dve, "ff1b", squares_ff)
            ph[0] = "ff2b"
            each_block(dve, "ff2b", ahead)
            dve.wait_ge(block_done, NBLOCKS)
            for c in range(8):
                gated_add(1, 5, c, 0, pb[c // 2][:, 256 * (c % 2):256 * (c % 2) + 256]).then_inc(evac["ff2b"], 1)

        @block.gpsimd
        def _(pool):
            chain = [0]

            def link(ins):
                chain[0] += 1
                ins.then_inc(pch, 1)
                pool.wait_ge(pch, chain[0])

            pool.memset(tab[:, :, 0, :, 0:1], 1.0)
            link(pool.memset(tab[:, :, 1, :, 0:1], 0.0))
            lo_parts(pool, 0)
            pool.wait_ge(sin_out, 2)
            link(pool.tensor_copy(powers[:, 0, 0, :], sp[:, 9, :]))
            link(pool.tensor_copy(powers[:, 0, 1, :], sp[:, 8, :]))
            for n in range(1, 8):
                c, s = powers[:, n - 1, 0, :], powers[:, n - 1, 1, :]
                a, b = tta[:, 0:16], ttb[:, 0:16]
                pool.tensor_tensor(a, c, c, ALU.mult)
                link(pool.tensor_tensor(b, s, s, ALU.mult))
                pool.tensor_tensor(powers[:, n, 0, :], a, b, ALU.subtract)
                link(pool.tensor_tensor(tta[:, 16:32], c, s, ALU.mult))
                link(pool.tensor_tensor(powers[:, n, 1, :], tta[:, 16:32], tta[:, 16:32], ALU.add))

            def tables(g, part):
                if g >= 2 and part == 0:
                    pool.wait_ge(g_ready, 2 * g - 2)
                for n in (range(6), range(6, 8))[part]:
                    w = 1 << n
                    old = tab[:, g % 2, :, :, 0:w]
                    cn, sn = (powers[:, n, s, 2 * g:2 * g + 2].unsqueeze(1).unsqueeze(3)
                              .broadcast_to([P, 2, 2, w]) for s in range(2))
                    a = tta[:, 0:4 * w].rearrange("p (s j t) -> p s j t", s=2, j=2)
                    b = ttb[:, 0:4 * w].rearrange("p (s j t) -> p s j t", s=2, j=2)
                    pool.tensor_tensor(a, old, cn, ALU.mult)
                    link(pool.tensor_tensor(b, old, sn, ALU.mult))
                    pool.tensor_tensor(tab[:, g % 2, 0, :, w:2 * w], a[:, 0], b[:, 1], ALU.subtract)
                    i = pool.tensor_tensor(tab[:, g % 2, 1, :, w:2 * w], a[:, 1], b[:, 0], ALU.add)
                    if n < 7:
                        link(i)
                    else:
                        i.then_inc(tab_ready, 1)
                        pool.wait_ge(tab_ready, g + 1)

            def turn_forward(j):
                s, jj = j // 2 % 2, j % 2
                cb, sbb = (tab[:, s, k, jj, :].unsqueeze(1).broadcast_to([P, 2, T1]) for k in range(2))
                pool.wait_ge(g_ready, j + 1)
                if j >= 2:
                    pool.wait_ge(y_done, j - 1)
                pool.tensor_tensor(q1, g_s[:, j % 2, :, :], cb, ALU.mult)
                link(pool.tensor_tensor(q2, g_s[:, j % 2, :, :], sbb, ALU.mult))
                pool.tensor_tensor(h_s[:, j % 2, 0, :], q1[:, 0, :], q2[:, 1, :], ALU.subtract)
                pool.tensor_tensor(h_s[:, j % 2, 1, :], q1[:, 1, :], q2[:, 0, :], ALU.add).then_inc(h_ready, 1)
                pool.wait_ge(h_ready, j + 1)

            for g in range(2):
                tables(g, 0)
                tables(g, 1)
            for j in range(NTILE):
                if j >= 2 and j // 2 + 1 < 8:
                    tables(j // 2 + 1, j % 2)
                turn_forward(j)
            for c in range(4):
                pool.wait_ge(yhi_ready, c + 1)
                pool.tensor_tensor(alo[:, 3072 + 256 * c:3328 + 256 * c], u_s[:, c, :],
                                   ahi[:, 3072 + 256 * c:3328 + 256 * c].bitcast(F32), ALU.subtract)\
                    .then_inc(ylo_ready, 1)
            for n in range(8):
                pool.wait_ge(evac["in"], GATE0 + n + 1)
                g = gates[:, 2 * n:2 * n + 2, :]
                pool.tensor_scalar(g, g, 0.5, 0.5, ALU.mult, ALU.add).then_inc(gate_ready, 1)
            lo_parts(pool, 1)

            def hidden_lo(n, count, w, h, at):
                for l in range(count):
                    s = l % 4
                    pool.wait_ge(hhi_ready, n + l + 1)
                    pool.tensor_tensor(alo[:, at + w * s:at + w * s + w], h[:, w * l:w * l + w],
                                       ahi[:, at + w * s:at + w * s + w].bitcast(F32), ALU.subtract)\
                        .then_inc(hlo_ready, 1)

            hidden_lo(0, 11, 512, hid1, 2048)
            pool.wait_ge(phi_ready, 1)
            pool.tensor_tensor(alo[:, 3584:4096], pin, ahi[:, 3584:4096].bitcast(F32), ALU.subtract)\
                .then_inc(plo_ready, 1)
            pool.wait_ge(evac["ple"], 4)
            pool.memset(upad[:, :, :, 0:15], 0.0)
            pool.memset(upad[:, :, :, 15 + T1:UPW], 0.0).then_inc(pad_ready, 1)
            lo_parts(pool, 3)
            for i, c in enumerate(CONV_POOL):
                acc = cacc[:, c, :, :]
                pool.wait_ge(conv_init, i + 1)
                for j in range(1, 31):
                    n = 30 * i + j - 1
                    pool.wait_ge(cp_ready, n + 1)
                    if j > 1:
                        pool.wait_ge(cp_used, n)
                    pool.tensor_tensor(acc, acc, ctp[:, n % 2, :].rearrange("p (s t) -> p s t", s=2), ALU.add)\
                        .then_inc(cp_used, 1)
            for u in range(KD):
                pool.wait_ge(lnhi_ready, u + 1)
                pool.tensor_tensor(alo[:, 512 * u:512 * u + 512], cacc[:, u, :, :].rearrange("p s t -> p (s t)"),
                                   ahi[:, 512 * u:512 * u + 512].bitcast(F32), ALU.subtract).then_inc(lnlo_ready, 1)
            lo_parts(pool, 4)

            def squares_of(n, count):
                with pool.Fori(0, count // 2) as i:
                    for m in range(2):
                        pool.wait_ge(relu_ready, 2 * i + (n + m + 1))
                        pool.tensor_tensor(hid[:, bass.ds(1024 * i + 512 * m, 512)], rl[:, m, :], rl[:, m, :],
                                           ALU.mult).then_inc(hid_sq, 1)

            squares_of(0, 32)
            hidden_lo(11, 16, 1024, hid, 0)
            lo_parts(pool, 5)
            lo_parts(pool, 6)
            squares_of(32, 16)
            hidden_lo(27, 16, 512, hid, 2048)

        @block.tensor
        def _(pe):
            def three(out_, w_hi, w_lo, a_hi, a_lo, start, stop, **kw):
                pe.matmul(out_, w_hi, a_hi, start=start, stop=False, **kw)
                pe.matmul(out_, w_hi, a_lo, start=False, stop=False, **kw)
                return pe.matmul(out_, w_lo, a_hi, start=False, stop=stop, **kw)

            def tiles(p, kn):
                w = BLK // kn
                return (t[:, p.k % 2, :].rearrange("p (c m) -> p c m", c=kn) for t in (whi, wlo)), w

            def feature_block(p, kn, outs, at, t, chunk_wait=None):
                pe.wait_ge(wlo_ready, p.b + 1)
                (wh, wl), w = tiles(p, kn)
                for m in range(w // P):
                    for c in range(kn):
                        if chunk_wait and m == 0:
                            chunk_wait(c)
                        mm = three(outs(m), wh[:, c, P * m:P * m + P], wl[:, c, P * m:P * m + P],
                                   ahi[:, at + t * c:at + t * c + t], alo[:, at + t * c:at + t * c + t],
                                   c == 0, c == kn - 1)
                mm.then_inc(block_done, 1)

            def token_block(p, t, na):
                pe.wait_ge(wlo_ready, p.b + 1)
                (wh, wl), _ = tiles(p, KD)
                for a in range(na):
                    for c in range(KD):
                        x0 = t * c + P * a
                        bank = pb[(p.l % 2 if na == 2 else 2 + a // 2)]
                        mm = three(bank[:, 256 * (a % 2):256 * (a % 2) + 256], ahi[:, x0:x0 + P], alo[:, x0:x0 + P],
                                   wh[:, c, :], wl[:, c, :], c == 0, c == KD - 1)
                mm.then_inc(block_done, 1)

            def row_block(p, base, at, t, last, bank0=0):
                pe.wait_ge(wlo_ready, p.b + 1)
                (wh, wl), _ = tiles(p, 2)
                s = at + 2 * t * (p.least % 4)
                per = 512 // t
                for c in range(2):
                    for m in range(8):
                        o_ = pb[bank0 + m // per][:, t * (m % per):t * (m % per) + t]
                        mm = three(o_, wh[:, c, P * m:P * m + P], wl[:, c, P * m:P * m + P],
                                   ahi[:, s + t * c:s + t * c + t], alo[:, s + t * c:s + t * c + t],
                                   p.least == 0 and c == 0 and m % per == 0, last and c == 1,
                                   skip_group_check=True)
                mm.then_inc(block_done, 1)

            def half(bank, m):
                return pb[bank][:, 256 * m:256 * m + 256]

            def mod_piece(layer, t):
                m, c = divmod(t, KD)
                bank = pb[2 + m % 2] if layer else pb[7]
                ring_, landed_ = (modraw1, modraw1_landed) if layer else (modraw, modraw_landed)
                r, k = divmod(t, len(landed_))
                if c == 0 and m >= 1 + layer:
                    pe.wait_ge(modrow_ready, 6 * layer + m - layer)
                pe.wait_ge(landed_[k], 16 * (r + 1))
                for n in range(4):
                    mm = pe.matmul(bank[32 * n:32 * n + 32, 0:256], scc[:, 2 * c:2 * c + 32],
                                   ring_[:, k, 256 * n:256 * n + 256], start=(c == 0), stop=(c == KD - 1))
                mm.then_inc(modraw_used, 1)

            def mod_turn(layer, m):
                pe.wait_ge(modrow_ready, 6 * layer + m + 1)
                pick = C["ident"].rearrange("p (g w) -> p g w", g=4)[:, :, 0:2]
                for n in range(2):
                    x0 = 256 + 16 * m + 8 * n
                    mm = pe.matmul(pb[7][:, x0:x0 + 8], modrow[:, m % 2, P * n:P * n + P], pick,
                                   start=True, stop=True)
                mm.then_inc(mod_turned, 1)

            pe.wait_ge(cst_landed, 16)
            sums(pe, 0)

            def ssm_bu(j):
                r = 32 * (j % 4)
                if j == 0:
                    pe.wait_ge(ssm_landed, 32)
                    pe.wait_ge(evac["in"], 2)
                if j >= 2:
                    pe.wait_ge(bu_used, j - 1)
                for s in range(2):
                    mm = pe.matmul(half(2 + 2 * (j % 2), s), bl[r:r + 32, j // 4, s, :], u_s[r:r + 32, j // 4, :],
                                   start=True, stop=True)
                mm.then_inc(bu_done, 1)

            def ssm_y(j):
                r, c = 32 * (j % 4), j // 4
                if j == 0:
                    pe.wait_ge(ct_ready, 1)
                if c >= 1:
                    pe.wait_ge(ysum_ready, c)
                pe.wait_ge(h_ready, j + 1)
                for s in range(2):
                    mm = pe.matmul(pb[6][r:r + 32, 256 * (c % 2):256 * (c % 2) + 256], ct[:, s, j, :],
                                   h_s[:, j % 2, s, :], start=(s == 0), stop=(s == 1))
                mm.then_inc(y_done, 1)

            def rotation(n):
                t, m = (q_s if n < 6 else k_s), n % 6
                pe.wait_ge(evac["in"], Q0 + n + 1)
                if n >= 1:
                    pe.wait_ge(roped, n)
                pe.matmul(pb[3][0:32, :], C["rotg"][0:32, 0:32], t[0:32, 2 * m:2 * m + 2, :],
                          start=True, stop=True).then_inc(rot_done, 1)

            def scores(n):
                h, qt = n // 2, n % 2
                if n == 0:
                    pe.wait_ge(roped, 12)
                if n >= 1:
                    pe.wait_ge(s_used, n)
                for kt in range(1 + qt):
                    for g in range(NG):
                        mm = pe.matmul(pb[4 + kt][:, P * g:P * g + P], q_s[:, NHG * g + h, P * qt:P * qt + P],
                                       k_s[:, NHG * g + h, P * kt:P * kt + P], start=True, stop=True)
                mm.then_inc(s_done, 1)

            def turn_probs(n):
                pe.wait_ge(pn_ready, n + 1)
                if n >= 1:
                    pe.wait_ge(pt_ready, n)
                for kt in range(1 + n % 2):
                    for g in range(NG):
                        x0 = 384 * kt + P * g
                        mm = pe.transpose(pb[2 + kt][:, P * g:P * g + P], pr[:, n % 2, x0:x0 + P], C["ident"])
                mm.then_inc(pt_done, 1)

            def weigh(n):
                h, qt = n // 2, n % 2
                pe.wait_ge(pt_ready, n + 1)
                if n == 0:
                    pe.wait_ge(evac["in"], GATE0)
                    pe.wait_ge(ysum_ready, 4)
                if n >= 1:
                    pe.wait_ge(olo_ready, n)
                for kt in range(1 + qt):
                    for g in range(NG):
                        mm = pe.matmul(pb[6][:, 0:128], v_s[:, kt, P * (NHG * g + h):P * (NHG * g + h) + P],
                                       pt[:, 384 * kt + P * g:384 * kt + P * g + P],
                                       start=(kt == 0 and g == 0), stop=(kt == qt and g == NG - 1))
                mm.then_inc(o_done, 1)

            def attention(n):
                if 0 <= n < TR:
                    scores(n)
                if 0 <= n - 2 < TR:
                    turn_probs(n - 2)
                if 0 <= n - 3 < TR:
                    weigh(n - 3)

            for l in range(28):
                p = Pos(l, l)
                if l >= 2:
                    pe.wait_ge(evac["in"], l - 1)
                if V0 <= l < GATE0:
                    token_block(p, T1, 2)
                else:
                    feature_block(p, KD, lambda m: half(l % 2, m), 0, T1,
                                  (lambda c: wait_norm(pe, 0, c)) if l == 0 else None)
                if 2 <= l < 26:
                    if l == 2:
                        pe.wait_ge(ct_ready, 1)
                    if l % 4 == 2 and l > 2:
                        mod_turn(0, (l - 6) // 4)
                    mod_piece(0, 2 * (l - 2))
                    mod_piece(0, 2 * (l - 2) + 1)
                if l == 26:
                    mod_turn(0, 5)
                if Q0 <= l - 1 < V0:
                    rotation(l - 1 - Q0)
                if 3 <= l < 3 + NTILE:
                    ssm_bu(l - 3)
                if 5 <= l < 5 + NTILE:
                    ssm_y(l - 5)
                attention(l - GATE0)
            for n in range(8, TR + 3):
                attention(n)

            pe.wait_ge(olo_ready, TR)
            for l in range(2):
                feature_block(Pos(FIRST["attnproj"] + l, l), 4, lambda m: half(2 * l + m // 2, m % 2), 2048, T1)
            pe.wait_ge(ylo_ready, 4)
            pe.wait_ge(mod_ready, 1)
            for l in range(4):
                if l == 2:
                    pe.wait_ge(evac["glu"], 2)
                feature_block(Pos(FIRST["glu"] + l, l), 4, lambda m: half(4 + 2 * (l % 2) + m // 2, m % 2), 3072, T1)
            pe.wait_ge(evac["attnproj"], 2)
            for l in range(4):
                feature_block(Pos(FIRST["out"] + l, l), KD, lambda m: half(l, m), 0, T1,
                              (lambda c: pe.wait_ge(mixlo_ready, c // 2 + 1)) if l == 0 else None)
            sums(pe, 1)

            def pe_ffn(p):
                if p.least >= 4:
                    pe.wait_ge(evac["ffn"], 2 * p.h - 2)
                feature_block(p, KD, lambda m: half(p.k, m), 0, T1,
                              (lambda c: wait_norm(pe, 1, c)) if p.least == 0 else None)

            each_block(pe, "ffn", pe_ffn)
            pe.wait_ge(evac["ffn"], 22)
            for l in range(11):
                pe.wait_ge(hlo_ready, l + 1)
                row_block(Pos(FIRST["down"] + l, l), 0, 2048, T1, l == 10)
            pe.wait_ge(plo_ready, 1)
            for l in range(5):
                p = Pos(FIRST["ple"] + l, l)
                if l == 0:
                    feature_block(p, 2, lambda m: half(4 + m // 2, m % 2), 3584, T1)
                else:
                    feature_block(p, KD, lambda m: half(l - 1, m), 0, T1,
                                  (lambda c: pe.wait_ge(xlo_ready, c // 2 + 1)) if l == 1 else None)
            pe.wait_ge(plep_ready, 1)
            sums(pe, 2)
            pe.wait_ge(std_ready, 3)
            sums(pe, 3)

            for l in range(8):
                p = Pos(FIRST["pw1"] + l, l)
                if l >= 4:
                    pe.wait_ge(u_ready, 2 * ((l - 4) // 2 + 1))
                feature_block(p, KD, lambda m: pb[2 * p.k + m][:, :], 0, 512,
                              (lambda c: wait_norm(pe, 3, c)) if l == 0 else None)
            pieces = list(range(HALVES))

            def mod_pieces(most):
                while pieces and most > 0:
                    t = pieces.pop(0)
                    most -= 1
                    mod_piece(1, t)
                    if t % KD == 5 and KD < t < 5 * KD:
                        mod_turn(1, t // KD - 1)

            mod_pieces(PRE)
            pe.wait_ge(u_ready, KD)
            for i in range(len(CONV_PE) * TAPS):
                n, j = divmod(i, TAPS)
                pe.wait_ge(diag_ready, i + 1)
                pe.matmul(pb[n][:, :], diag[:, i % 8, :], upad[:, CONV_PE[n], :, j:j + T1],
                          start=(j == 0), stop=(j == TAPS - 1)).then_inc(tap_done, 1)
                if i % EV == EV - 1:
                    mod_pieces(1)
            mod_pieces(LNP)
            for i, c in enumerate(CONV_ORDER):
                if c in CONV_DVE:
                    pe.wait_ge(conv_dve, CONV_DVE.index(c) + 1)
                elif c in CONV_POOL:
                    pe.wait_ge(cp_used, 30 * (CONV_POOL.index(c) + 1))
                else:
                    pe.wait_ge(conv_out, CONV_PE.index(c) + 1)
                mm = pe.matmul(pb[6][:, :], C["ones"], cacc[:, c, :, :], start=(i == 0), stop=(i == KD - 1))
            mm.then_inc(msum_done, 1)
            for u in range(KD):
                pe.wait_ge(vsq_ready, u + 1)
                pe.matmul(pb[6][:, :], C["ones"], csq[:, u % 4, :], start=(u == 0), stop=(u == KD - 1))\
                  .then_inc(vsum_done, 1)
                mod_pieces(1)
            mod_pieces(HALVES)
            for l in range(4):
                p = Pos(FIRST["pw2"] + l, l)
                if l == 1:
                    mod_turn(1, 4)
                    mod_turn(1, 5)
                if l == 3:
                    pe.wait_ge(mod_ready, 2)
                feature_block(p, KD, lambda m: pb[2 * p.k + m][:, :], 0, 512,
                              (lambda c: pe.wait_ge(lnlo_ready, c + 1)) if l == 0 else None)
            pe.wait_ge(evac["pw2"], 8)
            sums(pe, 4)

            def pe_ff1(p, one, r):
                if p.least >= 4:
                    pe.wait_ge(relu_ready, 32 + p.l - 3 if one else 2 * p.l - 6)
                feature_block(p, KD, (lambda m: half(p.k, m)) if one else (lambda m: pb[2 * p.k + m][:, :]), 0,
                              T1 if one else 512, (lambda c: wait_norm(pe, r, c)) if p.least == 0 else None)

            each_block(pe, "ff1a", lambda p: pe_ff1(p, False, 4))
            pe.wait_ge(relu_ready, 32)

            def pe_ff2(p, name, n, at, t):
                pe.wait_ge(hlo_ready, n + 1 + p.l)
                row_block(p, 0, at, t, p.least == COUNT[name] - 1)

            each_block(pe, "ff2a", lambda p: pe_ff2(p, "ff2a", 11, 0, 512))
            pe.wait_ge(evac["ff2a"], 8)
            sums(pe, 5)

            for l in range(6):
                p = Pos(FIRST["qkv"] + l, l)
                if l == 0:
                    feature_block(p, KD, lambda m: pb[m][:, :], 0, 512, lambda c: wait_norm(pe, 5, c))
                elif l == 1:
                    token_block(p, 512, 4)
                else:
                    pe.wait_ge(wlo_ready, p.b + 1)
                    (wh, wl), _ = tiles(p, KD)
                    for m in range(2):
                        for c in range(KD):
                            mm = three(half(2 + l, m), wh[:, c, P * m:P * m + P], wl[:, c, P * m:P * m + P],
                                       ahi[:, 512 * c:512 * c + 256], alo[:, 512 * c:512 * c + 256],
                                       c == 0, c == KD - 1)
                    mm.then_inc(block_done, 1)
            for n in range(6):
                pe.wait_ge(gq_sq, n + 1)
                if n >= 4:
                    pe.wait_ge(gq_std, n - 3)
                pe.matmul(pb[n % 4][:, :], C["halves"], gsq[:, 512 * n:512 * n + 512], start=True, stop=True)\
                  .then_inc(gq_ms, 1)
            pe.wait_ge(gq_std, 6)
            for n in range(6):
                pe.wait_ge(gq_n, n + 1)
                if n >= 4:
                    pe.wait_ge(gq_ready, n - 3)
                w = 512 if n < 4 else 256
                pe.matmul(pb[n % 4][:, 0:w], C["rotg"], area(512 * n, w), start=True, stop=True)\
                  .then_inc(gq_rot, 1)

            def gscores(h):
                kh, g = h // 4, h % 4
                l0, c = 64 * (kh % 2), 4 * (kh // 2) + g
                if h == 0:
                    pe.wait_ge(gq_ready, 6)
                if h >= 2:
                    pe.wait_ge(exp_done, TR + 2 * (h - 1))
                for qt in range(2):
                    mm = pe.matmul(pb[2 * (h % 2) + qt][:, :], qg[l0:l0 + 64, c, P * qt:P * qt + P],
                                   kg[l0:l0 + 64, kh // 2, :], start=True, stop=True)
                mm.then_inc(s_done, 1)

            def gturn(h):
                pe.wait_ge(pn_ready, TR + h + 1)
                if h >= 1:
                    pe.wait_ge(pt_ready, TR + h)
                for qt in range(2):
                    for kt in range(4):
                        x0 = 256 * (kt % 2) + P * qt
                        mm = pe.transpose(pb[4 + kt // 2][:, x0:x0 + P], pg[:, h % 2, qt, P * kt:P * kt + P],
                                          C["ident"])
                mm.then_inc(pt_done, 1)

            def gweigh(h):
                kh = h // 4
                l0 = 64 * (kh % 2)
                pe.wait_ge(pt_ready, TR + h + 1)
                if h >= 2:
                    pe.wait_ge(olo_ready, TR + h - 1)
                for kt in range(4):
                    mm = pe.matmul(pb[6 + h % 2][l0:l0 + 64, 0:256], vg[:, kt, 64 * kh:64 * kh + 64],
                                   ptg[:, h % 2, 256 * kt:256 * kt + 256], start=(kt == 0), stop=(kt == 3))
                mm.then_inc(o_done, 1)

            for h in range(16 + 3):
                if h < 16:
                    gscores(h)
                if 0 <= h - 2 < 16:
                    gturn(h - 2)
                if h >= 3:
                    gweigh(h - 3)
            pe.wait_ge(olo_ready, TR + 16)
            for l in range(4):
                feature_block(Pos(FIRST["wo"] + l, l), KD, lambda m: half(l, m), 0, T1)
            sums(pe, 6)
            each_block(pe, "ff1b", lambda p: pe_ff1(p, True, 6))
            pe.wait_ge(relu_ready, 48)
            each_block(pe, "ff2b", lambda p: pe_ff2(p, "ff2b", 27, 2048, 256))


def chunked(v, n=KD):
    return np.asarray(v).reshape(n, P).T


def constants():
    f = np.float32
    rot = np.zeros((P, P), f)
    for m in range(P):
        rot[m + 16 if m % 32 < 16 else m - 16, m] = -1 if m % 32 < 16 else 1
    halves = np.zeros((P, P), f)
    halves[:64, :64] = halves[64:, 64:] = 1
    invf = np.zeros((P, 1), f)
    invf[:32, 0] = np.tile(f(500000.0) ** (-np.arange(16, dtype=f) * f(2.0) / f(32)), 2)
    t = np.arange(T1)
    inv = f(10000.0) ** (-np.arange(16, dtype=f) / f(16))
    row, col = (t // 64).astype(f)[:, None] * inv, (t % 64).astype(f)[:, None] * inv
    ang = np.concatenate([row, row, col, col] * 2, axis=1).T
    gtab = np.stack([np.cos(ang), np.sin(ang)], axis=1).astype(f)
    q, k = np.arange(P)[:, None], np.arange(P)[None, :]
    masks = []
    for qt, kt in ((0, 0), (1, 0), (1, 1)):
        for r in (1, 4, 16):
            d = q + P * qt - k - P * kt
            ok = (d >= 0) & (d % r == 0) & (d // r <= 128)
            masks.append(np.where(ok, 0.0, NSCORE).astype(f))
    return dict(ident=np.eye(P, dtype=f), ones=np.ones((P, P), f), halves=halves, rotg=rot, invf=invf), \
        gtab, np.concatenate(masks, axis=1)


def kernel(**a):
    import concourse.bacc as bacc
    from concourse.bass_utils import run_bass_kernel_spmd as run

    a = {k: np.asarray(v) for k, v in a.items()}
    f = np.float32
    own, gtab, masks = constants()

    def states(v):
        return v.reshape(NTILE, P).T

    def both(v):
        return np.concatenate([chunked(v[0]), chunked(v[1])], axis=1)

    parts = dict(own)
    parts.update(
        gmix=chunked(a["g_mix"][0]), gffn=chunked(a["g_ffn"][0]), gfinal=chunked(a["g_final"]),
        convb=chunked(a["conv_b_dw_2"][0]), lng=chunked(a["conv_ln_g_2"][0]), lnb=chunked(a["conv_ln_b_2"][0]),
        g1=both(a["norm1_g_2"]), g2=both(a["norm2_g_2"]),
        bmod=np.concatenate([chunked(a["b_mod_2"][i], MODS) for i in range(2)], axis=1),
        qn=np.tile(a["gqa_q_norm_2"][0], 2)[:, None], kn=np.tile(a["gqa_k_norm_2"][0], 2)[:, None],
        dskip=chunked(a["d_skip"][0].reshape(-1), 4), lr=states(a["a_re"][0]), li=states(a["a_im"][0]),
        ldt=states(np.repeat(a["log_dt"][0][:, None], 64, axis=1)),
        cc=np.stack([chunked(a["c_2"][0]), chunked(a["c_ctx_2"])], axis=2).reshape(P, 16))
    consts = np.concatenate([parts[name] for name, _ in CONSTS], axis=1)

    def tokens(x):
        t, d = x.shape
        return np.ascontiguousarray(x.T.reshape(d // P, P, t).transpose(1, 0, 2))

    bl = np.zeros((4, 4, 2, 16, 2, 2, 64), f)
    ct = np.zeros((2, 64, 2, NTILE, 2, 16), f)
    for part, (b, c) in enumerate(((a["b_re"], a["c_re"]), (a["b_im"], a["c_im"]))):
        b4 = b[0].reshape(4, 4, 2, 64, 16)
        c4 = c[0].reshape(NTILE, 2, 16, 64)
        for g in range(2):
            bl[:, :, g, :, part, g, :] = b4[:, :, g].transpose(1, 0, 3, 2)
            ct[g, :, part, :, g, :] = c4[:, g].transpose(2, 0, 1)
    bl = np.ascontiguousarray(bl.transpose(0, 2, 3, 1, 4, 5, 6)).reshape(P, 1024)
    ct = ct.reshape(P, 1024)

    wq = a["gqa_w_qkv_2"][0]
    wqkv = np.concatenate([wq[:, :D].reshape(D, 2, 2, 4, 64).transpose(0, 1, 3, 2, 4).reshape(D, D), wq[:, D:]], axis=1)
    wo = a["gqa_w_o_2"][0].reshape(2, 2, 4, 64, D).transpose(0, 2, 1, 3, 4).reshape(D, D)

    arrays = dict(
        x=tokens(a["x"][0]), ctx=tokens(a["ctx_2"][0]), p=tokens(a["p"][0, 0]).reshape(P, 512), consts=consts,
        bl=bl, ct=ct, pos=np.broadcast_to(a["positions"], (32, T1)), gtab=gtab, masks=masks,
        w_dw=a["conv_w_dw_2"][0].T.reshape(KD, P, 31).transpose(1, 0, 2),
        w_in=a["w_in"][0], w_attn_proj=a["w_attn_proj"][0], w_glu_a=a["w_glu_a"][0], w_glu_b=a["w_glu_b"][0],
        w_out=a["w_out"][0], w_ffn_gate=a["w_ffn_gate"][0], w_ffn_up=a["w_ffn_up"][0],
        w_ffn_down=a["w_ffn_down"][0], w_ple_gate=a["w_ple_gate"][0], w_ple_proj=a["w_ple_proj"][0],
        pw1=a["conv_w_pw1_2"][0], pw2=a["conv_w_pw2_2"][0], w_qkv=wqkv, w_o=wo,
        w_mod=a["w_mod_2"], w_ff1=a["w_ff1_2"], w_ff2=a["w_ff2_2"])
    nc = bacc.Bacc("TRN2", target_bir_lowering=False, num_devices=1)
    aps, sent = {}, {}
    for name, v in arrays.items():
        v = np.ascontiguousarray(v)
        sent[f"in_{name}"] = v
        aps[name] = nc.dram_tensor(f"in_{name}", v.shape, mybir.dt.from_np(v.dtype), kind="ExternalInput").ap()
    out = nc.dram_tensor("out_t", (P, KD, T1), F32, kind="ExternalOutput").ap()
    program(nc, aps, out)
    r = run(nc, [sent], core_ids=[0])
    got = r.results[0]["out_t"]
    return np.ascontiguousarray(got.transpose(2, 1, 0)).reshape(1, T1, D)
```

```python
from contextlib import ExitStack

import numpy as np

import concourse.bass as bass
from concourse import mybir

ALU = mybir.AluOpType
ACT = mybir.ActivationFunctionType
F32 = mybir.dt.float32
F32R = mybir.dt.float32r
I32 = mybir.dt.int32
AX_X = mybir.AxisListType.X

P = 128
TR = 8
D = 1024
KD = D // P
T1 = 256
HD = 128
NHG = 4
NG = 3
QKW = NHG * NG * HD
SSMW = 512
NTILE = 16
DFF = 2816
DFF2 = 4096
EPS = 1e-6
NSCORE = -1e30
BLK = 2048
RAW = 4
TWO_PI = 2.0 * np.pi
C1 = 6.28125
C2 = float(np.float32(TWO_PI - C1))
C3 = float(np.float32(TWO_PI - C1 - np.float64(np.float32(TWO_PI - C1))))
MAGIC = 12582912.0
L2E = float(np.float32(1.0 / np.log(2.0)))
LN2A = 0.693359375
LN2B = float(np.float32(np.log(2.0) - 0.693359375))
PI_LO = 3.1415925

PHASES = [("in", 28), ("attnproj", 2), ("glu", 4), ("out", 4), ("ffn", 22), ("down", 11), ("ple", 5),
          ("pw1", 8), ("pw2", 4), ("ff1a", 16), ("ff2a", 16), ("qkv", 6), ("wo", 4), ("ff1b", 16), ("ff2b", 16)]
FIRST = {}
_b = 0
for _name, _n in PHASES:
    FIRST[_name] = _b
    _b += _n
NBLOCKS = _b
COUNT = dict(PHASES)
U0, Q0, K0, V0, GATE0 = 0, 2, 8, 14, 20
MODS = 48
HALVES = 48


class Pos:

    def __init__(self, b, l, i=0):
        self.b, self.l, self.q, self.k, self.h = b + 4 * i, l + 4 * i, b // 4 + i, b % 4, l // 2 + 2 * i
        self.least = l


def each_block(eng, phase, body, roll=True):
    b0, n = FIRST[phase], COUNT[phase]
    l = 0
    while l < n:
        if roll and l >= 4 and (b0 + l) % 4 == 0 and n - l >= 8:
            quads = (n - l - 1) // 4
            with eng.Fori(0, quads) as i:
                for k in range(4):
                    body(Pos(b0 + l + k, l + k, i))
            l += 4 * quads
        else:
            body(Pos(b0 + l, l))
            l += 1


CONV_DVE = [(0, 0, 2), (2, 0, 2), (4, 0, 2), (5, 0, 2), (6, 0, 1)]
CONV_POOL = [(1, 0, 2), (3, 0, 2), (6, 1, 1)]
CONV_PE = [7]
TAPS = 31
CONV_ORDER = [0, 2, 1, 4, 3, 7, 5, 6]
MOD_BEFORE = 12
MOD_EVERY = 4
MOD_AFTER = 13

CONSTS = [("ident", 128), ("ones", 128), ("halves", 128), ("rotg", 128), ("invf", 1),
          ("gmix", 8), ("gffn", 8), ("gfinal", 8), ("convb", 8), ("lng", 8), ("lnb", 8), ("g1", 16), ("g2", 16),
          ("bmod", 96), ("qn", 1), ("kn", 1), ("dskip", 4), ("lr", 16), ("li", 16), ("ldt", 16), ("cc", 16)]
CW = sum(w for _, w in CONSTS)


def program(nc, I, out):
    ctx = ExitStack()
    with ctx:
        def sb(name, shape, dt=F32):
            return ctx.enter_context(nc.sbuf_tensor(name, shape, dt))

        def sem(name):
            return ctx.enter_context(nc.semaphore(name))

        raw = sb("raw", [P, RAW, BLK])
        whi = sb("whi", [P, 2, BLK], F32R)
        wlo = sb("wlo", [P, 2, BLK], F32R)
        ahi = sb("ahi", [P, 4096], F32R)
        alo = sb("alo", [P, 4096], F32R)
        X = sb("X", [P, 2, KD, T1])
        cst = sb("cst", [P, CW])
        C = {}
        at = 0
        for name, w in CONSTS:
            C[name] = cst[:, at:at + w]
            at += w
        rope = sb("rope", [P, 2, T1])
        rstd = sb("rstd", [P, 512])
        sp = sb("sp", [P, 24, 16])
        mods = sb("mods", [P, 2, MODS, 2])
        amul = sb("amul", [P, 8, 2])
        scc = sb("scc", [P, 46])
        stat = sb("stat", [P, 64])
        A = sb("A", [P, 22016])

        def area(start, n):
            return A[:, start:start + n]

        o = 0
        q_s = area(o, 3072).rearrange("p (h t) -> p h t", h=12); o += 3072
        k_s = area(o, 3072).rearrange("p (h t) -> p h t", h=12); o += 3072
        v_s = area(o, 3072).rearrange("p (a w) -> p a w", a=2); o += 3072
        u_s = area(o, 1024).rearrange("p (c t) -> p c t", c=4); o += 1024
        GATES = o
        tab = area(o, 2048).rearrange("p (r s j t) -> p r s j t", r=2, s=2, j=2); o += 2048
        tta = area(o, 512); o += 512
        ttb = area(o, 512); o += 512
        h_s = area(o, 1024).rearrange("p (r s t) -> p r s t", r=2, s=2); o += 1024
        gates = area(GATES, 4096).rearrange("p (c t) -> p c t", c=16)
        WORK = o
        p1 = area(o, 512).rearrange("p (s t) -> p s t", s=2); o += 512
        p2 = area(o, 512).rearrange("p (s t) -> p s t", s=2); o += 512
        w_s = area(o, 512).rearrange("p (s t) -> p s t", s=2); o += 512
        g_s = area(o, 1024).rearrange("p (r s t) -> p r s t", r=2, s=2); o += 1024
        q1 = area(o, 512).rearrange("p (s t) -> p s t", s=2); o += 512
        q2 = area(o, 512).rearrange("p (s t) -> p s t", s=2); o += 512
        sm = area(WORK, 768)
        pr = area(WORK + 768, 1536).rearrange("p (r w) -> p r w", r=2)
        pt = area(WORK + 2304, 768)
        bl = area(o, 1024).rearrange("p (c s w) -> p c s w", c=4, s=2); o += 1024
        ct = area(o, 1024).rearrange("p (s j w) -> p s j w", s=2, j=NTILE); o += 1024
        MODRAW = o
        modraw = area(o, 2048).rearrange("p (r w) -> p r w", r=2); o += 2048
        assert o <= 22016, o
        crw = area(6144, 1024).rearrange("p (s j w) -> p s j w", s=2, j=NTILE)
        ctt = area(7168, 1024).rearrange("p (s j w) -> p s j w", s=2, j=NTILE)
        posw = area(8192, 1024)[0:32, :].rearrange("p (r w) -> p r w", r=4)
        msk = X[:, 1, :, :].rearrange("p c t -> p (c t)")
        mask0 = msk[:, 0:384]
        mask1 = msk[:, 384:1152]
        rotb = msk[0:32, 1152:1664].rearrange("p (a t) -> p a t", a=2)
        powers = msk[:, 1664:1920].rearrange("p (n s j) -> p n s j", n=8, s=2)
        mix = area(0, 2048)
        glus = area(2048, 1024)
        glut = area(3072, 1024)
        hid1 = area(0, DFF // P * T1)
        sg1 = area(6144, 1024).rearrange("p (r w) -> p r w", r=2)
        tg1 = area(7168, 1024).rearrange("p (r w) -> p r w", r=2)
        pin = area(8192, 512)
        plep = area(6144, 2048)
        hid = area(0, 32 * 512)
        rl = area(16384, 1024).rearrange("p (r w) -> p r w", r=2)
        UPW = T1 + 30
        upad = area(0, 16 * UPW).rearrange("p (c s t) -> p c s t", c=KD, s=2)
        cacc = area(16 * UPW, 4096).rearrange("p (c s t) -> p c s t", c=KD, s=2)
        SB2 = 16 * UPW + 4096
        wdw = area(SB2, KD * 31).rearrange("p (c j) -> p c j", c=KD)
        sgc = area(SB2 + 248, 1024).rearrange("p (r w) -> p r w", r=2)
        ctp = area(SB2 + 248 + 1024, 1024).rearrange("p (r w) -> p r w", r=2)
        mean_s = area(SB2 + 2296, 512)
        csq = area(SB2 + 2808, 2048).rearrange("p (r w) -> p r w", r=4)
        modrow = [t.rearrange("p (r w) -> p r w", r=2) for t in (rstd[:, :], area(SB2 + 4856, 512))]
        diag = area(14336, 1024).rearrange("p (r w) -> p r w", r=8)
        assert SB2 + 4856 + 512 <= 14336
        modraw1 = area(15872, 6144).rearrange("p (r w) -> p r w", r=6)
        qg = area(0, 2048).rearrange("p (c t) -> p c t", c=8)
        kg = area(2048, 1024).rearrange("p (c t) -> p c t", c=2)
        vg = area(3072, 1024).rearrange("p (a w) -> p a w", a=4)
        gtab = area(17408, 512).rearrange("p (s t) -> p s t", s=2)
        gt1 = area(4608, 1024).rearrange("p (r w) -> p r w", r=2)
        gt2 = area(5632, 1024).rearrange("p (r w) -> p r w", r=2)
        gsq = area(6656, 3072)
        pg = area(9728, 2048).rearrange("p (r a w) -> p r a w", r=2, a=2)
        ptg = area(11776, 2048).rearrange("p (r w) -> p r w", r=2)
        pb = [ctx.enter_context(nc.psum_tensor(f"bank{n}", [P, 512], F32)) for n in range(8)]

        landed = [sem(f"raw_landed{n}") for n in range(RAW)]
        whi_ready = sem("whi_ready")
        wlo_ready = sem("wlo_ready")
        block_done = sem("block_done")
        bank_done = sem("bank_done")
        chunks_free = sem("chunks_free")
        modraw_landed = [sem(f"modraw_landed{n}") for n in range(2)]
        modraw1_landed = [sem(f"modraw1_landed{n}") for n in range(6)]
        modraw_used = sem("modraw_used")
        modrow_ready = sem("modrow_ready")
        mod_turned = sem("mod_turned")
        mod_ready = sem("mod_ready")
        x_landed = sem("x_landed")
        cst_landed = sem("cst_landed")
        ssm_landed = sem("ssm_landed")
        mask_landed = sem("mask_landed")
        pos_landed = sem("pos_landed")
        ctx_landed = sem("ctx_landed")
        p_landed = sem("p_landed")
        dw_landed = sem("dw_landed")
        gtab_landed = sem("gtab_landed")
        out_stored = sem("out_stored")
        ctx_squares = sem("ctx_squares")
        ctx_summed = sem("ctx_summed")
        ctx_std = sem("ctx_std")
        sq_ready = sem("sq_ready")
        sq_used = sem("sq_used")
        std_ready = sem("std_ready")
        rstd_ready = sem("rstd_ready")
        n_ready = sem("n_ready")
        nhi_ready = sem("nhi_ready")
        nlo_ready = sem("nlo_ready")
        evac = {name: sem("evac_" + name) for name, _ in PHASES}
        dch = sem("dve_chain")
        pch = sem("pool_chain")
        ach = sem("act_chain")
        scc_ready = sem("scc_ready")
        silu_ready = sem("silu_ready")
        sin_in = sem("sin_in")
        sin_out = sem("sin_out")
        rtab_ready = sem("rtab_ready")
        tab_ready = sem("tab_ready")
        ct_ready = sem("ct_ready")
        bu_done = sem("bu_done")
        bu_used = sem("bu_used")
        g_ready = sem("g_ready")
        h_ready = sem("h_ready")
        y_done = sem("y_done")
        ysum_ready = sem("ysum_ready")
        gelu_ready = sem("gelu_ready")
        yhi_ready = sem("yhi_ready")
        ylo_ready = sem("ylo_ready")
        rot_done = sem("rot_done")
        roped = sem("roped")
        s_done = sem("scores_done")
        s_used = sem("scores_used")
        nmax_ready = sem("nmax_ready")
        exp_done = sem("exp_done")
        pn_ready = sem("probs_ready")
        pt_done = sem("probs_transposed")
        pt_ready = sem("pt_ready")
        o_done = sem("o_done")
        ohi_ready = sem("ohi_ready")
        olo_ready = sem("olo_ready")
        gsig_ready = sem("gsig_ready")
        gate_ready = sem("gate_ready")
        mix_ready = sem("mix_ready")
        mixhi_ready = sem("mixhi_ready")
        mixlo_ready = sem("mixlo_ready")
        sig_ready = sem("sig_ready")
        th_ready = sem("th_ready")
        hhi_ready = sem("hidden_hi_ready")
        hlo_ready = sem("hidden_lo_ready")
        x_ready = sem("x_ready")
        phi_ready = sem("p_hi_ready")
        plo_ready = sem("p_lo_ready")
        xhi_ready = sem("x_hi_ready")
        xlo_ready = sem("x_lo_ready")
        plep_ready = sem("plep_ready")
        am_ready = sem("amul_ready")
        pad_ready = sem("pad_ready")
        u_ready = sem("conv_in_ready")
        cp_ready = sem("conv_product_ready")
        cp_used = sem("conv_product_used")
        conv_pool = sem("conv_pool")
        conv_dve = sem("conv_dve")
        diag_ready = sem("diag_ready")
        tap_done = sem("tap_done")
        conv_out = sem("conv_out")
        msum_done = sem("mean_done")
        mean_ready = sem("mean_ready")
        cen_ready = sem("centred_ready")
        vsq_ready = sem("var_sq_ready")
        vsum_done = sem("var_sum_done")
        lstd_ready = sem("ln_std_ready")
        lnx_ready = sem("ln_scaled_ready")
        lns_ready = sem("ln_silu_ready")
        lny_ready = sem("ln_silu_product_ready")
        lnhi_ready = sem("ln_hi_ready")
        lnlo_ready = sem("ln_lo_ready")
        relu_ready = sem("relu_ready")
        hid_sq = sem("hidden_ready")
        conv_init = sem("conv_init")
        gq_sq = sem("gq_squares")
        gq_ms = sem("gq_sums")
        gq_std = sem("gq_std")
        gq_n = sem("gq_normed")
        gq_rot = sem("gq_rotated")
        gq_ready = sem("gq_ready")

        block = ctx.enter_context(nc.Block())

        def cols(w, lo, n, kn=KD):
            return w.rearrange("(c p) m -> p c m", p=P)[:, 0:kn, bass.ds(lo, n)]

        def rows(w, k0):
            return w.rearrange("(c p) m -> p c m", p=P)[:, bass.ds(k0, 2), :]

        def in_col(l):
            if l < Q0:
                return 3 * QKW + 256 * l
            if l < GATE0:
                return 256 * (l - Q0)
            return 3 * QKW + SSMW + 256 * (l - GATE0)

        def source(phase, p):
            l, odd = p.l, p.least % 2
            if phase == "in":
                return cols(I["w_in"], in_col(l), 256)
            if phase == "attnproj":
                return cols(I["w_attn_proj"], 512 * l, 512, 4)
            if phase == "glu":
                return cols(I["w_glu_b" if odd else "w_glu_a"], 512 * p.h, 512, 4)
            if phase == "out":
                return cols(I["w_out"], 256 * l, 256)
            if phase == "ffn":
                return cols(I["w_ffn_up" if odd else "w_ffn_gate"], 256 * p.h, 256)
            if phase == "down":
                return rows(I["w_ffn_down"], 2 * l)
            if phase == "ple":
                return rows(I["w_ple_proj"], 0) if p.least == 0 else cols(I["w_ple_gate"], 256 * (l - 1), 256)
            if phase == "pw1":
                return cols(I["pw1"], (D if odd else 0) + 256 * p.h, 256)
            if phase == "pw2":
                return cols(I["pw2"], 256 * l, 256)
            if phase in ("ff1a", "ff1b"):
                return cols(I["w_ff1"][int(phase == "ff1b")], 256 * l, 256)
            if phase in ("ff2a", "ff2b"):
                return rows(I["w_ff2"][int(phase == "ff2b")], 2 * l)
            if phase == "qkv":
                return cols(I["w_qkv"], D + 256 * l if p.least < 2 else 256 * (l - 2), 256)
            return cols(I["w_o"], 256 * l, 256)

        @block.sync
        def _(sync):
            def load(phase, p):
                if p.least >= 4 or FIRST[phase] >= 4:
                    sync.wait_ge(wlo_ready, p.b - 3)
                src = source(phase, p)
                dst = raw[:, p.k, :].rearrange("p (c m) -> p c m", c=src.shape[1])
                sync.dma_start(dst, src).then_inc(landed[p.k], 16)

            def load_mod(layer, t):
                ring_, landed_ = (modraw1, modraw1_landed) if layer else (modraw, modraw_landed)
                n = len(landed_)
                if t >= n:
                    sync.wait_ge(modraw_used, layer * HALVES + t - n + 1)
                m, c = divmod(t, KD)
                sync.dma_start(ring_[:, t % n, :], I["w_mod"][layer][P * c:P * c + P, D * m:D * m + D])\
                    .then_inc(landed_[t % n], 16)

            sync.dma_start(X[:, 0, :, :], I["x"]).then_inc(x_landed, 16)
            for name, _ in PHASES:
                if name == "in":
                    for l in range(28):
                        load(name, Pos(l, l))
                        if l == 1:
                            sync.dma_start(crw, I["ct"]).then_inc(ssm_landed, 16)
                            sync.dma_start(bl, I["bl"]).then_inc(ssm_landed, 16)
                        if 4 <= l:
                            load_mod(0, 2 * (l - 4))
                            load_mod(0, 2 * (l - 4) + 1)
                        if l == 4:
                            sync.dma_start(msk[:, 0:1152], I["masks"]).then_inc(mask_landed, 16)
                    continue
                if name == "out":
                    sync.wait_ge(s_used, TR)
                    sync.wait_ge(roped, 12)
                    sync.wait_ge(y_done, NTILE)
                    sync.dma_start(X[:, 1, :, :], I["ctx"]).then_inc(ctx_landed, 16)
                    sync.wait_ge(o_done, TR)
                    sync.dma_start(pin, I["p"]).then_inc(p_landed, 16)
                if name == "pw1":
                    for l in range(8):
                        load(name, Pos(FIRST[name] + l, l))
                        if l == 4:
                            sync.wait_ge(nlo_ready, 16)
                        if l >= 4:
                            load_mod(1, l - 4)
                    load_mod(1, 4)
                    load_mod(1, 5)
                else:
                    each_block(sync, name, lambda p: load(name, p))
                if name == "pw2":
                    for t in range(6, HALVES):
                        load_mod(1, t)
                    sync.wait_ge(modraw_used, 2 * HALVES)
                    sync.dma_start(gtab, I["gtab"]).then_inc(gtab_landed, 16)
            for u in range(4):
                sync.wait_ge(evac["ff2b"], 2 * (u + 1))
                sync.dma_start(out[:, 2 * u:2 * u + 2, :], X[:, 0, 2 * u:2 * u + 2, :]).then_inc(out_stored, 16)
            sync.wait_ge(out_stored, 64)

        NU = [4, 4, 4, 8, 8, 8, 4]
        NBASE = [sum(NU[:r]) for r in range(8)]
        NSQ = [4, 4, 4, 4, 8, 8, 4]
        SQBASE = [sum(NSQ[:r]) for r in range(8)]
        SQ_AT = [0, 8704, 8704, 14336, 0, 0, 0]
        SUM_BANK = [7, 0, 0, 2, 7, 7, 7]
        NB_AT = [4096, 10752, 10752, 16384, 4096, 4096, 4096]

        def unit(t, r, u):
            return t[:, 0, 2 * u:2 * u + 2, :] if NSQ[r] == 4 else t[:, :, u, :]

        def ring(at, u):
            return area(at + 512 * (u % 4), 512).rearrange("p (a t) -> p a t", a=2)

        def flat(at, u):
            return area(at + 512 * (u % 4), 512)

        def squares(act, r, waits):
            act.activation(stat[:, 40 + r:41 + r], epsb, ACT.Sqrt)
            for u in range(NSQ[r]):
                for s, v in waits(u):
                    act.wait_ge(s, v)
                if u >= 4:
                    act.wait_ge(sq_used, SQBASE[r] + u - 3)
                act.activation(ring(SQ_AT[r], u), unit(X, r, u), ACT.Square).then_inc(sq_ready, 1)

        def sum_pair(pe, bank, s, u):
            pe.matmul(bank, C["ones"], s[:, 0:256], start=(u == 0), stop=False)
            return pe.matmul(bank, C["ones"], s[:, 256:512], start=False, stop=(u == 3))

        def sums(pe, r):
            for u in range(NSQ[r]):
                pe.wait_ge(sq_ready, SQBASE[r] + u + 1)
                s = flat(SQ_AT[r], u)
                if NSQ[r] == 4:
                    mm = sum_pair(pe, pb[SUM_BANK[r]][:, 0:256], s, u)
                else:
                    mm = pe.matmul(pb[SUM_BANK[r]][:, :], C["ones"], s, start=(u == 0), stop=(u == 7))
                mm.then_inc(sq_used, 1)

        def std(act, r):
            w = 256 if NSQ[r] == 4 else 512
            act.wait_ge(sq_used, SQBASE[r + 1])
            act.activation(rstd[:, 0:w], pb[SUM_BANK[r]][:, 0:w], ACT.Sqrt, scale=1.0 / D, bias=epsb).then_inc(std_ready, 1)

        def hi_parts(act, r):
            for u in range(NU[r]):
                act.wait_ge(n_ready, NBASE[r] + u + 1)
                act.activation(ahi[:, 512 * u:512 * u + 512], flat(NB_AT[r], u), ACT.Copy).then_inc(nhi_ready, 1)

        def lo_parts(pool, r):
            for u in range(NU[r]):
                pool.wait_ge(nhi_ready, NBASE[r] - 4 * (r > 2) + u + 1)
                pool.tensor_tensor(alo[:, 512 * u:512 * u + 512], flat(NB_AT[r], u),
                                   ahi[:, 512 * u:512 * u + 512].bitcast(F32), ALU.subtract).then_inc(nlo_ready, 1)

        def wait_norm(pe, r, kc=None):
            n = NU[r] if kc is None else (kc // 2 + 1 if NU[r] == 4 else kc + 1)
            pe.wait_ge(nlo_ready, NBASE[r] - 4 * (r > 2) + n)

        epsb = stat[:, 60:61]

        UNITS = [4, 5, 0, 1, 2, 3]
        UNIT_BLOCK = [0, 0, 2, 3, 4, 5]
        MS_BANK = [0, 1, 2, 3, 2, 3]
        ROT_BANK = [0, 1, 0, 5, 4, 7]

        def units_of(l):
            return [e for e in range(6) if UNIT_BLOCK[e] == l]

        @block.scalar
        def _(act):
            chain = [0]

            def link(ins):
                chain[0] += 1
                ins.then_inc(ach, 1)
                act.wait_ge(ach, chain[0])

            def hi(p_b, q, k):
                b, kk, qq = p_b + 2, (k + 2) % 4, q + (k + 2) // 4
                act.wait_ge(landed[kk], qq * 16 + 16)
                act.wait_ge(block_done, p_b + 1)
                act.activation(whi[:, k % 2, :], raw[:, kk, :], ACT.Copy).then_inc(whi_ready, 1)

            def ahead(p):
                if not (p.least + 2 >= COUNT[ph[0]] and ph[0] == PHASES[-1][0]):
                    hi(p.b, p.q, p.k)

            ph = ["in"]

            act.dma_start(cst[:, :], I["consts"]).then_inc(cst_landed, 16)
            act.dma_start(posw[:, 0, :].bitcast(I32), I["pos"]).then_inc(pos_landed, 16)
            for b in range(2):
                if b == 0:
                    act.wait_ge(am_ready, 1)
                    squares(act, 0, lambda u: [(x_landed, 16)])
                act.wait_ge(landed[b], 16)
                act.activation(whi[:, b, :], raw[:, b, :], ACT.Copy).then_inc(whi_ready, 1)
                if b == 0:
                    std(act, 0)
            act.wait_ge(cst_landed, 16)
            act.activation(scc[:, 0:16], C["cc"], ACT.Sigmoid).then_inc(scc_ready, 1)
            hi_parts(act, 0)
            act.wait_ge(sin_in, 1)
            act.activation(sp[:, 8, :], sp[:, 6, :], ACT.Sin).then_inc(sin_out, 1)
            act.activation(sp[:, 9, :], sp[:, 7, :], ACT.Sin).then_inc(sin_out, 1)

            def rotary_sines():
                act.wait_ge(sin_in, 2)
                act.activation(rope[0:32, 1, :], posw[:, 1, :], ACT.Sin).then_inc(sin_out, 1)
                act.activation(rope[0:32, 0, :], posw[:, 2, :], ACT.Sin).then_inc(sin_out, 1)

            def but_last(phase):
                def body(p):
                    if p.least < COUNT[phase] - 1:
                        ahead(p)
                return body

            def last_ahead(phase):
                ahead(Pos(FIRST[phase] + COUNT[phase] - 1, COUNT[phase] - 1))

            def attention_exp(n):
                w = 384 if n % 2 == 0 else 768
                act.wait_ge(nmax_ready, n + 1)
                if n >= 2:
                    act.wait_ge(pt_done, n - 1)
                act.activation(pr[:, n % 2, 0:w], sm[:, 0:w], ACT.Exp, bias=stat[:, n:n + 1],
                               accum_out=stat[:, 8 + n:9 + n]).then_inc(exp_done, 1)

            def attention_pt(n):
                act.wait_ge(pt_done, n + 1)
                if n >= 1:
                    act.wait_ge(o_done, n)
                for kt in range(1 + n % 2):
                    c = act.activation(pt[:, 384 * kt:384 * kt + 384], pb[2 + kt][:, 0:384], ACT.Copy)
                c.then_inc(pt_ready, 1)

            def attention_out(n):
                c0 = 2048 + 256 * (n // 2) + 128 * (n % 2)
                act.wait_ge(o_done, n + 1)
                act.activation(ahi[:, c0:c0 + 128], pb[6][:, 0:128], ACT.Copy).then_inc(ohi_ready, 1)

            def attention_early(n):
                if 0 <= n - 4 < TR:
                    attention_out(n - 4)
                if 0 <= n - 1 < TR:
                    attention_exp(n - 1)

            def attention_late(n):
                if 0 <= n - 2 < TR:
                    attention_pt(n - 2)

            def gelu(c):
                act.wait_ge(ysum_ready, c + 1)
                act.activation(u_s[:, c, :], u_s[:, c, :], ACT.Gelu_apprx_tanh).then_inc(gelu_ready, 1)

            def yhi(c):
                act.wait_ge(gelu_ready, c + 1)
                act.activation(ahi[:, 3072 + 256 * c:3328 + 256 * c], u_s[:, c, :], ACT.Copy).then_inc(yhi_ready, 1)

            def mod_rows(layer, m):
                n = 6 * layer + m
                act.wait_ge(modraw_used, HALVES * layer + KD * (m + 1))
                if m >= 2:
                    act.wait_ge(mod_turned, n - 1)
                bank = pb[2 + m % 2] if layer else pb[7]
                act.activation(modrow[layer][:, m % 2, :], bank[:, 0:256], ACT.Copy).then_inc(modrow_ready, 1)

            for l in range(28):
                p = Pos(l, l)
                if l % 4 == 2 and l > 2:
                    mod_rows(0, (l - 6) // 4)
                attention_early(l - GATE0)
                ahead(p)
                bank = pb[l % 2][:, :].rearrange("p (a t) -> p a t", a=2)
                act.wait_ge(block_done, p.b + 1)
                if l < Q0:
                    act.activation(u_s[:, 2 * l:2 * l + 2, :], bank, ACT.Copy).then_inc(evac["in"], 1)
                    if l == 1:
                        rotary_sines()
                elif l < K0:
                    act.activation(q_s[:, 2 * (l - Q0):2 * (l - Q0) + 2, :], bank, ACT.Copy).then_inc(evac["in"], 1)
                elif l < V0:
                    act.activation(k_s[:, 2 * (l - K0):2 * (l - K0) + 2, :], bank, ACT.Copy).then_inc(evac["in"], 1)
                elif l < GATE0:
                    if l == V0:
                        act.wait_ge(ct_ready, 1)
                    act.activation(v_s[:, :, 256 * (l - V0):256 * (l - V0) + 256], bank, ACT.Copy)\
                       .then_inc(evac["in"], 1)
                else:
                    if l == GATE0:
                        act.wait_ge(y_done, NTILE)
                    act.activation(gates[:, 2 * (l - GATE0):2 * (l - GATE0) + 2, :], bank, ACT.Tanh, scale=0.5)\
                       .then_inc(evac["in"], 1)
                if l == 22:
                    for c in range(4):
                        gelu(c)
                    for c in range(4):
                        yhi(c)
                attention_late(l - GATE0)
            for n in range(8, TR + 4):
                attention_early(n)
                attention_late(n)

            ph[0] = "attnproj"
            each_block(act, "attnproj", ahead)
            ph[0] = "glu"

            def mix_hi(j):
                for n in (2 * j, 2 * j + 1):
                    act.wait_ge(mix_ready, n + 1)
                    act.activation(ahi[:, 512 * n:512 * n + 512], mix[:, 512 * n:512 * n + 512], ACT.Copy)\
                       .then_inc(mixhi_ready, 1)

            for l in range(4):
                p = Pos(FIRST["glu"] + l, l)
                if l % 2:
                    act.wait_ge(block_done, p.b + 1)
                    if l == 3:
                        act.wait_ge(mix_ready, 2)
                    for s in range(2):
                        act.activation(glus[:, 512 * s:512 * s + 512], pb[(6 if l == 1 else 2) + s][:, :],
                                       ACT.Sigmoid).then_inc(gsig_ready, 1)
                if l != 3:
                    ahead(p)
                if l >= 2:
                    mix_hi(l - 2)
            ahead(Pos(FIRST["glu"] + 3, 3))
            ph[0] = "out"
            each_block(act, "out", but_last("out"))
            squares(act, 1, lambda u: [(evac["out"], u + 1)])
            std(act, 1)
            last_ahead("out")
            hi_parts(act, 1)

            ph[0] = "ffn"

            def act_ffn(p):
                ahead(p)
                if p.least % 2 == 0:
                    act.wait_ge(block_done, p.b + 1)
                    if p.least >= 4:
                        act.wait_ge(evac["ffn"], p.l - 2)
                    act.activation(sg1[:, p.least // 2 % 2, :], pb[p.k][:, :], ACT.Sigmoid).then_inc(sig_ready, 1)

            def hidden_hi(l, base, total, w, h, at, l_static):
                if l_static + 2 >= total:
                    return
                s = (l_static + 2) % 4
                if l_static + 2 >= 4:
                    act.wait_ge(block_done, base + l - 1)
                act.activation(ahi[:, at + w * s:at + w * s + w], h[:, bass.ds(w * (l + 2), w)], ACT.Copy)\
                   .then_inc(hhi_ready, 1)

            def act_ffn_last(p):
                if p.least == 20:
                    for l in (-2, -1):
                        act.wait_ge(evac["ffn"], 2 * (l + 3))
                        hidden_hi(l, FIRST["down"], 11, 512, hid1, 2048, l)
                act_ffn(p)

            each_block(act, "ffn", act_ffn_last)
            ph[0] = "down"

            def act_down(p):
                hidden_hi(p.l, FIRST["down"], 11, 512, hid1, 2048, p.least)
                but_last("down")(p)

            act.wait_ge(evac["ffn"], 22)
            each_block(act, "down", act_down, roll=False)
            act.wait_ge(p_landed, 16)
            act.activation(ahi[:, 3584:4096], pin, ACT.Copy).then_inc(phi_ready, 1)
            for u in range(4):
                act.wait_ge(evac["down"], u + 1)
                act.activation(ahi[:, 512 * u:512 * u + 512].rearrange("p (a t) -> p a t", a=2),
                               X[:, 0, 2 * u:2 * u + 2, :], ACT.Copy).then_inc(xhi_ready, 1)
            last_ahead("down")
            ph[0] = "ple"
            for l in range(5):
                p = Pos(FIRST["ple"] + l, l)
                but_last("ple")(p)
                act.wait_ge(block_done, p.b + 1)
                if l == 0:
                    for s in range(4):
                        c = act.activation(plep[:, 512 * s:512 * s + 512], pb[s][:, :], ACT.Copy)
                    c.then_inc(plep_ready, 1)
                else:
                    act.activation(area(8704 + 512 * (l - 1), 512), pb[3 + l][:, :], ACT.Sigmoid).then_inc(sig_ready, 1)
                if l == 1:
                    act.wait_ge(ctx_landed, 16)
                    for u in range(4):
                        act.activation(ring(SQ_AT[3], u), X[:, 1, 2 * u:2 * u + 2, :], ACT.Square)\
                           .then_inc(ctx_squares, 1)
            squares(act, 2, lambda u: [(evac["ple"], u + 1)])
            std(act, 2)
            last_ahead("ple")
            act.wait_ge(ctx_summed, 4)
            act.activation(rstd[:, 256:512], pb[1][:, 256:512], ACT.Sqrt, scale=1.0 / D, bias=epsb)\
               .then_inc(ctx_std, 1)
            squares(act, 3, lambda u: [(n_ready, NBASE[2] + u + 1)])
            std(act, 3)
            act.dma_start(wdw, I["w_dw"]).then_inc(dw_landed, 16)
            hi_parts(act, 3)

            ph[0] = "pw1"
            taps = [(i, j) for i in range(len(CONV_POOL)) for j in range(TAPS)]

            def diagonal(i):
                if i >= 8:
                    act.wait_ge(tap_done, i - 7)
                act.activation(diag[:, i % 8, :], C["ident"], ACT.Copy,
                               scale=wdw[:, CONV_PE[i // TAPS], i % TAPS:i % TAPS + 1]).then_inc(diag_ready, 1)

            def convolved(n):
                c = CONV_PE[n]
                act.wait_ge(tap_done, TAPS * (n + 1))
                act.activation(cacc[:, c, :, :], pb[n][:, :].rearrange("p (s t) -> p s t", s=2), ACT.Identity,
                               bias=C["convb"][:, c:c + 1]).then_inc(conv_out, 1)

            def products(p, most):
                while taps and most > 0 and (p is None or CONV_POOL[taps[0][0]][0] // 2 * 2 + 1 < p.l):
                    i, j = taps.pop(0)
                    c, s, ns = CONV_POOL[i]
                    most -= 1
                    src = upad[:, c, s:s + ns, j:j + T1]
                    if j == 0:
                        act.wait_ge(dw_landed, 16)
                        act.wait_ge(pad_ready, 1)
                        act.wait_ge(u_ready, c + 1)
                        act.activation(cacc[:, c, s:s + ns, :], src, ACT.Identity, bias=C["convb"][:, c:c + 1],
                                       scale=wdw[:, c, 0:1]).then_inc(conv_init, 1)
                        continue
                    n = (TAPS - 1) * i + j - 1
                    if n >= 2:
                        act.wait_ge(cp_used, n - 1)
                    act.activation(ctp[:, n % 2, 0:T1 * ns].rearrange("p (s t) -> p s t", s=ns), src, ACT.Copy,
                                   scale=wdw[:, c, j:j + 1]).then_inc(cp_ready, 1)

            def act_pw1(p):
                ahead(p)
                if p.least % 2:
                    act.wait_ge(block_done, p.b + 1)
                    for m in range(2):
                        n = p.l - 1 + m
                        if n >= 2:
                            act.wait_ge(u_ready, n - 1)
                        act.activation(sgc[:, m, :], pb[2 * p.k + m][:, :], ACT.Sigmoid).then_inc(sig_ready, 1)
                products(p, 7)

            each_block(act, "pw1", act_pw1, roll=False)
            mod_rows(1, 0)
            for i in range(len(CONV_PE) * TAPS):
                diagonal(i)
                products(None, 1)
            products(None, 6)
            convolved(0)
            for m in range(1, 4):
                products(None, 5)
                mod_rows(1, m)
            products(None, 1000)
            for u in range(KD):
                act.wait_ge(cen_ready, u + 1)
                if u >= 4:
                    act.wait_ge(vsum_done, u - 3)
                act.activation(csq[:, u % 4, :], cacc[:, u, :, :].rearrange("p s t -> p (s t)"), ACT.Square)\
                   .then_inc(vsq_ready, 1)
            act.wait_ge(vsum_done, KD)
            act.activation(rstd[:, :], pb[6][:, :], ACT.Sqrt, scale=1.0 / D, bias=epsb).then_inc(lstd_ready, 1)
            for u in range(KD):
                act.wait_ge(lnx_ready, u + 1)
                act.activation(csq[:, u % 4, :], cacc[:, u, :, :].rearrange("p s t -> p (s t)"), ACT.Sigmoid)\
                   .then_inc(lns_ready, 1)
                if u >= 1:
                    v = u - 1
                    act.wait_ge(lny_ready, v + 1)
                    act.activation(ahi[:, 512 * v:512 * v + 512], cacc[:, v, :, :].rearrange("p s t -> p (s t)"),
                                   ACT.Copy).then_inc(lnhi_ready, 1)
            act.wait_ge(lny_ready, KD)
            act.activation(ahi[:, 512 * 7:4096], cacc[:, 7, :, :].rearrange("p s t -> p (s t)"),
                           ACT.Copy).then_inc(lnhi_ready, 1)
            mod_rows(1, 4)
            mod_rows(1, 5)
            ph[0] = "pw2"
            each_block(act, "pw2", but_last("pw2"))

            def relus(p):
                ahead(p)
                act.wait_ge(block_done, p.b + 1)
                one = ph[0] == "ff1b"
                for m in range(1 if one else 2):
                    if one:
                        n, w = p.l, 32 + p.l
                        par, src = (p.least % 2), pb[p.k]
                        first = p.least < 2
                    else:
                        n, w = p.l * 2 + m, p.l * 2 + m
                        par, src = m, pb[2 * p.k + m]
                        first = p.least < 1
                    if not first:
                        act.wait_ge(hid_sq, w - 1)
                    act.activation(rl[:, par, :], src[:, :], ACT.Relu).then_inc(relu_ready, 1)

            squares(act, 4, lambda u: [(evac["pw2"], u + 1)])
            std(act, 4)
            last_ahead("pw2")
            hi_parts(act, 4)

            def up2(name, hbase, w, u_at):
                def body(p):
                    if p.least == COUNT[name] - 1:
                        for l in (-2, -1):
                            if w == 1024:
                                act.wait_ge(chunks_free, l + 3)
                            act.wait_ge(hid_sq, hbase + w // 512 * (l + 3))
                            hidden_hi(l, 0, 16, w, hid, u_at, l)
                    relus(p)

                ph[0] = name
                each_block(act, name, body)

            def down2(name, hbase, w, u_at):
                ph[0] = name
                base = FIRST[name]
                act.wait_ge(hid_sq, hbase + (32 if w == 1024 else 16))

                def body(p):
                    if p.least == 0:
                        act.wait_ge(block_done, base)
                    hidden_hi(p.l, base, 16, w, hid, u_at, p.least)
                    but_last(name)(p)

                each_block(act, name, body, roll=False)

            up2("ff1a", 0, 1024, 0)
            down2("ff2a", 0, 1024, 0)
            squares(act, 5, lambda u: [(evac["ff2a"], u + 1)])
            std(act, 5)
            last_ahead("ff2a")
            hi_parts(act, 5)

            def head_squares(e, l):
                act.wait_ge(evac["qkv"], l + 1)
                n = UNITS[e]
                act.activation(gsq[:, 512 * n:512 * n + 512], area(512 * n, 512), ACT.Square).then_inc(gq_sq, 1)

            def head_std(e):
                n = UNITS[e]
                act.wait_ge(gq_ms, e + 1)
                act.activation(gsq[:, 512 * n:512 * n + 512], pb[MS_BANK[e]][:, :], ACT.Sqrt, scale=1.0 / 64,
                               bias=epsb).then_inc(gq_std, 1)

            ph[0] = "qkv"
            for l in range(7):
                if l == 6:
                    head_std(5)
                    continue
                p = Pos(FIRST["qkv"] + l, l)
                ahead(p)
                act.wait_ge(block_done, p.b + 1)
                if l == 0:
                    for m in range(2):
                        c = act.activation(kg[:, m, :], pb[m][:, :], ACT.Copy)
                elif l == 1:
                    for a in range(2):
                        c = act.activation(vg[:, 2 * a:2 * a + 2, :], pb[2 + a][:, :].rearrange("p (a w) -> p a w", a=2),
                                           ACT.Copy)
                else:
                    c = act.activation(qg[:, 2 * (l - 2):2 * (l - 2) + 2, :],
                                       pb[2 + l][:, :].rearrange("p (a t) -> p a t", a=2), ACT.Copy)
                c.then_inc(evac["qkv"], 1)
                for e in units_of(l - 1):
                    head_std(e)
                for e in units_of(l):
                    head_squares(e, l)

            def gexp(h):
                for qt in range(2):
                    act.wait_ge(nmax_ready, TR + h + 1)
                    if h >= 2 and qt == 0:
                        act.wait_ge(pt_done, TR + h - 1)
                    act.activation(pg[:, h % 2, qt, :], pb[2 * (h % 2) + qt][:, :], ACT.Exp,
                                   bias=stat[:, 16 + 2 * (h % 2) + qt:17 + 2 * (h % 2) + qt], scale=0.125,
                                   accum_out=stat[:, 20 + 2 * (h % 2) + qt:21 + 2 * (h % 2) + qt]).then_inc(exp_done, 1)

            def gpt(h):
                act.wait_ge(pt_done, TR + h + 1)
                if h >= 2:
                    act.wait_ge(o_done, TR + h - 1)
                for s in range(2):
                    c = act.activation(ptg[:, h % 2, 512 * s:512 * s + 512], pb[4 + s][:, :], ACT.Copy)
                c.then_inc(pt_ready, 1)

            def gout(h):
                kh, g = h // 4, h % 4
                lo_, c0 = 64 * (kh % 2), 256 * (4 * (kh // 2) + g)
                act.wait_ge(o_done, TR + h + 1)
                act.activation(ahi[lo_:lo_ + 64, c0:c0 + 256], pb[6 + h % 2][lo_:lo_ + 64, 0:256], ACT.Copy)\
                   .then_inc(ohi_ready, 1)

            for h in range(1, 16 + 4):
                if h - 1 < 16:
                    gexp(h - 1)
                if h >= 4:
                    gout(h - 4)
                if 0 <= h - 2 < 16:
                    gpt(h - 2)
            ph[0] = "wo"
            each_block(act, "wo", but_last("wo"))
            squares(act, 6, lambda u: [(evac["wo"], u + 1)])
            std(act, 6)
            last_ahead("wo")
            hi_parts(act, 6)
            up2("ff1b", 32, 512, 2048)
            down2("ff2b", 32, 512, 2048)

        @block.vector
        def _(dve):
            chain = [0]

            def link(ins):
                chain[0] += 1
                ins.then_inc(dch, 1)
                dve.wait_ge(dch, chain[0])

            def lo(p_b, k):
                dve.wait_ge(whi_ready, p_b + 3)
                dve.tensor_tensor(wlo[:, k % 2, :], raw[:, (k + 2) % 4, :], whi[:, k % 2, :].bitcast(F32),
                                  ALU.subtract).then_inc(wlo_ready, 1)

            ph = ["in"]

            def ahead(p):
                if not (p.least + 2 >= COUNT[ph[0]] and ph[0] == PHASES[-1][0]):
                    lo(p.b, p.k)

            def reduce_angle(a, k, tmp):
                link(dve.tensor_scalar(k, a, 1.0 / TWO_PI, MAGIC, ALU.mult, ALU.add))
                link(dve.tensor_scalar(k, k, -MAGIC, None, ALU.add))
                for c in (C1, C2, C3):
                    link(dve.scalar_tensor_tensor(a, k, -c, a, ALU.mult, ALU.add))
                link(dve.tensor_scalar(a, a, PI_LO, -PI_LO, ALU.min, ALU.max))
                link(dve.tensor_scalar(tmp, a, np.pi / 2, None, ALU.add))
                link(dve.tensor_scalar(k, tmp, np.pi, -TWO_PI, ALU.is_gt, ALU.mult))
                link(dve.tensor_tensor(tmp, tmp, k, ALU.add))
                link(dve.tensor_scalar(tmp, tmp, PI_LO, -PI_LO, ALU.min, ALU.max))

            def exact_exp(dst, a, k, r, bits):
                link(dve.tensor_scalar(a, a, -87.0, 88.0, ALU.max, ALU.min))
                link(dve.tensor_scalar(k, a, L2E, MAGIC, ALU.mult, ALU.add))
                link(dve.tensor_scalar(k, k, -MAGIC, None, ALU.add))
                link(dve.tensor_scalar(k, k, -126.0, 127.0, ALU.max, ALU.min))
                link(dve.scalar_tensor_tensor(r, k, -LN2A, a, ALU.mult, ALU.add))
                link(dve.scalar_tensor_tensor(r, k, -LN2B, r, ALU.mult, ALU.add))
                link(dve.tensor_scalar(k, k, 127.0, 8388608.0, ALU.add, ALU.mult))
                link(dve.tensor_copy(bits.bitcast(I32), k))
                link(dve.tensor_scalar(dst, r, 1.0 / 5040, 1.0 / 720, ALU.mult, ALU.add))
                for c in (1 / 120, 1 / 24, 1 / 6, 0.5, 1.0, 1.0):
                    link(dve.tensor_tensor(dst, dst, r, ALU.mult))
                    link(dve.tensor_scalar(dst, dst, c, None, ALU.add))
                link(dve.tensor_tensor(dst, dst, bits, ALU.mult))

            dve.memset(scc[:, 16:46], 0.0)
            dve.memset(stat[:, 60:61], EPS).then_inc(am_ready, 1)
            dve.wait_ge(cst_landed, 16)
            dt_, mag, th = sp[:, 0, :], sp[:, 1, :], sp[:, 6, :]
            exact_exp(dt_, C["ldt"], sp[:, 2, :], sp[:, 3, :], sp[:, 4, :])
            link(dve.tensor_tensor(th, C["li"], dt_, ALU.mult))
            reduce_angle(th, sp[:, 2, :], sp[:, 7, :])
            dve.tensor_copy(sp[:, 2, :], sp[:, 7, :]).then_inc(sin_in, 1)

            def reciprocal_std(r):
                w = 256 if NSQ[r] == 4 else 512
                dve.wait_ge(std_ready, r + 1)
                link(dve.reciprocal(rstd[:, 0:w], rstd[:, 0:w]))

            def norm_gain(r, g):
                reciprocal_std(r)
                for u in range(4):
                    nb = ring(NB_AT[r], u)
                    for a in range(2):
                        c = 2 * u + a
                        dst = X[:, 0, c, :] if r == 2 else nb[:, a, :]
                        i = dve.scalar_tensor_tensor(dst, X[:, 0, c, :], g[:, c:c + 1], rstd[:, 0:256],
                                                     ALU.mult, ALU.mult)
                    i.then_inc(n_ready, 1)

            dve.wait_ge(x_landed, 16)
            norm_gain(0, C["gmix"])
            for b in range(2):
                dve.wait_ge(whi_ready, b + 1)
                dve.tensor_tensor(wlo[:, b, :], raw[:, b, :], whi[:, b, :].bitcast(F32), ALU.subtract)\
                   .then_inc(wlo_ready, 1)

            dve.wait_ge(scc_ready, 1)
            dve.tensor_tensor(scc[:, 0:16], scc[:, 0:16], C["cc"], ALU.mult).then_inc(silu_ready, 1)

            dve.wait_ge(pos_landed, 16)
            ang, cosa, kk = posw[:, 1, :], posw[:, 2, :], posw[:, 3, :]
            link(dve.tensor_copy(ang, posw[:, 0, :].bitcast(I32)))
            link(dve.tensor_scalar(ang, ang, C["invf"][0:32, :], None, ALU.mult))
            reduce_angle(ang, kk, cosa)
            dve.tensor_copy(kk, cosa).then_inc(sin_in, 1)

            ahead(Pos(0, 0))
            link(dve.tensor_tensor(sp[:, 5, :], C["lr"], dt_, ALU.mult))
            exact_exp(mag, sp[:, 5, :], sp[:, 2, :], sp[:, 3, :], sp[:, 4, :])
            ahead(Pos(1, 1))
            dve.wait_ge(sin_out, 2)
            zr, zi, den, t0, t1 = (sp[:, n, :] for n in (10, 11, 12, 13, 14))
            lr, li = C["lr"], C["li"]
            link(dve.tensor_tensor(t0, mag, sp[:, 9, :], ALU.mult))
            link(dve.tensor_scalar(t0, t0, -1.0, None, ALU.add))
            link(dve.tensor_tensor(t1, mag, sp[:, 8, :], ALU.mult))
            link(dve.tensor_tensor(den, lr, lr, ALU.mult))
            link(dve.tensor_tensor(zr, li, li, ALU.mult))
            link(dve.tensor_tensor(den, den, zr, ALU.add))
            link(dve.reciprocal(den, den))
            link(dve.tensor_tensor(zr, t0, lr, ALU.mult))
            link(dve.tensor_tensor(sp[:, 15, :], t1, li, ALU.mult))
            link(dve.tensor_tensor(zr, zr, sp[:, 15, :], ALU.add))
            link(dve.tensor_tensor(zr, zr, den, ALU.mult))
            link(dve.tensor_tensor(zi, t1, lr, ALU.mult))
            link(dve.tensor_tensor(sp[:, 15, :], t0, li, ALU.mult))
            link(dve.tensor_tensor(zi, zi, sp[:, 15, :], ALU.subtract))
            link(dve.tensor_tensor(zi, zi, den, ALU.mult))
            dve.wait_ge(ssm_landed, 32)
            dve.wait_ge(nlo_ready, 4)

            def zb(z):
                return z.unsqueeze(2).broadcast_to([P, NTILE, 32])

            link(dve.tensor_tensor(ct[:, 0], crw[:, 0], zb(zr), ALU.mult))
            link(dve.tensor_tensor(ctt[:, 0], crw[:, 1], zb(zi), ALU.mult))
            link(dve.tensor_tensor(ct[:, 0], ct[:, 0], ctt[:, 0], ALU.subtract))
            link(dve.tensor_tensor(ct[:, 1], crw[:, 0], zb(zi), ALU.mult))
            link(dve.tensor_tensor(ctt[:, 1], crw[:, 1], zb(zr), ALU.mult))
            link(dve.tensor_tensor(ct[:, 1], ct[:, 1], ctt[:, 1], ALU.add))
            dve.tensor_scalar(ct[:, 1], ct[:, 1], -1.0, None, ALU.mult).then_inc(ct_ready, 1)

            def ssm_in(j):
                s, jj = j // 2 % 2, j % 2
                bu = pb[2 + 2 * (j % 2)][:, :].rearrange("p (s t) -> p s t", s=2)
                cb = tab[:, s, 0, jj, :].unsqueeze(1).broadcast_to([P, 2, T1])
                sbb = tab[:, s, 1, jj, :].unsqueeze(1).broadcast_to([P, 2, T1])
                dve.wait_ge(tab_ready, j // 2 + 1)
                dve.wait_ge(bu_done, j + 1)
                dve.tensor_tensor(p1, bu, cb, ALU.mult)
                dve.tensor_tensor(p2, bu, sbb, ALU.mult).then_inc(bu_used, 1)
                dve.wait_ge(bu_used, j + 1)
                dve.tensor_tensor(w_s[:, 0, :], p1[:, 0, :], p2[:, 1, :], ALU.add)
                link(dve.tensor_tensor(w_s[:, 1, :], p1[:, 1, :], p2[:, 0, :], ALU.subtract))
                if j >= 2:
                    dve.wait_ge(h_ready, j - 1)
                m = mag[:, j:j + 1].broadcast_to([P, T1])
                dve.tensor_tensor_scan(g_s[:, j % 2, 0, :], m, w_s[:, 0, :], 0.0, ALU.mult, ALU.add)
                dve.tensor_tensor_scan(g_s[:, j % 2, 1, :], m, w_s[:, 1, :], 0.0, ALU.mult, ALU.add)\
                   .then_inc(g_ready, 1)

            def ssm_out(c):
                dve.wait_ge(y_done, 4 * c + 4)
                dve.scalar_tensor_tensor(u_s[:, c, :], u_s[:, c, :], C["dskip"][:, c:c + 1],
                                         pb[6][:, 256 * (c % 2):256 * (c % 2) + 256], ALU.mult, ALU.add)\
                   .then_inc(ysum_ready, 1)

            def rotate(n):
                t = q_s if n < 6 else k_s
                m = n % 6
                part = t[0:32, 2 * m:2 * m + 2, :]
                cb = rope[0:32, 0, :].unsqueeze(1).broadcast_to([32, 2, T1])
                sbb = rope[0:32, 1, :].unsqueeze(1).broadcast_to([32, 2, T1])
                if n == 0:
                    dve.wait_ge(sin_out, 4)
                dve.wait_ge(rot_done, n + 1)
                dve.tensor_tensor(rotb, pb[3][0:32, :].rearrange("p (a t) -> p a t", a=2), sbb, ALU.mult)
                link(dve.tensor_tensor(part, part, cb, ALU.mult))
                dve.tensor_tensor(part, part, rotb, ALU.add).then_inc(roped, 1)

            def attention_max(n):
                w = 384 if n % 2 == 0 else 768
                dve.wait_ge(s_done, n + 1)
                if n == 0:
                    dve.wait_ge(mask_landed, 16)
                    dve.wait_ge(y_done, NTILE)
                if n >= 1:
                    dve.wait_ge(exp_done, n)
                for kt in range(1 + n % 2):
                    mk = (mask0 if n % 2 == 0 else mask1)[:, 384 * kt:384 * kt + 384]
                    i = dve.scalar_tensor_tensor(sm[:, 384 * kt:384 * kt + 384], pb[4 + kt][:, 0:384],
                                                 HD ** -0.5, mk, ALU.mult, ALU.add)
                i.then_inc(s_used, 1)
                dve.wait_ge(s_used, n + 1)
                link(dve.reduce_max(stat[:, 24:25], sm[:, 0:w], AX_X))
                dve.tensor_scalar(stat[:, n:n + 1], stat[:, 24:25], -1.0, None, ALU.mult).then_inc(nmax_ready, 1)

            def attention_scale(n):
                w = 384 if n % 2 == 0 else 768
                dve.wait_ge(exp_done, n + 1)
                link(dve.reciprocal(stat[:, 25:26], stat[:, 8 + n:9 + n]))
                dve.tensor_scalar(pr[:, n % 2, 0:w], pr[:, n % 2, 0:w], stat[:, 25:26], None, ALU.mult)\
                   .then_inc(pn_ready, 1)

            def attention_lo(n):
                c0 = 2048 + 256 * (n // 2) + 128 * (n % 2)
                dve.wait_ge(ohi_ready, n + 1)
                dve.tensor_tensor(alo[:, c0:c0 + 128], pb[6][:, 0:128], ahi[:, c0:c0 + 128].bitcast(F32),
                                  ALU.subtract).then_inc(olo_ready, 1)

            def attention(n):
                if 0 <= n - 4 < TR:
                    attention_lo(n - 4)
                if 0 <= n - 1 < TR:
                    attention_max(n - 1)
                    attention_scale(n - 1)

            def store_mods(layer):
                dve.wait_ge(mod_turned, 6 * layer + 6)
                bias = C["bmod"][:, MODS * layer:MODS * layer + MODS].rearrange("p (m g n) -> p m g n", m=6, n=2)
                for n in range(2):
                    i = dve.tensor_tensor(
                        mods[:, layer, :, :].rearrange("p (a n) s -> p a n s", n=2)[:, :, n, :]
                        .rearrange("p (m g) s -> p m g s", m=6),
                        pb[7][:, 256:352].rearrange("p (m n g s) -> p m n g s", m=6, n=2, g=4)[:, :, n, :, :],
                        bias[:, :, :, n].unsqueeze(3).broadcast_to([P, 6, 4, 2]), ALU.add)
                i.then_inc(mod_ready, 1)

            for l in range(2, 28):
                if l in (9, 13, 17, 21):
                    ssm_out((l - 9) // 4)
                if Q0 <= l - 1 < V0:
                    rotate(l - 1 - Q0)
                attention(l - GATE0)
                ahead(Pos(l, l))
                if 3 <= l < 3 + NTILE:
                    ssm_in(l - 3)
            for n in range(8, TR + 4):
                attention(n)
            store_mods(0)

            ph[0] = "attnproj"

            def dve_attnproj(p):
                ahead(p)
                dve.wait_ge(block_done, p.b + 1)
                dve.wait_ge(gate_ready, 8)
                for s in range(2):
                    i = dve.tensor_tensor(mix[:, 1024 * p.l + 512 * s:1024 * p.l + 512 * s + 512],
                                          pb[2 * p.l + s][:, :],
                                          area(GATES, 4096)[:, 1024 * p.l + 512 * s:1024 * p.l + 512 * s + 512],
                                          ALU.mult)
                i.then_inc(evac["attnproj"], 1)

            each_block(dve, "attnproj", dve_attnproj)
            ph[0] = "glu"

            def mix_lo(j):
                dve.wait_ge(mixhi_ready, j + 1)
                dve.tensor_tensor(alo[:, 512 * j:512 * j + 512], mix[:, 512 * j:512 * j + 512],
                                  ahi[:, 512 * j:512 * j + 512].bitcast(F32), ALU.subtract).then_inc(mixlo_ready, 1)

            for l in range(4):
                p = Pos(FIRST["glu"] + l, l)
                if l != 3:
                    ahead(p)
                if l % 2 == 0:
                    continue
                j = l // 2
                for s in range(2):
                    n = 2 * j + s
                    t = glut[:, 512 * s:512 * s + 512]
                    m = mix[:, 512 * n:512 * n + 512]
                    dve.wait_ge(gsig_ready, n + 1)
                    dve.tensor_tensor(t, glus[:, 512 * s:512 * s + 512], pb[(4 if j == 0 else 0) + s][:, :], ALU.mult)\
                       .then_inc(evac["glu"], 1)
                    dve.wait_ge(evac["glu"], n + 1)
                    link(dve.tensor_tensor(t, t, area(GATES + 2048 + 512 * n, 512), ALU.mult))
                    dve.tensor_tensor(m, m, t, ALU.add).then_inc(mix_ready, 1)
                    if j == 1 and s == 1:
                        for n in range(4):
                            mix_lo(n)
            ahead(Pos(FIRST["glu"] + 3, 3))
            ph[0] = "out"

            def wait_bank(name, u, count):
                if u < count - 1:
                    dve.wait_ge(bank_done, {"down": 0, "ff2a": 3, "ff2b": 10}[name] + u + 1)
                else:
                    dve.wait_ge(block_done, FIRST[name] + COUNT[name])

            def but_last(phase):
                def body(p):
                    if p.least < COUNT[phase] - 1:
                        ahead(p)
                return body

            def last_ahead(phase):
                ahead(Pos(FIRST[phase] + COUNT[phase] - 1, COUNT[phase] - 1))

            def add_to_x(name, p, bank):
                dve.wait_ge(block_done, p.b + 1)
                xu = X[:, 0, 2 * p.l:2 * p.l + 2, :]
                dve.tensor_tensor(xu, xu, bank[:, :].rearrange("p (a t) -> p a t", a=2), ALU.add)\
                   .then_inc(evac[name], 1)
                but_last(name)(p)

            each_block(dve, "out", lambda p: add_to_x("out", p, pb[4 + p.l]))
            norm_gain(1, C["gffn"])
            last_ahead("out")
            ph[0] = "ffn"

            def dve_ffn(p):
                if p.least % 2 == 0:
                    ahead(p)
                    return
                r = p.least // 2 % 2
                dve.wait_ge(sig_ready, p.h + 1)
                dve.tensor_tensor(tg1[:, r, :], sg1[:, r, :], pb[(p.k + 3) % 4][:, :], ALU.mult).then_inc(th_ready, 1)
                dve.wait_ge(th_ready, p.h + 1)
                dve.wait_ge(block_done, p.b + 1)
                dve.tensor_tensor(hid1[:, bass.ds(512 * p.h, 512)], tg1[:, r, :], pb[p.k][:, :], ALU.mult)\
                   .then_inc(evac["ffn"], 2)
                ahead(p)

            each_block(dve, "ffn", dve_ffn)
            ph[0] = "down"
            each_block(dve, "down", but_last("down"), roll=False)
            for u in range(4):
                xu = X[:, 0, 2 * u:2 * u + 2, :]
                wait_bank("down", u, 4)
                dve.tensor_tensor(xu, xu, pb[4 + u][:, :].rearrange("p (a t) -> p a t", a=2), ALU.add)\
                   .then_inc(evac["down"], 1)
            for u in range(4):
                dve.wait_ge(xhi_ready, u + 1)
                dve.tensor_tensor(alo[:, 512 * u:512 * u + 512].rearrange("p (a t) -> p a t", a=2),
                                  X[:, 0, 2 * u:2 * u + 2, :],
                                  ahi[:, 512 * u:512 * u + 512].bitcast(F32).rearrange("p (a t) -> p a t", a=2),
                                  ALU.subtract).then_inc(xlo_ready, 1)
            last_ahead("down")
            ph[0] = "ple"
            for l in range(5):
                p = Pos(FIRST["ple"] + l, l)
                if l:
                    u = l - 1
                    s = area(8704 + 512 * u, 512)
                    dve.wait_ge(sig_ready, 11 + u + 1)
                    dve.wait_ge(plep_ready, 1)
                    link(dve.tensor_tensor(s, s, plep[:, 512 * u:512 * u + 512], ALU.mult))
                    xu = X[:, 0, 2 * u:2 * u + 2, :]
                    dve.tensor_tensor(xu, xu, s.rearrange("p (a t) -> p a t", a=2), ALU.add).then_inc(evac["ple"], 1)
                but_last("ple")(p)
            norm_gain(2, C["gfinal"])

            def modulate_amul(layer, s, g):
                sc = mods[:, layer, 8 * s:8 * s + 8, :]
                gb = g.unsqueeze(2).broadcast_to([P, 8, 2])
                link(dve.scalar_tensor_tensor(amul[:, :, :], sc, 1.0, gb, ALU.add, ALU.mult))

            def norm_mod(r, layer, shift, g):
                modulate_amul(layer, shift + 1, g)
                reciprocal_std(r)
                rs = rstd[:, :].rearrange("p (s t) -> p s t", s=2)
                nb0 = NBASE[r] - 4 * (r > 2)
                for u in range(NU[r]):
                    nb = ring(NB_AT[r], u)
                    if u >= 4:
                        dve.wait_ge(nlo_ready, nb0 + u - 3)
                    if NU[r] == 8:
                        link(dve.tensor_tensor(nb, X[:, :, u, :], rs, ALU.mult))
                        for s in range(2):
                            i = dve.tensor_scalar(nb[:, s, :], nb[:, s, :], amul[:, u, s:s + 1],
                                                  mods[:, layer, 8 * shift + u, s:s + 1], ALU.mult, ALU.add)
                    else:
                        link(dve.tensor_tensor(nb, X[:, 0, 2 * u:2 * u + 2, :],
                                               rstd[:, 0:256].unsqueeze(1).broadcast_to([P, 2, T1]), ALU.mult))
                        for a in range(2):
                            c = 2 * u + a
                            i = dve.tensor_scalar(nb[:, a, :], nb[:, a, :], amul[:, c, 0:1],
                                                  mods[:, layer, 8 * shift + c, 0:1], ALU.mult, ALU.add)
                    i.then_inc(n_ready, 1)

            last_ahead("ple")
            dve.wait_ge(ctx_std, 1)
            link(dve.reciprocal(rstd[:, 256:512], rstd[:, 256:512]))
            norm_mod(3, 0, 0, C["g1"][:, 0:8])

            ph[0] = "pw1"
            taps = [(i, j) for i in range(len(CONV_DVE)) for j in range(TAPS)]

            def convolve(p, most):
                while taps and most > 0 and (p is None or CONV_DVE[taps[0][0]][0] // 2 * 2 + 1 <= p.l):
                    i, j = taps.pop(0)
                    c, s, ns = CONV_DVE[i]
                    most -= 1
                    src, acc = upad[:, c, s:s + ns, j:j + T1], cacc[:, c, s:s + ns, :]
                    if j == 0:
                        dve.wait_ge(dw_landed, 16)
                        dve.wait_ge(pad_ready, 1)
                        dve.wait_ge(u_ready, c + 1)
                        link(dve.tensor_scalar(acc, src, wdw[:, c, 0:1], C["convb"][:, c:c + 1], ALU.mult, ALU.add))
                    elif j < 30:
                        link(dve.scalar_tensor_tensor(acc, src, wdw[:, c, j:j + 1], acc, ALU.mult, ALU.add))
                    else:
                        dve.scalar_tensor_tensor(acc, src, wdw[:, c, j:j + 1], acc, ALU.mult, ALU.add)\
                           .then_inc(conv_dve, 1)

            def dve_pw1(p):
                if p.least % 2:
                    for m in range(2):
                        c = p.l - 1 + m
                        dve.wait_ge(sig_ready, 15 + c + 1)
                        dve.tensor_tensor(upad[:, c, :, 15:15 + T1],
                                          sgc[:, m, :].rearrange("p (s t) -> p s t", s=2),
                                          pb[2 * ((p.k + 3) % 4) + m][:, :].rearrange("p (s t) -> p s t", s=2),
                                          ALU.mult).then_inc(u_ready, 1)
                ahead(p)
                convolve(p, 10)

            each_block(dve, "pw1", dve_pw1, roll=False)
            convolve(None, 1000)
            dve.wait_ge(msum_done, 1)
            link(dve.tensor_scalar(mean_s, pb[6][:, :], 1.0 / D, None, ALU.mult))
            for u in range(KD):
                cu = cacc[:, u, :, :].rearrange("p s t -> p (s t)")
                dve.tensor_tensor(cu, cu, mean_s, ALU.subtract).then_inc(cen_ready, 1)
            dve.wait_ge(lstd_ready, 1)
            link(dve.reciprocal(rstd[:, :], rstd[:, :]))
            for u in range(KD):
                cu = cacc[:, u, :, :].rearrange("p s t -> p (s t)")
                link(dve.tensor_tensor(cu, cu, rstd[:, :], ALU.mult))
                dve.tensor_scalar(cu, cu, C["lng"][:, u:u + 1], C["lnb"][:, u:u + 1], ALU.mult, ALU.add)\
                   .then_inc(lnx_ready, 1)
                if u >= 1:
                    v = u - 1
                    cv = cacc[:, v, :, :].rearrange("p s t -> p (s t)")
                    dve.wait_ge(lns_ready, v + 1)
                    dve.tensor_tensor(cv, cv, csq[:, v % 4, :], ALU.mult).then_inc(lny_ready, 1)
            cv = cacc[:, 7, :, :].rearrange("p s t -> p (s t)")
            dve.wait_ge(lns_ready, 8)
            dve.tensor_tensor(cv, cv, csq[:, 3, :], ALU.mult).then_inc(lny_ready, 1)

            def gated_add(layer, gate, c, s, src):
                xs = X[:, s, c, :]
                return dve.scalar_tensor_tensor(xs, src, mods[:, layer, 8 * gate + c, s:s + 1], xs,
                                                ALU.mult, ALU.add)

            ph[0] = "pw2"
            for l in range(4):
                p = Pos(FIRST["pw2"] + l, l)
                dve.wait_ge(block_done, p.b + 1)
                if l == 2:
                    store_mods(1)
                for m in range(2):
                    for s in range(2):
                        i = gated_add(0, 2, 2 * l + m, s, pb[2 * p.k + m][:, 256 * s:256 * s + 256])
                    i.then_inc(evac["pw2"], 1)
                but_last("pw2")(p)
            norm_mod(4, 0, 3, C["g2"][:, 0:8])
            last_ahead("pw2")
            ph[0] = "ff1a"

            each_block(dve, "ff1a", ahead)
            ph[0] = "ff2a"
            each_block(dve, "ff2a", but_last("ff2a"))
            for c in range(8):
                wait_bank("ff2a", c, 8)
                for s in range(2):
                    i = gated_add(0, 5, c, s, pb[c][:, 256 * s:256 * s + 256])
                i.then_inc(evac["ff2a"], 1)
            norm_mod(5, 1, 0, C["g1"][:, 8:16])
            last_ahead("ff2a")

            ph[0] = "qkv"
            def head_norm(e):
                n = UNITS[e]
                x, rs = area(512 * n, 512), gsq[:, 512 * n:512 * n + 512]
                dve.wait_ge(gq_std, e + 1)
                link(dve.reciprocal(rs, rs))
                g = C["qn"] if n < 4 else C["kn"]
                dve.scalar_tensor_tensor(x, x, g, rs, ALU.mult, ALU.mult).then_inc(gq_n, 1)

            def head_rotate(e):
                n = UNITS[e]
                x = area(512 * n, 512)
                if n < 4:
                    part = x.rearrange("p (a t) -> p a t", a=2)
                    rot = pb[ROT_BANK[e]][:, :].rearrange("p (a t) -> p a t", a=2)
                    cb, sbb = (gtab[:, s, :].unsqueeze(1).broadcast_to([P, 2, T1]) for s in range(2))
                    a, b = (t[:, n % 2, :].rearrange("p (a t) -> p a t", a=2) for t in (gt1, gt2))
                else:
                    part, rot = x[:, 0:256], pb[ROT_BANK[e]][:, 0:256]
                    cb, sbb = gtab[:, 0, :], gtab[:, 1, :]
                    a, b = gt1[:, n % 2, 0:256], gt2[:, n % 2, 0:256]
                dve.wait_ge(gq_rot, e + 1)
                if e >= 2:
                    dve.wait_ge(gq_ready, e - 1)
                dve.tensor_tensor(b, rot, sbb, ALU.mult)
                link(dve.tensor_tensor(a, part, cb, ALU.mult))
                dve.tensor_tensor(part, a, b, ALU.add).then_inc(gq_ready, 1)

            dve.wait_ge(gtab_landed, 16)
            for l in range(7):
                for e in units_of(l - 2):
                    head_rotate(e)
                for e in units_of(l - 1):
                    head_norm(e)

            def gmax(h):
                s0, s1 = 16 + 2 * (h % 2), 32 + 2 * (h % 2)
                dve.wait_ge(s_done, TR + h + 1)
                for qt in range(2):
                    i = dve.reduce_max(stat[:, s1 + qt:s1 + qt + 1], pb[2 * (h % 2) + qt][:, :], AX_X)
                link(i)
                dve.tensor_scalar(stat[:, s0:s0 + 2], stat[:, s1:s1 + 2], -0.125, None, ALU.mult).then_inc(nmax_ready, 1)

            def gscale(h):
                s0, s1 = 20 + 2 * (h % 2), 36 + 2 * (h % 2)
                dve.wait_ge(exp_done, TR + 2 * (h + 1))
                link(dve.reciprocal(stat[:, s1:s1 + 2], stat[:, s0:s0 + 2]))
                for qt in range(2):
                    i = dve.tensor_scalar(pg[:, h % 2, qt, :], pg[:, h % 2, qt, :], stat[:, s1 + qt:s1 + qt + 1],
                                          None, ALU.mult)
                i.then_inc(pn_ready, 1)

            def glo(h):
                kh, g = h // 4, h % 4
                l0, c0 = 64 * (kh % 2), 256 * (4 * (kh // 2) + g)
                dve.wait_ge(ohi_ready, 8 + h + 1)
                dve.tensor_tensor(alo[l0:l0 + 64, c0:c0 + 256], pb[6 + h % 2][l0:l0 + 64, 0:256],
                                  ahi[l0:l0 + 64, c0:c0 + 256].bitcast(F32), ALU.subtract).then_inc(olo_ready, 1)

            for h in range(1, 16 + 4):
                if h - 1 < 16:
                    gmax(h - 1)
                if h == 3:
                    head_rotate(5)
                if h >= 4:
                    glo(h - 4)
                if h - 1 < 16:
                    gscale(h - 1)
            ph[0] = "wo"
            dve.wait_ge(wlo_ready, FIRST["wo"] + 2)
            for l in range(4):
                p = Pos(FIRST["wo"] + l, l)
                dve.wait_ge(block_done, p.b + 1)
                for m in range(2):
                    i = gated_add(1, 2, 2 * l + m, 0, pb[l][:, 256 * m:256 * m + 256])
                i.then_inc(evac["wo"], 1)
                but_last("wo")(p)
            norm_mod(6, 1, 3, C["g2"][:, 8:16])
            last_ahead("wo")
            ph[0] = "ff1b"
            each_block(dve, "ff1b", ahead)
            ph[0] = "ff2b"
            each_block(dve, "ff2b", ahead)
            for c in range(8):
                if c % 2 == 0:
                    wait_bank("ff2b", c // 2, 4)
                gated_add(1, 5, c, 0, pb[4 + c // 2][:, 256 * (c % 2):256 * (c % 2) + 256]).then_inc(evac["ff2b"], 1)

        @block.gpsimd
        def _(pool):
            chain = [0]

            def link(ins):
                chain[0] += 1
                ins.then_inc(pch, 1)
                pool.wait_ge(pch, chain[0])

            pool.memset(tab[:, :, 0, :, 0:1], 1.0)
            link(pool.memset(tab[:, :, 1, :, 0:1], 0.0))
            lo_parts(pool, 0)
            pool.wait_ge(sin_out, 2)
            link(pool.tensor_copy(powers[:, 0, 0, :], sp[:, 9, :]))
            link(pool.tensor_copy(powers[:, 0, 1, :], sp[:, 8, :]))
            for n in range(1, 8):
                c, s = powers[:, n - 1, 0, :], powers[:, n - 1, 1, :]
                a, b = tta[:, 0:16], ttb[:, 0:16]
                pool.tensor_tensor(a, c, c, ALU.mult)
                link(pool.tensor_tensor(b, s, s, ALU.mult))
                pool.tensor_tensor(powers[:, n, 0, :], a, b, ALU.subtract)
                link(pool.tensor_tensor(tta[:, 16:32], c, s, ALU.mult))
                link(pool.tensor_tensor(powers[:, n, 1, :], tta[:, 16:32], tta[:, 16:32], ALU.add))

            def tables(g, part):
                if g >= 2 and part == 0:
                    pool.wait_ge(g_ready, 2 * g - 2)
                for n in (range(6), range(6, 8))[part]:
                    w = 1 << n
                    old = tab[:, g % 2, :, :, 0:w]
                    cn, sn = (powers[:, n, s, 2 * g:2 * g + 2].unsqueeze(1).unsqueeze(3)
                              .broadcast_to([P, 2, 2, w]) for s in range(2))
                    a = tta[:, 0:4 * w].rearrange("p (s j t) -> p s j t", s=2, j=2)
                    b = ttb[:, 0:4 * w].rearrange("p (s j t) -> p s j t", s=2, j=2)
                    pool.tensor_tensor(a, old, cn, ALU.mult)
                    link(pool.tensor_tensor(b, old, sn, ALU.mult))
                    pool.tensor_tensor(tab[:, g % 2, 0, :, w:2 * w], a[:, 0], b[:, 1], ALU.subtract)
                    i = pool.tensor_tensor(tab[:, g % 2, 1, :, w:2 * w], a[:, 1], b[:, 0], ALU.add)
                    if n < 7:
                        link(i)
                    else:
                        i.then_inc(tab_ready, 1)
                        pool.wait_ge(tab_ready, g + 1)

            def turn_forward(j):
                s, jj = j // 2 % 2, j % 2
                cb, sbb = (tab[:, s, k, jj, :].unsqueeze(1).broadcast_to([P, 2, T1]) for k in range(2))
                pool.wait_ge(g_ready, j + 1)
                if j >= 2:
                    pool.wait_ge(y_done, j - 1)
                pool.tensor_tensor(q1, g_s[:, j % 2, :, :], cb, ALU.mult)
                link(pool.tensor_tensor(q2, g_s[:, j % 2, :, :], sbb, ALU.mult))
                pool.tensor_tensor(h_s[:, j % 2, 0, :], q1[:, 0, :], q2[:, 1, :], ALU.subtract)
                pool.tensor_tensor(h_s[:, j % 2, 1, :], q1[:, 1, :], q2[:, 0, :], ALU.add).then_inc(h_ready, 1)
                pool.wait_ge(h_ready, j + 1)

            for g in range(2):
                tables(g, 0)
                tables(g, 1)
            for j in range(NTILE):
                if j >= 2 and j // 2 + 1 < 8:
                    tables(j // 2 + 1, j % 2)
                turn_forward(j)
            for c in range(4):
                pool.wait_ge(yhi_ready, c + 1)
                pool.tensor_tensor(alo[:, 3072 + 256 * c:3328 + 256 * c], u_s[:, c, :],
                                   ahi[:, 3072 + 256 * c:3328 + 256 * c].bitcast(F32), ALU.subtract)\
                    .then_inc(ylo_ready, 1)
            for n in range(8):
                pool.wait_ge(evac["in"], GATE0 + n + 1)
                g = gates[:, 2 * n:2 * n + 2, :]
                pool.tensor_scalar(g, g, 0.5, 0.5, ALU.mult, ALU.add).then_inc(gate_ready, 1)
            lo_parts(pool, 1)

            def hidden_lo(n, first, end, w, h, at):
                for l in range(first, end):
                    s = l % 4
                    pool.wait_ge(hhi_ready, n + l + 1)
                    pool.tensor_tensor(alo[:, at + w * s:at + w * s + w], h[:, w * l:w * l + w],
                                       ahi[:, at + w * s:at + w * s + w].bitcast(F32), ALU.subtract)\
                        .then_inc(hlo_ready, 1)

            hidden_lo(0, 0, 11, 512, hid1, 2048)
            pool.wait_ge(phi_ready, 1)
            pool.tensor_tensor(alo[:, 3584:4096], pin, ahi[:, 3584:4096].bitcast(F32), ALU.subtract)\
                .then_inc(plo_ready, 1)
            pool.wait_ge(evac["ple"], 4)
            pool.memset(upad[:, :, :, 0:15], 0.0)
            pool.memset(upad[:, :, :, 15 + T1:UPW], 0.0).then_inc(pad_ready, 1)
            lo_parts(pool, 3)
            for i, (c, s, ns) in enumerate(CONV_POOL):
                acc = cacc[:, c, s:s + ns, :]
                pool.wait_ge(conv_init, i + 1)
                for j in range(1, 31):
                    n = 30 * i + j - 1
                    pool.wait_ge(cp_ready, n + 1)
                    if j > 1:
                        pool.wait_ge(cp_used, n)
                    pool.tensor_tensor(acc, acc, ctp[:, n % 2, 0:T1 * ns].rearrange("p (s t) -> p s t", s=ns),
                                       ALU.add)\
                        .then_inc(cp_used, 1)
            for u in range(KD):
                pool.wait_ge(lnhi_ready, u + 1)
                pool.tensor_tensor(alo[:, 512 * u:512 * u + 512], cacc[:, u, :, :].rearrange("p s t -> p (s t)"),
                                   ahi[:, 512 * u:512 * u + 512].bitcast(F32), ALU.subtract).then_inc(lnlo_ready, 1)
            lo_parts(pool, 4)

            def squares_of(n, first, end):
                with pool.Fori(first // 2, end // 2) as i:
                    for m in range(2):
                        pool.wait_ge(relu_ready, 2 * i + (n + m + 1))
                        pool.tensor_tensor(hid[:, bass.ds(1024 * i + 512 * m, 512)], rl[:, m, :], rl[:, m, :],
                                           ALU.mult).then_inc(hid_sq, 1)

            squares_of(0, 0, 30)
            hidden_lo(11, 0, 2, 1024, hid, 0)
            squares_of(0, 30, 32)
            hidden_lo(11, 2, 16, 1024, hid, 0)
            lo_parts(pool, 5)
            for l in range(6):
                b = FIRST["qkv"] + l
                k = b % 4
                pool.wait_ge(whi_ready, b + 3)
                pool.wait_ge(wlo_ready, b + 2)
                pool.tensor_tensor(wlo[:, k % 2, :], raw[:, (k + 2) % 4, :], whi[:, k % 2, :].bitcast(F32),
                                   ALU.subtract).then_inc(wlo_ready, 1)
            lo_parts(pool, 6)
            squares_of(32, 0, 14)
            hidden_lo(27, 0, 2, 512, hid, 2048)
            squares_of(32, 14, 16)
            hidden_lo(27, 2, 16, 512, hid, 2048)

        @block.tensor
        def _(pe):
            def three(out_, w_hi, w_lo, a_hi, a_lo, start, stop, **kw):
                pe.matmul(out_, w_hi, a_hi, start=start, stop=False, **kw)
                pe.matmul(out_, w_hi, a_lo, start=False, stop=False, **kw)
                return pe.matmul(out_, w_lo, a_hi, start=False, stop=stop, **kw)

            def tiles(p, kn):
                w = BLK // kn
                return (t[:, p.k % 2, :].rearrange("p (c m) -> p c m", c=kn) for t in (whi, wlo)), w

            def feature_block(p, kn, outs, at, t, chunk_wait=None, free=False):
                pe.wait_ge(wlo_ready, p.b + 1)
                (wh, wl), w = tiles(p, kn)
                ms = range(w // P)
                for c, m in ([(c, m) for c in range(kn) for m in ms] if (chunk_wait or free) and t == 512 else
                             [(c, m) for m in ms for c in range(kn)]):
                    if chunk_wait and m == 0:
                        chunk_wait(c)
                    mm = three(outs(m), wh[:, c, P * m:P * m + P], wl[:, c, P * m:P * m + P],
                               ahi[:, at + t * c:at + t * c + t], alo[:, at + t * c:at + t * c + t],
                               c == 0, c == kn - 1)
                    if free and m == ms[-1] and c in (1, 3):
                        mm.then_inc(chunks_free, 1)
                mm.then_inc(block_done, 1)

            def token_block(p, t, na):
                pe.wait_ge(wlo_ready, p.b + 1)
                (wh, wl), _ = tiles(p, KD)
                for a in range(na):
                    for c in range(KD):
                        x0 = t * c + P * a
                        bank = pb[(p.l % 2 if na == 2 else 2 + a // 2)]
                        mm = three(bank[:, 256 * (a % 2):256 * (a % 2) + 256], ahi[:, x0:x0 + P], alo[:, x0:x0 + P],
                                   wh[:, c, :], wl[:, c, :], c == 0, c == KD - 1)
                mm.then_inc(block_done, 1)

            def row_block(p, at, t, last, bank0=0, tile_wait=None):
                pe.wait_ge(wlo_ready, p.b + 1)
                (wh, wl), _ = tiles(p, 2)
                s = at + 2 * t * (p.least % 4)
                per = 512 // t
                for c, m in ([(c, m) for m in range(8) for c in range(2)] if last else
                             [(c, m) for c in range(2) for m in range(8)]):
                    if tile_wait and c == 0:
                        tile_wait(m)
                    o_ = pb[bank0 + m // per][:, t * (m % per):t * (m % per) + t]
                    mm = three(o_, wh[:, c, P * m:P * m + P], wl[:, c, P * m:P * m + P],
                               ahi[:, s + t * c:s + t * c + t], alo[:, s + t * c:s + t * c + t],
                               p.least == 0 and c == 0 and m % per == 0, last and c == 1,
                               skip_group_check=True)
                    if last and c == 1 and m % per == per - 1 and m < 7:
                        mm.then_inc(bank_done, 1)
                mm.then_inc(block_done, 1)

            def half(bank, m):
                return pb[bank][:, 256 * m:256 * m + 256]

            def mod_piece(layer, t):
                m, c = divmod(t, KD)
                bank = pb[2 + m % 2] if layer else pb[7]
                ring_, landed_ = (modraw1, modraw1_landed) if layer else (modraw, modraw_landed)
                r, k = divmod(t, len(landed_))
                if c == 0 and m >= 1 + layer:
                    pe.wait_ge(modrow_ready, 6 * layer + m - layer)
                pe.wait_ge(landed_[k], 16 * (r + 1))
                for n in range(4):
                    mm = pe.matmul(bank[32 * n:32 * n + 32, 0:256], scc[:, 2 * c:2 * c + 32],
                                   ring_[:, k, 256 * n:256 * n + 256], start=(c == 0), stop=(c == KD - 1))
                mm.then_inc(modraw_used, 1)

            def mod_turn(layer, m):
                pe.wait_ge(modrow_ready, 6 * layer + m + 1)
                pick = C["ident"].rearrange("p (g w) -> p g w", g=4)[:, :, 0:2]
                for n in range(2):
                    x0 = 256 + 16 * m + 8 * n
                    mm = pe.matmul(pb[7][:, x0:x0 + 8], modrow[layer][:, m % 2, P * n:P * n + P], pick,
                                   start=True, stop=True)
                mm.then_inc(mod_turned, 1)

            pe.wait_ge(cst_landed, 16)
            sums(pe, 0)

            def ssm_bu(j):
                r = 32 * (j % 4)
                if j == 0:
                    pe.wait_ge(ssm_landed, 32)
                    pe.wait_ge(evac["in"], 2)
                if j >= 2:
                    pe.wait_ge(bu_used, j - 1)
                for s in range(2):
                    mm = pe.matmul(half(2 + 2 * (j % 2), s), bl[r:r + 32, j // 4, s, :], u_s[r:r + 32, j // 4, :],
                                   start=True, stop=True)
                mm.then_inc(bu_done, 1)

            def ssm_y(j):
                r, c = 32 * (j % 4), j // 4
                if j == 0:
                    pe.wait_ge(ct_ready, 1)
                if c >= 1:
                    pe.wait_ge(ysum_ready, c)
                pe.wait_ge(h_ready, j + 1)
                for s in range(2):
                    mm = pe.matmul(pb[6][r:r + 32, 256 * (c % 2):256 * (c % 2) + 256], ct[:, s, j, :],
                                   h_s[:, j % 2, s, :], start=(s == 0), stop=(s == 1))
                mm.then_inc(y_done, 1)

            def rotation(n):
                t, m = (q_s if n < 6 else k_s), n % 6
                pe.wait_ge(evac["in"], Q0 + n + 1)
                if n >= 1:
                    pe.wait_ge(roped, n)
                pe.matmul(pb[3][0:32, :], C["rotg"][0:32, 0:32], t[0:32, 2 * m:2 * m + 2, :],
                          start=True, stop=True).then_inc(rot_done, 1)

            def scores(n):
                h, qt = n // 2, n % 2
                if n == 0:
                    pe.wait_ge(roped, 12)
                if n >= 1:
                    pe.wait_ge(s_used, n)
                for kt in range(1 + qt):
                    for g in range(NG):
                        mm = pe.matmul(pb[4 + kt][:, P * g:P * g + P], q_s[:, NHG * g + h, P * qt:P * qt + P],
                                       k_s[:, NHG * g + h, P * kt:P * kt + P], start=True, stop=True)
                mm.then_inc(s_done, 1)

            def turn_probs(n):
                pe.wait_ge(pn_ready, n + 1)
                if n >= 1:
                    pe.wait_ge(pt_ready, n)
                for kt in range(1 + n % 2):
                    for g in range(NG):
                        x0 = 384 * kt + P * g
                        mm = pe.transpose(pb[2 + kt][:, P * g:P * g + P], pr[:, n % 2, x0:x0 + P], C["ident"])
                mm.then_inc(pt_done, 1)

            def weigh(n):
                h, qt = n // 2, n % 2
                pe.wait_ge(pt_ready, n + 1)
                if n == 0:
                    pe.wait_ge(evac["in"], GATE0)
                    pe.wait_ge(ysum_ready, 4)
                if n >= 1:
                    pe.wait_ge(olo_ready, n)
                for kt in range(1 + qt):
                    for g in range(NG):
                        mm = pe.matmul(pb[6][:, 0:128], v_s[:, kt, P * (NHG * g + h):P * (NHG * g + h) + P],
                                       pt[:, 384 * kt + P * g:384 * kt + P * g + P],
                                       start=(kt == 0 and g == 0), stop=(kt == qt and g == NG - 1))
                mm.then_inc(o_done, 1)

            def attention(n):
                if 0 <= n < TR:
                    scores(n)
                if 0 <= n - 2 < TR:
                    turn_probs(n - 2)
                if 0 <= n - 3 < TR:
                    weigh(n - 3)

            for l in range(28):
                p = Pos(l, l)
                if l >= 2:
                    pe.wait_ge(evac["in"], l - 1)
                if V0 <= l < GATE0:
                    token_block(p, T1, 2)
                else:
                    feature_block(p, KD, lambda m: half(l % 2, m), 0, T1,
                                  (lambda c: wait_norm(pe, 0, c)) if l == 0 else None)
                if 2 <= l < 26:
                    if l == 2:
                        pe.wait_ge(silu_ready, 1)
                    if l % 4 == 2 and l > 2:
                        mod_turn(0, (l - 6) // 4)
                    mod_piece(0, 2 * (l - 2))
                    mod_piece(0, 2 * (l - 2) + 1)
                if l == 26:
                    mod_turn(0, 5)
                if Q0 <= l - 1 < V0:
                    rotation(l - 1 - Q0)
                if 3 <= l < 3 + NTILE:
                    ssm_bu(l - 3)
                if 5 <= l < 5 + NTILE:
                    ssm_y(l - 5)
                attention(l - GATE0)
            for n in range(8, TR + 3):
                attention(n)

            pe.wait_ge(olo_ready, TR)
            for l in range(2):
                feature_block(Pos(FIRST["attnproj"] + l, l), 4, lambda m: half(2 * l + m // 2, m % 2), 2048, T1)
            pe.wait_ge(ylo_ready, 4)
            pe.wait_ge(mod_ready, 1)
            for l in range(4):
                if l == 2:
                    pe.wait_ge(evac["attnproj"], 2)
                feature_block(Pos(FIRST["glu"] + l, l), 4,
                              lambda m: half((4 if l < 2 else 0) + 2 * (l % 2) + m // 2, m % 2), 3072, T1)
            for l in range(4):
                feature_block(Pos(FIRST["out"] + l, l), KD, lambda m: half(4 + l, m), 0, T1,
                              (lambda c: pe.wait_ge(mixlo_ready, c // 2 + 1)) if l == 0 else None)
            sums(pe, 1)

            def pe_ffn(p):
                if p.least >= 4:
                    pe.wait_ge(evac["ffn"], 2 * p.h - 2)
                feature_block(p, KD, lambda m: half(p.k, m), 0, T1,
                              (lambda c: wait_norm(pe, 1, c)) if p.least == 0 else None)

            each_block(pe, "ffn", pe_ffn)
            for l in range(11):
                pe.wait_ge(hlo_ready, l + 1)
                row_block(Pos(FIRST["down"] + l, l), 2048, T1, l == 10, 4)
            pe.wait_ge(plo_ready, 1)
            for l in range(5):
                p = Pos(FIRST["ple"] + l, l)
                if l == 0:
                    feature_block(p, 2, lambda m: half(m // 2, m % 2), 3584, T1)
                else:
                    feature_block(p, KD, lambda m: half(3 + l, m), 0, T1,
                                  (lambda c: pe.wait_ge(xlo_ready, c // 2 + 1)) if l == 1 else None)
                if l == 2:
                    pe.wait_ge(plep_ready, 1)
                    for u in range(4):
                        pe.wait_ge(ctx_squares, u + 1)
                        sum_pair(pe, pb[1][:, 256:512], flat(SQ_AT[3], u), u).then_inc(ctx_summed, 1)
            sums(pe, 2)
            pe.wait_ge(std_ready, 3)
            sums(pe, 3)

            for l in range(8):
                p = Pos(FIRST["pw1"] + l, l)
                if l >= 4:
                    pe.wait_ge(u_ready, 2 * ((l - 4) // 2 + 1))
                feature_block(p, KD, lambda m: pb[2 * p.k + m][:, :], 0, 512,
                              (lambda c: wait_norm(pe, 3, c)) if l == 0 else None)
            pieces = list(range(HALVES))

            def mod_pieces(most):
                while pieces and most > 0:
                    t = pieces.pop(0)
                    most -= 1
                    mod_piece(1, t)
                    if t % KD == 5 and KD < t < 5 * KD:
                        mod_turn(1, t // KD - 1)

            mod_pieces(MOD_BEFORE)
            pe.wait_ge(u_ready, KD)
            for i in range(len(CONV_PE) * TAPS):
                n, j = divmod(i, TAPS)
                pe.wait_ge(diag_ready, i + 1)
                pe.matmul(pb[n][:, :], diag[:, i % 8, :], upad[:, CONV_PE[n], :, j:j + T1],
                          start=(j == 0), stop=(j == TAPS - 1)).then_inc(tap_done, 1)
                if i % MOD_EVERY == MOD_EVERY - 1:
                    mod_pieces(1)
            mod_pieces(MOD_AFTER)
            for i, c in enumerate(CONV_ORDER):
                for n, part in enumerate(CONV_DVE):
                    if part[0] == c:
                        pe.wait_ge(conv_dve, n + 1)
                for n, part in enumerate(CONV_POOL):
                    if part[0] == c:
                        pe.wait_ge(cp_used, (TAPS - 1) * (n + 1))
                if c in CONV_PE:
                    pe.wait_ge(conv_out, CONV_PE.index(c) + 1)
                mm = pe.matmul(pb[6][:, :], C["ones"], cacc[:, c, :, :], start=(i == 0), stop=(i == KD - 1))
            mm.then_inc(msum_done, 1)
            for u in range(KD):
                pe.wait_ge(vsq_ready, u + 1)
                pe.matmul(pb[6][:, :], C["ones"], csq[:, u % 4, :], start=(u == 0), stop=(u == KD - 1))\
                  .then_inc(vsum_done, 1)
            mod_pieces(HALVES)
            for l in range(4):
                p = Pos(FIRST["pw2"] + l, l)
                if l == 1:
                    mod_turn(1, 4)
                    mod_turn(1, 5)
                if l == 3:
                    pe.wait_ge(mod_ready, 2)
                feature_block(p, KD, lambda m: pb[2 * p.k + m][:, :], 0, 512,
                              (lambda c: pe.wait_ge(lnlo_ready, c + 1)) if l == 0 else None)
            pe.wait_ge(evac["pw2"], 8)
            sums(pe, 4)

            def pe_ff1(p, one, r):
                if p.least >= 4:
                    pe.wait_ge(relu_ready, 32 + p.l - 3 if one else 2 * p.l - 6)
                feature_block(p, KD, (lambda m: half(p.k, m)) if one else (lambda m: pb[2 * p.k + m][:, :]), 0,
                              T1 if one else 512, (lambda c: wait_norm(pe, r, c)) if p.least == 0 else None,
                              not one and p.least == 15)

            each_block(pe, "ff1a", lambda p: pe_ff1(p, False, 4))

            def pe_ff2(p, name, n, at, t):
                pe.wait_ge(hlo_ready, n + 1 + p.l)
                row_block(p, at, t, p.least == COUNT[name] - 1, 0 if t == 512 else 4,
                          (lambda m: pe.wait_ge(relu_ready, 25 + m)) if t == 512 and p.least == 0 else None)

            each_block(pe, "ff2a", lambda p: pe_ff2(p, "ff2a", 11, 0, 512))
            pe.wait_ge(evac["ff2a"], 8)
            sums(pe, 5)

            def head_sums(e):
                n = UNITS[e]
                pe.wait_ge(gq_sq, e + 1)
                if e >= 4:
                    pe.wait_ge(gq_std, e - 1)
                pe.matmul(pb[MS_BANK[e]][:, :], C["halves"], gsq[:, 512 * n:512 * n + 512], start=True, stop=True)\
                  .then_inc(gq_ms, 1)

            def head_turn(e):
                n = UNITS[e]
                pe.wait_ge(gq_n, e + 1)
                if e == 2:
                    pe.wait_ge(gq_ready, 1)
                w = 512 if n < 4 else 256
                pe.matmul(pb[ROT_BANK[e]][:, 0:w], C["rotg"], area(512 * n, w), start=True, stop=True)\
                  .then_inc(gq_rot, 1)

            for l in range(7):
                p = Pos(FIRST["qkv"] + l, l)
                if l == 0:
                    feature_block(p, KD, lambda m: pb[m][:, :], 0, 512, lambda c: wait_norm(pe, 5, c))
                elif l == 1:
                    token_block(p, 512, 4)
                elif l < 6:
                    pe.wait_ge(wlo_ready, p.b + 1)
                    (wh, wl), _ = tiles(p, KD)
                    for m in range(2):
                        for c in range(KD):
                            mm = three(half(2 + l, m), wh[:, c, P * m:P * m + P], wl[:, c, P * m:P * m + P],
                                       ahi[:, 512 * c:512 * c + 256], alo[:, 512 * c:512 * c + 256],
                                       c == 0, c == KD - 1)
                    mm.then_inc(block_done, 1)
                for e in units_of(l - 1):
                    if UNIT_BLOCK[e] == 2:
                        pe.wait_ge(evac["qkv"], 2)
                    head_sums(e)
                for e in units_of(l - 2):
                    head_turn(e)
            def gscores(h):
                kh, g = h // 4, h % 4
                l0, c = 64 * (kh % 2), 4 * (kh // 2) + g
                if h == 0:
                    pe.wait_ge(gq_ready, 3)
                if h == 1:
                    pe.wait_ge(gq_std, 6)
                if h == 2:
                    pe.wait_ge(gq_ready, 4)
                if h == 8:
                    pe.wait_ge(gq_ready, 6)
                if h >= 2:
                    pe.wait_ge(exp_done, TR + 2 * (h - 1))
                for qt in range(2):
                    mm = pe.matmul(pb[2 * (h % 2) + qt][:, :], qg[l0:l0 + 64, c, P * qt:P * qt + P],
                                   kg[l0:l0 + 64, kh // 2, :], start=True, stop=True)
                mm.then_inc(s_done, 1)

            def gturn(h):
                pe.wait_ge(pn_ready, TR + h + 1)
                if h >= 1:
                    pe.wait_ge(pt_ready, TR + h)
                for qt in range(2):
                    for kt in range(4):
                        x0 = 256 * (kt % 2) + P * qt
                        mm = pe.transpose(pb[4 + kt // 2][:, x0:x0 + P], pg[:, h % 2, qt, P * kt:P * kt + P],
                                          C["ident"])
                mm.then_inc(pt_done, 1)

            def gweigh(h):
                kh = h // 4
                l0 = 64 * (kh % 2)
                pe.wait_ge(pt_ready, TR + h + 1)
                if h >= 2:
                    pe.wait_ge(olo_ready, TR + h - 1)
                for kt in range(4):
                    mm = pe.matmul(pb[6 + h % 2][l0:l0 + 64, 0:256], vg[:, kt, 64 * kh:64 * kh + 64],
                                   ptg[:, h % 2, 256 * kt:256 * kt + 256], start=(kt == 0), stop=(kt == 3))
                mm.then_inc(o_done, 1)

            for h in range(16 + 3):
                if h < 16:
                    gscores(h)
                if h == 2:
                    head_turn(5)
                    pe.wait_ge(gq_ready, 5)
                if 0 <= h - 2 < 16:
                    gturn(h - 2)
                if h == 4:
                    pe.wait_ge(gq_ready, 6)
                if h >= 3:
                    gweigh(h - 3)
            pe.wait_ge(olo_ready, TR + 16)
            for l in range(4):
                feature_block(Pos(FIRST["wo"] + l, l), KD, lambda m: half(l, m), 0, T1)
            sums(pe, 6)
            each_block(pe, "ff1b", lambda p: pe_ff1(p, True, 6))
            each_block(pe, "ff2b", lambda p: pe_ff2(p, "ff2b", 27, 2048, 256))


def chunked(v, n=KD):
    return np.asarray(v).reshape(n, P).T


def constants():
    f = np.float32
    rot = np.zeros((P, P), f)
    for m in range(P):
        rot[m + 16 if m % 32 < 16 else m - 16, m] = -1 if m % 32 < 16 else 1
    halves = np.zeros((P, P), f)
    halves[:64, :64] = halves[64:, 64:] = 1
    invf = np.zeros((P, 1), f)
    invf[:32, 0] = np.tile(f(500000.0) ** (-np.arange(16, dtype=f) * f(2.0) / f(32)), 2)
    t = np.arange(T1)
    inv = f(10000.0) ** (-np.arange(16, dtype=f) / f(16))
    row, col = (t // 64).astype(f)[:, None] * inv, (t % 64).astype(f)[:, None] * inv
    ang = np.concatenate([row, row, col, col] * 2, axis=1).T
    gtab = np.stack([np.cos(ang), np.sin(ang)], axis=1).astype(f)
    q, k = np.arange(P)[:, None], np.arange(P)[None, :]
    masks = []
    for qt, kt in ((0, 0), (1, 0), (1, 1)):
        for r in (1, 4, 16):
            d = q + P * qt - k - P * kt
            ok = (d >= 0) & (d % r == 0) & (d // r <= 128)
            masks.append(np.where(ok, 0.0, NSCORE).astype(f))
    return dict(ident=np.eye(P, dtype=f), ones=np.ones((P, P), f), halves=halves, rotg=rot, invf=invf), \
        gtab, np.concatenate(masks, axis=1)


def kernel(**a):
    import concourse.bacc as bacc
    from concourse.bass_utils import run_bass_kernel_spmd as run

    a = {k: np.asarray(v) for k, v in a.items()}
    f = np.float32
    own, gtab, masks = constants()

    def states(v):
        return v.reshape(NTILE, P).T

    def both(v):
        return np.concatenate([chunked(v[0]), chunked(v[1])], axis=1)

    parts = dict(own)
    parts.update(
        gmix=chunked(a["g_mix"][0]), gffn=chunked(a["g_ffn"][0]), gfinal=chunked(a["g_final"]),
        convb=chunked(a["conv_b_dw_2"][0]), lng=chunked(a["conv_ln_g_2"][0]), lnb=chunked(a["conv_ln_b_2"][0]),
        g1=both(a["norm1_g_2"]), g2=both(a["norm2_g_2"]),
        bmod=np.concatenate([chunked(a["b_mod_2"][i], MODS) for i in range(2)], axis=1),
        qn=np.tile(a["gqa_q_norm_2"][0], 2)[:, None], kn=np.tile(a["gqa_k_norm_2"][0], 2)[:, None],
        dskip=chunked(a["d_skip"][0].reshape(-1), 4), lr=states(a["a_re"][0]), li=states(a["a_im"][0]),
        ldt=states(np.repeat(a["log_dt"][0][:, None], 64, axis=1)),
        cc=np.stack([chunked(a["c_2"][0]), chunked(a["c_ctx_2"])], axis=2).reshape(P, 16))
    consts = np.concatenate([parts[name] for name, _ in CONSTS], axis=1)

    def tokens(x):
        t, d = x.shape
        return np.ascontiguousarray(x.T.reshape(d // P, P, t).transpose(1, 0, 2))

    bl = np.zeros((4, 4, 2, 16, 2, 2, 64), f)
    ct = np.zeros((2, 64, 2, NTILE, 2, 16), f)
    for part, (b, c) in enumerate(((a["b_re"], a["c_re"]), (a["b_im"], a["c_im"]))):
        b4 = b[0].reshape(4, 4, 2, 64, 16)
        c4 = c[0].reshape(NTILE, 2, 16, 64)
        for g in range(2):
            bl[:, :, g, :, part, g, :] = b4[:, :, g].transpose(1, 0, 3, 2)
            ct[g, :, part, :, g, :] = c4[:, g].transpose(2, 0, 1)
    bl = np.ascontiguousarray(bl.transpose(0, 2, 3, 1, 4, 5, 6)).reshape(P, 1024)
    ct = ct.reshape(P, 1024)

    wq = a["gqa_w_qkv_2"][0]
    wqkv = np.concatenate([wq[:, :D].reshape(D, 2, 2, 4, 64).transpose(0, 1, 3, 2, 4).reshape(D, D), wq[:, D:]], axis=1)
    wo = a["gqa_w_o_2"][0].reshape(2, 2, 4, 64, D).transpose(0, 2, 1, 3, 4).reshape(D, D)

    arrays = dict(
        x=tokens(a["x"][0]), ctx=tokens(a["ctx_2"][0]), p=tokens(a["p"][0, 0]).reshape(P, 512), consts=consts,
        bl=bl, ct=ct, pos=np.broadcast_to(a["positions"], (32, T1)), gtab=gtab, masks=masks,
        w_dw=a["conv_w_dw_2"][0].T.reshape(KD, P, 31).transpose(1, 0, 2),
        w_in=a["w_in"][0], w_attn_proj=a["w_attn_proj"][0], w_glu_a=a["w_glu_a"][0], w_glu_b=a["w_glu_b"][0],
        w_out=a["w_out"][0], w_ffn_gate=a["w_ffn_gate"][0], w_ffn_up=a["w_ffn_up"][0],
        w_ffn_down=a["w_ffn_down"][0], w_ple_gate=a["w_ple_gate"][0], w_ple_proj=a["w_ple_proj"][0],
        pw1=a["conv_w_pw1_2"][0], pw2=a["conv_w_pw2_2"][0], w_qkv=wqkv, w_o=wo,
        w_mod=a["w_mod_2"], w_ff1=a["w_ff1_2"], w_ff2=a["w_ff2_2"])
    nc = bacc.Bacc("TRN2", target_bir_lowering=False, num_devices=1)
    aps, sent = {}, {}
    for name, v in arrays.items():
        v = np.ascontiguousarray(v)
        sent[f"in_{name}"] = v
        aps[name] = nc.dram_tensor(f"in_{name}", v.shape, mybir.dt.from_np(v.dtype), kind="ExternalInput").ap()
    out = nc.dram_tensor("out_t", (P, KD, T1), F32, kind="ExternalOutput").ap()
    program(nc, aps, out)
    r = run(nc, [sent], core_ids=[0])
    got = r.results[0]["out_t"]
    return np.ascontiguousarray(got.transpose(2, 1, 0)).reshape(1, T1, D)
```
